# Optimizing a Trainium2 kernel written in Bass

```python
import jax, jax.numpy as jnp
from jax import lax
import numpy as np
import jax
import jax.numpy as jnp

D_MODEL = 1024
BATCH = 1
SEQ = 256
DEPTH = 4

N_MIXERS = 3
HEAD_DIM = 64
N_HEADS = 12
MIX_WIDTH = N_HEADS * HEAD_DIM
N_MEM = 256
N_MEM_HEADS = 4
MEM_WIDTH = N_MEM_HEADS * HEAD_DIM
ROPE_DIM = HEAD_DIM // 4
ROPE_THETA = 500000.0
POS_OFFSET_RANGE = 8192
IDX_HEADS = 8
IDX_DIM = 64
TOPK_MAX = 256
QBLOCK_A = 64
DIL_PAIRS = ((128, 1), (512, 4), (2048, 16))
B_GROUP_HEADS = 4
B_V_DIM = MIX_WIDTH // B_GROUP_HEADS
MOBA_BLOCK = 256
MOBA_TOPK = 3
QBLOCK_C = 16
D_FF = -(-8 * D_MODEL // (3 * 256)) * 256
ALPHA = (2 * DEPTH) ** 0.25
BETA = (8 * DEPTH) ** -0.25
LN_EPS = 1e-5

WIDTH_A = 3 * MIX_WIDTH + IDX_HEADS * IDX_DIM + IDX_HEADS + IDX_DIM + MEM_WIDTH
WIDTH_BC = 3 * MIX_WIDTH + MEM_WIDTH


def layer_norm(x, g, b):
    xf = x.astype(jnp.float32)
    mu = jnp.mean(xf, -1, keepdims=True)
    var = jnp.mean(jnp.square(xf - mu), -1, keepdims=True)
    return ((xf - mu) * lax.rsqrt(var + LN_EPS) * g + b).astype(x.dtype)

def split_cols(h, widths):
    cuts = [int(c) for c in np.cumsum(widths)[:-1]]
    return jnp.split(h, cuts, axis=-1)

def rope_tables(positions):
    half = ROPE_DIM // 2
    inv = ROPE_THETA ** (-jnp.arange(half, dtype=jnp.float32) / half)
    ang = positions.astype(jnp.float32)[..., None] * inv
    return jnp.cos(ang)[:, :, None, :], jnp.sin(ang)[:, :, None, :]

def apply_rope(x, cos, sin):
    half = ROPE_DIM // 2
    c, s = cos.astype(x.dtype), sin.astype(x.dtype)
    x1, x2, rest = x[..., :half], x[..., half:ROPE_DIM], x[..., ROPE_DIM:]
    return jnp.concatenate([x1 * c - x2 * s, x2 * c + x1 * s, rest], axis=-1)

def dsa_attention(q, k, v, q_idx, w_idx, k_idx):
    Bsz, S, H, dh = q.shape
    topk = min(TOPK_MAX, S // 4)
    key_pos = jnp.arange(S)
    scale = dh ** -0.5

    def block(i):
        t0 = i * QBLOCK_A
        qpos = t0 + jnp.arange(QBLOCK_A)
        qi = lax.dynamic_slice_in_dim(q_idx, t0, QBLOCK_A, axis=1)
        wi = lax.dynamic_slice_in_dim(w_idx, t0, QBLOCK_A, axis=1)
        dots = jnp.einsum('bqhd,bsd->bqhs', qi, k_idx).astype(jnp.float32)
        score = jnp.einsum('bqhs,bqh->bqs', jax.nn.relu(dots), wi.astype(jnp.float32))
        causal = key_pos[None, :] <= qpos[:, None]
        score = jnp.where(causal[None], score, -jnp.inf)
        _, sel = lax.top_k(score, topk)
        valid = sel <= qpos[None, :, None]
        ks = jax.vmap(lambda kb, ib: kb[ib])(k, sel)
        vs = jax.vmap(lambda vb, ib: vb[ib])(v, sel)
        qb = lax.dynamic_slice_in_dim(q, t0, QBLOCK_A, axis=1)
        logits = jnp.einsum('bqhd,bqkhd->bhqk', qb, ks).astype(jnp.float32) * scale
        logits = jnp.where(valid[:, None], logits, -jnp.inf)
        p = jax.nn.softmax(logits, axis=-1).astype(v.dtype)
        return jnp.einsum('bhqk,bqkhd->bqhd', p, vs)

    out = lax.map(block, jnp.arange(S // QBLOCK_A))
    return out.transpose(1, 0, 2, 3, 4).reshape(Bsz, S, H, dh)

def dilated_group(q, k, v, window, dilation):
    Bsz, S, G, dh = q.shape
    dv = v.shape[-1]
    n = window // dilation
    L = S // dilation
    nb = -(-L // n)
    Lp = nb * n

    def to_sub(a):
        a = a.reshape(Bsz, L, dilation, G, a.shape[-1]).transpose(0, 2, 1, 3, 4)
        a = jnp.pad(a, ((0, 0), (0, 0), (0, Lp - L), (0, 0), (0, 0)))
        return a.reshape(Bsz, dilation, nb, n, G, a.shape[-1])

    qs, ks, vs = to_sub(q), to_sub(k), to_sub(v)
    shift = ((0, 0), (0, 0), (1, 0), (0, 0), (0, 0), (0, 0))
    kk = jnp.concatenate([jnp.pad(ks[:, :, :-1], shift), ks], axis=3)
    vv = jnp.concatenate([jnp.pad(vs[:, :, :-1], shift), vs], axis=3)
    qi = jnp.arange(n)[:, None] + n
    ki = jnp.arange(2 * n)[None, :]
    dist = qi - ki
    ksub = jnp.arange(nb)[:, None, None] * n + ki[None] - n
    mask = ((dist >= 0) & (dist <= n))[None] & (ksub >= 0)
    logits = jnp.einsum('brnqgd,brnkgd->brngqk', qs, kk).astype(jnp.float32) * (dh ** -0.5)
    logits = jnp.where(mask[None, None, :, None], logits, -jnp.inf)
    lse = jax.nn.logsumexp(logits, axis=-1)
    p = jnp.exp(logits - lse[..., None]).astype(v.dtype)
    out = jnp.einsum('brngqk,brnkgd->brnqgd', p, vv)
    out = out.reshape(Bsz, dilation, Lp, G, dv)[:, :, :L]
    out = out.transpose(0, 2, 1, 3, 4).reshape(Bsz, S, G, dv)
    lse = lse.transpose(0, 1, 2, 4, 3).reshape(Bsz, dilation, Lp, G)[:, :, :L]
    lse = lse.transpose(0, 2, 1, 3).reshape(Bsz, S, G)
    return out, lse

def dilated_attention(q, k, v):
    outs, lses = [], []
    for g, (window, dilation) in enumerate(DIL_PAIRS):
        hs = slice(g * B_GROUP_HEADS, (g + 1) * B_GROUP_HEADS)
        o, l = dilated_group(q[:, :, hs], k[:, :, hs], v, window, dilation)
        outs.append(o)
        lses.append(l)
    wts = jax.nn.softmax(jnp.stack(lses, 0), axis=0).astype(v.dtype)
    return jnp.einsum('gbsh,gbshd->bshd', wts, jnp.stack(outs, 0))

def moba_attention(q, k, v):
    Bsz, S, H, dh = q.shape
    nblk = -(-S // MOBA_BLOCK)
    Sp = nblk * MOBA_BLOCK
    pad = lambda a: jnp.pad(a, ((0, 0), (0, Sp - S), (0, 0), (0, 0)))
    qp = pad(q)
    kbt = pad(k).reshape(Bsz, nblk, MOBA_BLOCK, H, dh).transpose(0, 3, 1, 2, 4)
    vbt = pad(v).reshape(Bsz, nblk, MOBA_BLOCK, H, dh).transpose(0, 3, 1, 2, 4)
    kmean = jnp.mean(kbt.astype(jnp.float32), axis=3)
    ksel = min(MOBA_TOPK, nblk)
    scale = dh ** -0.5
    bidx = jnp.arange(Bsz)[:, None, None, None]
    hidx = jnp.arange(H)[None, :, None, None]

    def block(i):
        t0 = i * QBLOCK_C
        own = t0 // MOBA_BLOCK
        qpos = t0 + jnp.arange(QBLOCK_C)
        qh = lax.dynamic_slice_in_dim(qp, t0, QBLOCK_C, axis=1).transpose(0, 2, 1, 3)
        gate = jnp.einsum('bhqd,bhnd->bhqn', qh.astype(jnp.float32), kmean)
        gate = jnp.where(jnp.arange(nblk) < own, gate, -jnp.inf)
        _, sel = lax.top_k(gate, ksel)
        valid = jnp.repeat(jnp.arange(ksel) < own, MOBA_BLOCK)
        kg = kbt[bidx, hidx, sel]
        vg = vbt[bidx, hidx, sel]
        ko = lax.dynamic_index_in_dim(kbt, own, axis=2, keepdims=False)
        vo = lax.dynamic_index_in_dim(vbt, own, axis=2, keepdims=False)
        kpos = own * MOBA_BLOCK + jnp.arange(MOBA_BLOCK)
        s_sel = jnp.einsum('bhqd,bhqnkd->bhqnk', qh, kg).astype(jnp.float32)
        s_sel = jnp.where(valid, s_sel.reshape(Bsz, H, QBLOCK_C, ksel * MOBA_BLOCK), -jnp.inf)
        s_own = jnp.einsum('bhqd,bhkd->bhqk', qh, ko).astype(jnp.float32)
        s_own = jnp.where(kpos[None, :] <= qpos[:, None], s_own, -jnp.inf)
        p = jax.nn.softmax(jnp.concatenate([s_sel, s_own], -1) * scale, axis=-1).astype(v.dtype)
        p_sel = p[..., :ksel * MOBA_BLOCK].reshape(Bsz, H, QBLOCK_C, ksel, MOBA_BLOCK)
        o = jnp.einsum('bhqnk,bhqnkd->bhqd', p_sel, vg) + jnp.einsum('bhqk,bhkd->bhqd', p[..., ksel * MOBA_BLOCK:], vo)
        return o.transpose(0, 2, 1, 3)

    out = lax.map(block, jnp.arange(Sp // QBLOCK_C))
    return out.transpose(1, 0, 2, 3, 4).reshape(Bsz, Sp, H, dh)[:, :S]

def memory_attention(q, mk, mv):
    logits = jnp.einsum('bshd,bnhd->bhsn', q, mk).astype(jnp.float32) * (HEAD_DIM ** -0.5)
    p = jax.nn.softmax(logits, axis=-1).astype(mv.dtype)
    return jnp.einsum('bhsn,bnhd->bshd', p, mv)

def swiglu(x, w_gate_up, w_down):
    g, u = jnp.split(x @ w_gate_up, 2, axis=-1)
    return (jax.nn.silu(g) * u) @ w_down

def first_inputs(seed: int = 0) -> dict:
    key = jax.random.key(seed)
    ks = jax.random.split(key, 18)
    n_a, n_b, n_c = (DEPTH + 2) // 3, (DEPTH + 1) // 3, DEPTH // 3
    nrm = lambda k, shape, s: jax.random.normal(k, shape, jnp.float32) * s
    gain = lambda k, shape: 1.0 + nrm(k, shape, 0.02)
    offs = jax.random.randint(ks[2], (BATCH, 1), 0, POS_OFFSET_RANGE, dtype=jnp.int32)
    positions = offs + jnp.arange(SEQ, dtype=jnp.int32)[None, :]
    return {
        'x': nrm(ks[0], (BATCH, SEQ, D_MODEL), 1.0),
        'mem': nrm(ks[1], (BATCH, N_MEM, D_MODEL), 1.0),
        'positions': positions,
        'mem_ln_g': gain(ks[3], (D_MODEL,)),
        'mem_ln_b': nrm(ks[4], (D_MODEL,), 0.02),
        'w_in_a': nrm(ks[5], (n_a, D_MODEL, WIDTH_A), D_MODEL ** -0.5),
        'idx_kn_g': gain(ks[6], (n_a, IDX_DIM)),
        'idx_kn_b': nrm(ks[7], (n_a, IDX_DIM), 0.02),
        'w_in_b': nrm(ks[8], (n_b, D_MODEL, WIDTH_BC), D_MODEL ** -0.5),
        'w_in_c': nrm(ks[9], (n_c, D_MODEL, WIDTH_BC), D_MODEL ** -0.5),
        'w_mem_kv': nrm(ks[10], (DEPTH, D_MODEL, 2 * MEM_WIDTH), D_MODEL ** -0.5),
        'w_out': nrm(ks[11], (DEPTH, MIX_WIDTH + MEM_WIDTH, D_MODEL), BETA * (MIX_WIDTH + MEM_WIDTH) ** -0.5),
        'ln1_g': gain(ks[12], (DEPTH, D_MODEL)),
        'ln1_b': nrm(ks[13], (DEPTH, D_MODEL), 0.02),
        'w_gate_up': nrm(ks[14], (DEPTH, D_MODEL, 2 * D_FF), D_MODEL ** -0.5),
        'w_down': nrm(ks[15], (DEPTH, D_FF, D_MODEL), BETA * D_FF ** -0.5),
        'ln2_g': gain(ks[16], (DEPTH, D_MODEL)),
        'ln2_b': nrm(ks[17], (DEPTH, D_MODEL), 0.02),
    }

def first_block(x, mem, positions, mem_ln_g, mem_ln_b, w_in_a, idx_kn_g, idx_kn_b, w_in_b, w_in_c,
              w_mem_kv, w_out, ln1_g, ln1_b, w_gate_up, w_down, ln2_g, ln2_b):
    Bsz, S, _ = x.shape
    cos, sin = rope_tables(positions)
    mem_n = layer_norm(mem, mem_ln_g, mem_ln_b)
    heads = lambda a, h, d: a.reshape(Bsz, S, h, d)
    for i in range(DEPTH):
        kind, j = i % N_MIXERS, i // N_MIXERS
        if kind == 0:
            q, k, v, qi, wi, ki, qm = split_cols(
                x @ w_in_a[j],
                (MIX_WIDTH, MIX_WIDTH, MIX_WIDTH, IDX_HEADS * IDX_DIM, IDX_HEADS, IDX_DIM, MEM_WIDTH))
            q = apply_rope(heads(q, N_HEADS, HEAD_DIM), cos, sin)
            k = apply_rope(heads(k, N_HEADS, HEAD_DIM), cos, sin)
            qi = apply_rope(heads(qi, IDX_HEADS, IDX_DIM), cos, sin)
            ki = apply_rope(layer_norm(ki, idx_kn_g[j], idx_kn_b[j])[:, :, None, :], cos, sin)[:, :, 0]
            wi = wi * (IDX_HEADS * IDX_DIM) ** -0.5
            mix = dsa_attention(q, k, heads(v, N_HEADS, HEAD_DIM), qi, wi, ki)
        elif kind == 1:
            q, k, v, qm = split_cols(x @ w_in_b[j], (MIX_WIDTH, MIX_WIDTH, MIX_WIDTH, MEM_WIDTH))
            q = apply_rope(heads(q, N_HEADS, HEAD_DIM), cos, sin)
            k = apply_rope(heads(k, N_HEADS, HEAD_DIM), cos, sin)
            mix = dilated_attention(q, k, heads(v, B_GROUP_HEADS, B_V_DIM))
        else:
            q, k, v, qm = split_cols(x @ w_in_c[j], (MIX_WIDTH, MIX_WIDTH, MIX_WIDTH, MEM_WIDTH))
            q = apply_rope(heads(q, N_HEADS, HEAD_DIM), cos, sin)
            k = apply_rope(heads(k, N_HEADS, HEAD_DIM), cos, sin)
            mix = moba_attention(q, k, heads(v, N_HEADS, HEAD_DIM))
        mk, mv = jnp.split(mem_n @ w_mem_kv[i], 2, axis=-1)
        mo = memory_attention(heads(qm, N_MEM_HEADS, HEAD_DIM),
                              mk.reshape(Bsz, N_MEM, N_MEM_HEADS, HEAD_DIM),
                              mv.reshape(Bsz, N_MEM, N_MEM_HEADS, HEAD_DIM))
        mixed = jnp.concatenate([mix.reshape(Bsz, S, MIX_WIDTH), mo.reshape(Bsz, S, MEM_WIDTH)], -1) @ w_out[i]
        x = layer_norm(ALPHA * x + mixed, ln1_g[i], ln1_b[i])
        x = layer_norm(ALPHA * x + swiglu(x, w_gate_up[i], w_down[i]), ln2_g[i], ln2_b[i])
    return x


DEPTH_2 = 2

RW_HEADS = 8
RW_HEAD = 64
RW_DIM = RW_HEADS * RW_HEAD
RW_LORA_W = 64
RW_LORA_A = 64
RW_LORA_G = 128
RW_SPLITS = [RW_DIM, 2 * RW_DIM, 3 * RW_DIM, 3 * RW_DIM + RW_LORA_W,
             3 * RW_DIM + RW_LORA_W + RW_LORA_A]
SG_GROUPS = 4
SG_CHUNK = 128
SG_GROUP_DIM = 128
SG_DIM = SG_GROUPS * SG_GROUP_DIM
AB_SHIFT_DIM = 3 * RW_DIM + RW_LORA_W + RW_LORA_A + RW_LORA_G
AB_IN_DIM = AB_SHIFT_DIM + 2 * SG_DIM
AB_MIX_DIM = RW_DIM + SG_DIM

MLA_HEADS = 16
MLA_Q_RANK = 256
MLA_KV_RANK = 256
MLA_NOPE = 64
MLA_ROPE = 32
MLA_V = 64
MLA_QK = MLA_NOPE + MLA_ROPE
MLA_IN_DIM = MLA_Q_RANK + MLA_KV_RANK + MLA_ROPE
MLA_MIX_DIM = MLA_HEADS * MLA_V
ROPE_THETA_2 = 10000.0
Q_BLOCK = 128

MEM_LEN = 256
XA_HEADS = 4
XA_HEAD = D_MODEL // XA_HEADS

MOE_GROUPS = 4
MOE_PER_GROUP = 8
MOE_EXPERTS = MOE_GROUPS * MOE_PER_GROUP
MOE_TOPK = 2
MOE_FF = 512
MOE_BLOCK = 128

DN_ALPHA = (2 * DEPTH_2) ** 0.25
DN_BETA = (8 * DEPTH_2) ** -0.25
RMS_EPS = 1e-6
RW_GN_EPS = 64e-5
N_EVEN = (DEPTH_2 + 1) // 2
N_ODD = DEPTH_2 // 2


def _standardize(x, eps):
    xf = x.astype(jnp.float32)
    mu = jnp.mean(xf, -1, keepdims=True)
    var = jnp.mean(jnp.square(xf - mu), -1, keepdims=True)
    return ((xf - mu) * lax.rsqrt(var + eps)).astype(x.dtype)

def layer_norm_2(x, g, b, eps=LN_EPS):
    return _standardize(x, eps) * g + b

def rms_norm(x, g, eps=RMS_EPS):
    xf = x.astype(jnp.float32)
    return (xf * lax.rsqrt(jnp.mean(xf * xf, -1, keepdims=True) + eps)).astype(x.dtype) * g

def token_shift(p):
    return jnp.pad(p, ((0, 0), (1, 0), (0, 0)))[:, :-1]

def rwkv7_recurrence(r, w, k, v, kk, a):
    B, S, H, N = r.shape

    def step(state, inp):
        r_t, w_t, k_t, v_t, kk_t, a_t = inp
        sa = jnp.einsum('bhvk,bhk->bhv', state, -kk_t)
        state = (state * w_t[:, :, None, :]
                 + sa[..., None] * (kk_t * a_t)[:, :, None, :]
                 + v_t[..., None] * k_t[:, :, None, :])
        return state, jnp.einsum('bhvk,bhk->bhv', state, r_t)

    xs = tuple(jnp.moveaxis(t.astype(jnp.float32), 1, 0) for t in (r, w, k, v, kk, a))
    state0 = jnp.zeros((B, H, N, N), jnp.float32)
    _, y = lax.scan(step, state0, xs)
    return jnp.moveaxis(y, 0, 1)

def rwkv7_mix(p, w0, w2, a0, a2, g2, k_k, k_a, r_k, gn_g, gn_b):
    B, S, _ = p.shape
    heads = lambda t: t.reshape(B, S, RW_HEADS, RW_HEAD)
    r, k, v, w_lo, a_lo, g_lo = jnp.split(p, RW_SPLITS, axis=-1)
    w_log = -jax.nn.softplus(-(w0 + jnp.tanh(w_lo) @ w2)) - 0.5
    decay = jnp.exp(-jnp.exp(w_log.astype(jnp.float32)))
    a = jax.nn.sigmoid(a0 + a_lo @ a2)
    g = jax.nn.sigmoid(g_lo) @ g2
    kk = heads(k * k_k).astype(jnp.float32)
    kk = kk / jnp.maximum(jnp.sqrt(jnp.sum(kk * kk, -1, keepdims=True)), 1e-12)
    k = k * (1.0 + (a - 1.0) * k_a)
    r_h, k_h, v_h = heads(r), heads(k), heads(v)
    y = rwkv7_recurrence(r_h, heads(decay), k_h, v_h, kk, heads(a))
    y = _standardize(y, RW_GN_EPS).astype(p.dtype).reshape(B, S, RW_DIM) * gn_g + gn_b
    bonus = jnp.sum(r_h * k_h * r_k, -1, keepdims=True) * v_h
    return (y + bonus.reshape(B, S, RW_DIM)) * g

def spatial_gating(pu, pv, ln_g, ln_b, ws, bs):
    B, S, _ = pu.shape
    n_chunk = S // SG_CHUNK
    u = jax.nn.gelu(pu)
    z = jax.nn.gelu(pv).reshape(B, n_chunk, SG_CHUNK, SG_GROUPS, SG_GROUP_DIM)
    z = layer_norm_2(z, ln_g, ln_b)
    causal = jnp.tril(jnp.ones((SG_CHUNK, SG_CHUNK), dtype=bool))
    wm = jnp.where(causal, ws, jnp.zeros_like(ws))
    zs = jnp.einsum('gts,bcsgd->bctgd', wm, z) + bs.T[:, :, None]
    return u * zs.reshape(B, S, SG_DIM)

def mixer_ab(x, w_in, mu, w0, w2, a0, a2, g2, k_k, k_a, r_k, gn_g, gn_b,
             ln_g, ln_b, ws, bs, w_out):
    p = x @ w_in
    ps = p[..., :AB_SHIFT_DIM]
    pu = p[..., AB_SHIFT_DIM:AB_SHIFT_DIM + SG_DIM]
    pv = p[..., AB_SHIFT_DIM + SG_DIM:]
    ps = ps + (token_shift(ps) - ps) * mu
    ya = rwkv7_mix(ps, w0, w2, a0, a2, g2, k_k, k_a, r_k, gn_g, gn_b)
    yb = spatial_gating(pu, pv, ln_g, ln_b, ws, bs)
    return jnp.concatenate([ya, yb], axis=-1) @ w_out

def rope(x):
    S = x.shape[1]
    half = x.shape[-1] // 2
    inv = ROPE_THETA_2 ** (-jnp.arange(half, dtype=jnp.float32) / half)
    ang = jnp.arange(S, dtype=jnp.float32)[:, None] * inv[None, :]
    cos = jnp.cos(ang)[None, :, None, :]
    sin = jnp.sin(ang)[None, :, None, :]
    xf = x.astype(jnp.float32)
    x1, x2 = xf[..., :half], xf[..., half:]
    return jnp.concatenate([x1 * cos - x2 * sin, x1 * sin + x2 * cos], -1).astype(x.dtype)

def causal_block_attention(q, k, v):
    B, S, H, Dk = q.shape
    n_blk = S // Q_BLOCK
    scale = Dk ** -0.5
    qb = jnp.moveaxis(q.reshape(B, n_blk, Q_BLOCK, H, Dk), 1, 0)
    k_idx = jnp.arange(S)

    def one_block(args):
        q_blk, i = args
        s = jnp.einsum('bqhd,bkhd->bhqk', q_blk, k).astype(jnp.float32) * scale
        q_idx = i * Q_BLOCK + jnp.arange(Q_BLOCK)
        s = jnp.where(k_idx[None, :] <= q_idx[:, None], s, -jnp.inf)
        pr = jax.nn.softmax(s, axis=-1).astype(v.dtype)
        return jnp.einsum('bhqk,bkhd->bqhd', pr, v)

    o = lax.map(one_block, (qb, jnp.arange(n_blk)))
    return jnp.moveaxis(o, 0, 1).reshape(B, S, H, v.shape[-1])

def mla(x, w_in, q_norm, kv_norm, wq_b, wkv_b, w_out):
    B, S, _ = x.shape
    p = x @ w_in
    cq = p[..., :MLA_Q_RANK]
    ckv = p[..., MLA_Q_RANK:MLA_Q_RANK + MLA_KV_RANK]
    k_pe = p[..., MLA_Q_RANK + MLA_KV_RANK:]
    q = (rms_norm(cq, q_norm) @ wq_b).reshape(B, S, MLA_HEADS, MLA_QK)
    kv = (rms_norm(ckv, kv_norm) @ wkv_b).reshape(B, S, MLA_HEADS, MLA_NOPE + MLA_V)
    q_nope, q_pe = q[..., :MLA_NOPE], rope(q[..., MLA_NOPE:])
    k_nope, v = kv[..., :MLA_NOPE], kv[..., MLA_NOPE:]
    k_pe = rope(k_pe[:, :, None, :])
    qf = jnp.concatenate([q_nope, q_pe], -1)
    kf = jnp.concatenate([k_nope, jnp.broadcast_to(k_pe, (B, S, MLA_HEADS, MLA_ROPE))], -1)
    o = causal_block_attention(qf, kf, v)
    return o.reshape(B, S, MLA_MIX_DIM) @ w_out

def mem_cross_attention(x, mem, wq, wkv, wo):
    B, S, D = x.shape
    M = mem.shape[1]
    q = (x @ wq).reshape(B, S, XA_HEADS, XA_HEAD)
    kv = (mem @ wkv).reshape(B, M, 2, XA_HEADS, XA_HEAD)
    k, v = kv[:, :, 0], kv[:, :, 1]
    s = jnp.einsum('bqhd,bmhd->bhqm', q, k).astype(jnp.float32) * (XA_HEAD ** -0.5)
    pr = jax.nn.softmax(s, axis=-1).astype(v.dtype)
    o = jnp.einsum('bhqm,bmhd->bqhd', pr, v)
    return o.reshape(B, S, D) @ wo

def grouped_experts(xf, expert, gate, w_gate, w_up, w_down):
    T, D = xf.shape
    A = T * MOE_TOPK
    n_blk = -(-A // MOE_BLOCK) + MOE_EXPERTS
    L = n_blk * MOE_BLOCK
    flat_e = expert.reshape(-1)
    order = jnp.argsort(flat_e)
    sorted_e = flat_e[order]
    tok = (order // MOE_TOPK).astype(jnp.int32)
    counts = jnp.bincount(flat_e, length=MOE_EXPERTS)
    padded = (counts + MOE_BLOCK - 1) // MOE_BLOCK * MOE_BLOCK
    pad_end = jnp.cumsum(padded)
    pad_start = pad_end - padded
    start = jnp.cumsum(counts) - counts
    dest = (pad_start[sorted_e] + jnp.arange(A) - start[sorted_e]).astype(jnp.int32)
    row_tok = jnp.full((L,), T, dtype=jnp.int32).at[dest].set(tok)
    blk_expert = jnp.minimum(
        jnp.searchsorted(pad_end, jnp.arange(n_blk) * MOE_BLOCK, side='right'),
        MOE_EXPERTS - 1)
    x_rows = jnp.concatenate([xf, jnp.zeros((1, D), xf.dtype)], 0)[row_tok]
    x_rows = x_rows.reshape(n_blk, MOE_BLOCK, D)

    def expert_block(args):
        xb, e = args
        h = jax.nn.silu(xb @ w_gate[e]) * (xb @ w_up[e])
        return h @ w_down[e]

    y_rows = lax.map(expert_block, (x_rows, blk_expert)).reshape(L, D)
    y_assign = y_rows[dest] * gate.reshape(-1)[order][:, None]
    return jax.ops.segment_sum(y_assign, tok, num_segments=T)

def hier_moe(x, w_group, b_group, w_expert, b_expert, w_gate, w_up, w_down):
    B, S, D = x.shape
    xf = x.reshape(-1, D)
    T = xf.shape[0]
    g_logits = (xf @ w_group).astype(jnp.float32) + b_group
    g_prob = jax.nn.softmax(g_logits, axis=-1)
    grp = jnp.argmax(g_logits, axis=-1)
    p_grp = jnp.take_along_axis(g_prob, grp[:, None], axis=-1)
    e_logits = ((xf @ w_expert).astype(jnp.float32) + b_expert).reshape(
        T, MOE_GROUPS, MOE_PER_GROUP)
    e_logits = jnp.take_along_axis(e_logits, grp[:, None, None], axis=1)[:, 0]
    top_v, top_i = lax.top_k(e_logits, MOE_TOPK)
    gate = (jax.nn.softmax(top_v, axis=-1) * p_grp).astype(x.dtype)
    expert = (grp[:, None] * MOE_PER_GROUP + top_i).astype(jnp.int32)
    y = grouped_experts(xf, expert, gate, w_gate, w_up, w_down)
    return y.reshape(B, S, D)

def second_inputs(seed: int = 0) -> dict:
    key = jax.random.key(seed)
    ks = iter(jax.random.split(key, 48))

    def normal(shape, scale):
        return jax.random.normal(next(ks), shape, jnp.float32) * scale

    def gain(shape):
        return 1.0 + normal(shape, 0.02)

    D = D_MODEL
    NE, NO, L = N_EVEN, N_ODD, DEPTH_2
    return {
        'x': normal((BATCH, SEQ, D), 1.0),
        'mem': normal((BATCH, MEM_LEN, D), 1.0),
        'ab_w_in': normal((NE, D, AB_IN_DIM), D ** -0.5),
        'ab_mu': jax.random.uniform(next(ks), (NE, AB_SHIFT_DIM), jnp.float32),
        'rw_w0': jax.random.uniform(next(ks), (NE, RW_DIM), jnp.float32, -6.5, -1.5),
        'rw_w2': normal((NE, RW_LORA_W, RW_DIM), 0.5 * RW_LORA_W ** -0.5),
        'rw_a0': normal((NE, RW_DIM), 0.3),
        'rw_a2': normal((NE, RW_LORA_A, RW_DIM), RW_LORA_A ** -0.5),
        'rw_g2': normal((NE, RW_LORA_G, RW_DIM), RW_LORA_G ** -0.5),
        'rw_k_k': 0.85 + normal((NE, RW_DIM), 0.05),
        'rw_k_a': 1.0 + normal((NE, RW_DIM), 0.05),
        'rw_r_k': normal((NE, RW_HEADS, RW_HEAD), 0.1),
        'rw_gn_g': gain((NE, RW_DIM)),
        'rw_gn_b': normal((NE, RW_DIM), 0.02),
        'sg_ln_g': gain((NE, SG_GROUPS, SG_GROUP_DIM)),
        'sg_ln_b': normal((NE, SG_GROUPS, SG_GROUP_DIM), 0.02),
        'sg_ws': normal((NE, SG_GROUPS, SG_CHUNK, SG_CHUNK), 0.5 * SG_CHUNK ** -0.5),
        'sg_b': 1.0 + normal((NE, SG_GROUPS, SG_CHUNK), 0.1),
        'ab_w_out': normal((NE, AB_MIX_DIM, D), DN_BETA * AB_MIX_DIM ** -0.5),
        'mla_w_in': normal((NO, D, MLA_IN_DIM), D ** -0.5),
        'mla_q_norm': gain((NO, MLA_Q_RANK)),
        'mla_kv_norm': gain((NO, MLA_KV_RANK)),
        'mla_wq_b': normal((NO, MLA_Q_RANK, MLA_HEADS * MLA_QK), MLA_Q_RANK ** -0.5),
        'mla_wkv_b': normal((NO, MLA_KV_RANK, MLA_HEADS * (MLA_NOPE + MLA_V)), MLA_KV_RANK ** -0.5),
        'mla_w_out': normal((NO, MLA_MIX_DIM, D), DN_BETA * MLA_MIX_DIM ** -0.5),
        'ln1_g': gain((L, D)),
        'ln1_b': normal((L, D), 0.02),
        'xa_wq': normal((L, D, D), D ** -0.5),
        'xa_wkv': normal((L, D, 2 * D), D ** -0.5),
        'xa_wo': normal((L, D, D), DN_BETA * D ** -0.5),
        'ln2_g': gain((L, D)),
        'ln2_b': normal((L, D), 0.02),
        'moe_w_group': normal((L, D, MOE_GROUPS), D ** -0.5),
        'moe_b_group': normal((L, MOE_GROUPS), 0.01),
        'moe_w_expert': normal((L, D, MOE_EXPERTS), D ** -0.5),
        'moe_b_expert': normal((L, MOE_EXPERTS), 0.01),
        'moe_w_gate': normal((L, MOE_EXPERTS, D, MOE_FF), D ** -0.5),
        'moe_w_up': normal((L, MOE_EXPERTS, D, MOE_FF), D ** -0.5),
        'moe_w_down': normal((L, MOE_EXPERTS, MOE_FF, D), DN_BETA * MOE_FF ** -0.5),
        'ln3_g': gain((L, D)),
        'ln3_b': normal((L, D), 0.02),
    }

def second_block(x, mem, ab_w_in, ab_mu, rw_w0, rw_w2, rw_a0, rw_a2, rw_g2, rw_k_k,
              rw_k_a, rw_r_k, rw_gn_g, rw_gn_b, sg_ln_g, sg_ln_b, sg_ws, sg_b,
              ab_w_out, mla_w_in, mla_q_norm, mla_kv_norm, mla_wq_b, mla_wkv_b,
              mla_w_out, ln1_g, ln1_b, xa_wq, xa_wkv, xa_wo, ln2_g, ln2_b,
              moe_w_group, moe_b_group, moe_w_expert, moe_b_expert, moe_w_gate,
              moe_w_up, moe_w_down, ln3_g, ln3_b):
    h = x
    for layer in range(DEPTH_2):
        j = layer // 2
        if layer % 2 == 0:
            mix = mixer_ab(h, ab_w_in[j], ab_mu[j], rw_w0[j], rw_w2[j], rw_a0[j],
                           rw_a2[j], rw_g2[j], rw_k_k[j], rw_k_a[j], rw_r_k[j],
                           rw_gn_g[j], rw_gn_b[j], sg_ln_g[j], sg_ln_b[j], sg_ws[j],
                           sg_b[j], ab_w_out[j])
        else:
            mix = mla(h, mla_w_in[j], mla_q_norm[j], mla_kv_norm[j], mla_wq_b[j],
                      mla_wkv_b[j], mla_w_out[j])
        h = layer_norm_2(DN_ALPHA * h + mix, ln1_g[layer], ln1_b[layer])
        xa = mem_cross_attention(h, mem, xa_wq[layer], xa_wkv[layer], xa_wo[layer])
        h = layer_norm_2(DN_ALPHA * h + xa, ln2_g[layer], ln2_b[layer])
        ff = hier_moe(h, moe_w_group[layer], moe_b_group[layer], moe_w_expert[layer],
                      moe_b_expert[layer], moe_w_gate[layer], moe_w_up[layer],
                      moe_w_down[layer])
        h = layer_norm_2(DN_ALPHA * h + ff, ln3_g[layer], ln3_b[layer])
    return h


def setup_inputs(seed=0):
    out = dict(first_inputs(seed))
    for name, value in second_inputs(seed + 1).items():
        if name != "x":
            out[name + "_2"] = value
    return out


def reference(
    x, mem, positions, mem_ln_g, mem_ln_b, w_in_a, idx_kn_g, idx_kn_b, w_in_b, w_in_c, w_mem_kv,
    w_out, ln1_g, ln1_b, w_gate_up, w_down, ln2_g, ln2_b, mem_2, ab_w_in_2, ab_mu_2, rw_w0_2,
    rw_w2_2, rw_a0_2, rw_a2_2, rw_g2_2, rw_k_k_2, rw_k_a_2, rw_r_k_2, rw_gn_g_2, rw_gn_b_2,
    sg_ln_g_2, sg_ln_b_2, sg_ws_2, sg_b_2, ab_w_out_2, mla_w_in_2, mla_q_norm_2, mla_kv_norm_2,
    mla_wq_b_2, mla_wkv_b_2, mla_w_out_2, ln1_g_2, ln1_b_2, xa_wq_2, xa_wkv_2, xa_wo_2, ln2_g_2,
    ln2_b_2, moe_w_group_2, moe_b_group_2, moe_w_expert_2, moe_b_expert_2, moe_w_gate_2,
    moe_w_up_2, moe_w_down_2, ln3_g_2, ln3_b_2,
):
    x = first_block(
        x, mem, positions, mem_ln_g, mem_ln_b, w_in_a, idx_kn_g, idx_kn_b, w_in_b, w_in_c,
        w_mem_kv, w_out, ln1_g, ln1_b, w_gate_up, w_down, ln2_g, ln2_b,
    )
    return second_block(
        x, mem_2, ab_w_in_2, ab_mu_2, rw_w0_2, rw_w2_2, rw_a0_2, rw_a2_2, rw_g2_2, rw_k_k_2,
        rw_k_a_2, rw_r_k_2, rw_gn_g_2, rw_gn_b_2, sg_ln_g_2, sg_ln_b_2, sg_ws_2, sg_b_2,
        ab_w_out_2, mla_w_in_2, mla_q_norm_2, mla_kv_norm_2, mla_wq_b_2, mla_wkv_b_2,
        mla_w_out_2, ln1_g_2, ln1_b_2, xa_wq_2, xa_wkv_2, xa_wo_2, ln2_g_2, ln2_b_2,
        moe_w_group_2, moe_b_group_2, moe_w_expert_2, moe_b_expert_2, moe_w_gate_2, moe_w_up_2,
        moe_w_down_2, ln3_g_2, ln3_b_2,
    )


_drawn_inputs = setup_inputs


def setup_inputs(seed=0):
    import zlib

    import numpy as np

    out = dict(_drawn_inputs(seed))
    spreads = {}
    factors = {'mem_ln_g': 8.0,
     'mem_ln_b': 5.239,
     'idx_kn_g': 6.04,
     'idx_kn_b': 8.0,
     'rw_w2_2': 8.0,
     'rw_a0_2': 2.786,
     'rw_k_k_2': 6.945,
     'rw_k_a_2': 4.851,
     'rw_gn_g_2': 8.0,
     'rw_gn_b_2': 8.0,
     'sg_ln_g_2': 8.0,
     'sg_ln_b_2': 8.0,
     'mla_q_norm_2': 8.0,
     'mla_kv_norm_2': 8.0,
     'moe_b_group_2': 8.0,
     'moe_b_expert_2': 8.0}
    for name, (base, spread) in spreads.items():
        noise = np.random.default_rng([zlib.crc32(name.encode()), seed]).standard_normal(out[name].shape)
        drawn = base * np.exp(spread * noise) if base else spread * noise
        out[name] = jnp.asarray(drawn.astype(out[name].dtype))
    for name, factor in factors.items():
        out[name] = (out[name] * factor).astype(out[name].dtype)
    return out
```

```python
import math
from contextlib import ExitStack, contextmanager

import numpy as np

import concourse.bass as bass
from concourse import mybir

ALU = mybir.AluOpType
ACT = mybir.ActivationFunctionType
AX = mybir.AxisListType
F32 = mybir.dt.float32
I32 = mybir.dt.int32
U32 = mybir.dt.uint32

P = 128
D = 1024
SEQ = 256
NT = SEQ // P
KD = D // P
MASKED = -1.0e30
TAKEN = -2.0e30
LN_EPS = 1e-5

DEPTH = 4
HEADS, DH = 12, 64
MIX = HEADS * DH
MEM_HEADS = 4
ROPE_HALF = DH // 8
ROPE_THETA = 500000.0
IDX_HEADS = 8
TOPK = SEQ // 4
WIDTH_A = 3 * MIX + IDX_HEADS * DH + IDX_HEADS + DH + MEM_HEADS * DH
WIDTH_BC = 3 * MIX + MEM_HEADS * DH
D_FF = -(-8 * D // (3 * 256)) * 256
ALPHA = (2 * DEPTH) ** 0.25
DILATIONS = (1, 4, 16)
DIL_WINDOW = 128

DEPTH_2 = 2
ALPHA_2 = (2 * DEPTH_2) ** 0.25
RW_HEADS, RW_DIM = 8, 512
RW_CHUNK = 64
RW_SHIFT = 3 * RW_DIM + 64 + 64 + 128
RW_GN_EPS = 64e-5
SG_GROUPS = 4
AB_IN = RW_SHIFT + 1024
MLA_HEADS = 16
MLA_IN = 256 + 256 + 32
RMS_EPS = 1e-6
XA_HEADS = 4
GROUPS, PER_GROUP = 4, 8
EXPERTS = GROUPS * PER_GROUP
MOE_FF = 512

RING = 12
SLOT = 2048

FIRST_LAYERS = DEPTH
SECOND_LAYERS = DEPTH_2
ROOTS = NT * (1 + 2 * FIRST_LAYERS + len(range(0, FIRST_LAYERS, 3)) + 3 * SECOND_LAYERS
              + 3 * len(range(0, SECOND_LAYERS, 2)) + len(range(1, SECOND_LAYERS, 2)))
LAYER_NORMS = 1 + 2 * FIRST_LAYERS + 3 * SECOND_LAYERS
RW_SLOTS = (1, 4, 3, 5, 2, 1)

CONST_PARTS = [("ident", P), ("causal", NT * SEQ), ("dilated", 3 * NT * SEQ), ("inv_freq", ROPE_HALF),
               ("rw_masks", 4 * P), ("rw_levels", 6 * P), ("rw_chunk", 2), ("sg_mask", P),
               ("rope2_cos", NT * 16), ("rope2_sin", NT * 16), ("numbers", EXPERTS), ("one", P)]
CONST_AT = {}
for _name, _size in CONST_PARTS:
    CONST_AT[_name] = (sum(n for _, n in CONST_PARTS[:len(CONST_AT)]), _size)
CONST_WIDTH = sum(n for _, n in CONST_PARTS)


def shape_constants():
    c = np.zeros((P, CONST_WIDTH), np.float32)

    def put(name, a):
        at, n = CONST_AT[name]
        c[:, at:at + n] = np.asarray(a, np.float32).reshape(P, n)

    p = np.arange(P)
    q = p[:, None, None] + P * np.arange(NT)[None, :, None]
    k = np.arange(SEQ)[None, None, :]
    put("ident", np.eye(P))
    put("causal", np.where(k <= q, 0.0, MASKED))
    put("dilated", np.stack([np.where((k <= q) & ((q - k) % r == 0) & (q - k <= r * DIL_WINDOW), 0.0, MASKED)
                             for r in DILATIONS], axis=1))
    put("inv_freq", np.tile(np.float32(ROPE_THETA) ** (-np.arange(ROPE_HALF, dtype=np.float32) / ROPE_HALF), (P, 1)))
    row, col = p[:, None], p[None, :]
    same = row // RW_CHUNK == col // RW_CHUNK
    strict, upto = same & (row < col), same & (row <= col)
    put("rw_masks", np.concatenate([strict, upto, strict, upto], axis=1))
    put("rw_levels", np.concatenate([(row // s + 1 == col // s) & (col // s % 2 == 1)
                                     for s in (1, 2, 4, 8, 16, 32)], axis=1))
    put("rw_chunk", p[:, None] // RW_CHUNK == np.arange(2)[None, :])
    put("sg_mask", col <= row)
    inv2 = np.float32(10000.0) ** (-np.arange(16, dtype=np.float32) / 16)
    ang = (p[:, None] + P * np.arange(NT)[None, :]).astype(np.float32)[..., None] * inv2
    put("rope2_cos", np.cos(ang))
    put("rope2_sin", np.sin(ang))
    put("numbers", np.tile(np.arange(EXPERTS), (P, 1)))
    put("one", np.broadcast_to(row == 0, (P, P)))
    return c


class Tally:

    def __init__(self, sem, ahead=0):
        self.sem = sem
        self.n = -ahead
        self.turn = None

    def skip(self, k=1):
        self.n += k

    def next(self, k=1):
        self.n += k
        return self.value()

    def due(self):
        self.n += 1
        return self.turn is not None or self.n > 0

    def value(self):
        if self.turn is None:
            return self.n
        i, per = self.turn
        assert self.n > 0
        return i * per + self.n


@contextmanager
def rounds(eng, count, per):
    first = {t: t.n for t in per}
    with eng.Fori(0, count) as i:
        for t, k in per.items():
            t.turn = (i, k)
        yield i
        for t, k in per.items():
            assert t.n - first[t] == k, (t.sem, t.n - first[t], k)
            t.turn = None
            t.n = first[t] + k * count


def chunks_of(width):
    return [(c, min(512, width - c)) for c in range(0, width, 512)]


def build(nc, A, out):
    ctx = ExitStack()
    with ctx:
        def sem(name):
            return ctx.enter_context(nc.semaphore(name))

        def psum(name, banks):
            return ctx.enter_context(nc.psum_tensor(name, [P, banks, 512], F32))

        ring = ctx.enter_context(nc.sbuf_tensor("ring", [P, RING, SLOT], F32))
        x = ctx.enter_context(nc.sbuf_tensor("x", [P, NT, D], F32))
        ident = ctx.enter_context(nc.sbuf_tensor("ident", [P, P], F32))
        causal = ctx.enter_context(nc.sbuf_tensor("causal", [P, NT, SEQ], F32))
        small = ctx.enter_context(nc.sbuf_tensor("small", [P, 128], F32))
        ints = ctx.enter_context(nc.sbuf_tensor("ints", [P, 16], U32))
        roots = ctx.enter_context(nc.sbuf_tensor("roots", [P, 5, 8], F32))
        ARENA = 25056
        arena = ctx.enter_context(nc.sbuf_tensor("arena", [P, ARENA], F32))

        def at(offset, *dims):
            n = math.prod(dims)
            assert offset + n <= ARENA, (offset, dims)
            v = arena[:, offset:offset + n]
            if len(dims) == 1:
                return v
            names = "abcde"[:len(dims)]
            return v.rearrange(f"p ({' '.join(names)}) -> p {' '.join(names)}",
                               **dict(zip(names, dims)))

        xT = at(0, KD, SEQ)
        mixT = at(2048, KD, SEQ)
        memT = at(4096, KD, SEQ)
        PROJ = 6144
        projA = at(PROJ, NT, WIDTH_A)
        projBC = at(PROJ, NT, WIDTH_BC)
        dilated12 = at(PROJ + NT * WIDTH_BC, 2, NT, SEQ)
        QKT = PROJ + NT * WIDTH_A
        qkT = at(QKT, 21, SEQ)
        mkv = at(QKT + 21 * SEQ, NT, 512)
        ATT = QKT + 21 * SEQ + NT * 512
        S1 = at(ATT, 2, NT, 1, SEQ)
        S3 = at(ATT, 2, NT, 3, SEQ)
        Pn = at(ATT + 3072, 2, NT, SEQ)
        PT = at(ATT + 4096, 2, NT, SEQ)
        dsa_mask = at(ATT + 5120, NT, SEQ)
        dilated0 = dsa_mask
        idx_relu = at(ATT + 2048, 2, 2, SEQ)
        idx_score = at(ATT + 1024, NT, SEQ)
        ki2 = at(ATT, NT, 2, DH)
        rope_tmp = at(ATT + 3072, 4, 24 * ROPE_HALF)
        memrows = at(PROJ, NT, D)
        silu_g = at(PROJ, 2, SEQ)
        hT = at(PROJ + 512, 2, 4, SEQ)
        GATE = PROJ + 512 + 2048
        gates = at(GATE, NT, EXPERTS)
        logits36 = at(GATE + 64, NT, GROUPS + EXPERTS)
        picked = at(GATE + 160, NT, GROUPS, PER_GROUP)
        group_hot = at(GATE + 224, NT, GROUPS)
        group8 = at(GATE + 240, NT, 8)
        top8 = at(GATE + 256, NT, 8)
        router = at(GATE + 272, NT, 16)
        hot = at(GATE + 304, NT, EXPERTS)
        numbers = at(GATE + 368, EXPERTS)
        p_ab = at(PROJ, NT, AB_IN)
        RW = PROJ + NT * AB_IN
        shifted = at(RW, NT, RW_SHIFT)
        rw_a, rw_kk, rw_b, rw_k, rw_r, rw_pinv, rw_pexc, rw_tmp, rw_g, rw_lw = [at(RW + 512 * j, 512) for j in range(10)]
        rwT = at(RW + 5120, 4, 4, P)
        rw_G = at(RW + 7168, RW_HEADS, 4 * P)
        rw_X = at(RW + 11264, RW_HEADS, P)
        rw_XT = at(0, RW_HEADS, P)
        rw_T1 = at(1024, RW_HEADS, P)
        rw_BT = at(4096, RW_HEADS, P)
        loraT = at(5120, 2, P)
        rw_state = at(5376, 4, 64)
        rw_U = at(5632, 512)
        rw_SA = at(RW + 12288, 512)
        rw_decay = at(RW + 12800, 4, 2)
        stat8 = at(RW + 12816, 8)
        wmT = at(2048, SG_GROUPS, P)
        rw_y = at(2560, 512)
        mla_q = at(PROJ, NT, MLA_HEADS, 96)
        mla_kv = at(PROJ + 3072, NT, MLA_HEADS, P)
        mlaT = at(PROJ + 7168, 21, SEQ)
        mlaT_more = at(0, 4, SEQ)
        mla_p = at(ATT, NT, MLA_IN)
        mla_qpe = at(ATT + 1088, NT, MLA_HEADS, 2, 32)
        mla_tmp = at(ATT + 3200, 4, 256)
        rope2 = at(ATT + 4480, 64)
        mla_kpe = at(ATT + 4224, NT, 4, 32)
        mla_qn = at(2048, NT, MLA_HEADS, 64)
        mla_kn = [at(1024, MLA_HEADS, 64), at(ATT + 5120, MLA_HEADS, 64)]
        latentT = at(2304, 4, SEQ)
        xa_v = at(PROJ, NT, D)
        xa_qT = at(PROJ + 2048, KD, SEQ)
        xa_kT = at(PROJ + 4096, KD, SEQ)
        root_in, root_out, root_power = roots[:, 0:2, :], roots[:, 2:4, :], roots[:, 4, :]
        rope_cos = small[:, 0:16].rearrange("p (t f) -> p t f", t=NT)
        rope_sin = small[:, 16:32].rearrange("p (t f) -> p t f", t=NT)
        bn = small[:, 32:56].rearrange("p (t f) -> p t f", t=NT)
        mean_var = small[:, 56:60].rearrange("p (t f) -> p t f", t=NT)
        negmax = small[:, 64:68].rearrange("p (b t) -> p b t", b=2)
        rowsum = small[:, 68:72].rearrange("p (b t) -> p b t", b=2)
        rinv = small[:, 72:76].rearrange("p (b t) -> p b t", b=2)
        pos_f = small[:, 76:78]
        inv_freq = small[:, 80:88]
        top_score = small[:, 88:96]
        angle = small[:, 96:112].rearrange("p (t f) -> p t f", t=NT)
        turns = small[:, 112:128].rearrange("p (t f) -> p t f", t=NT)

        lin = psum("lin", 4)
        trp = psum("trp", 2)
        sco = psum("sco", 2)

        slot_full = [sem(f"slot_full{s}") for s in range(RING)]
        slots_used = sem("slots_used")
        input_loaded = sem("input_loaded")
        proj_done = sem("proj_done")
        tr_full, tr_done = sem("tr_full"), sem("tr_done")
        ln_done = sem("ln_done")
        rope_done = sem("rope_done")
        logit_full, logit_free = sem("logit_full"), sem("logit_free")
        smax_done, exp_done, p_done = sem("smax_done"), sem("exp_done"), sem("p_done")
        pt_full, pt_done = sem("pt_full"), sem("pt_done")
        pv_full, pv_done = sem("pv_full"), sem("pv_done")
        dots_full, dots_done, score_added = sem("dots_full"), sem("dots_done"), sem("score_added")
        gu_full, silu_done, h_done = sem("gu_full"), sem("silu_done"), sem("h_done")
        y_added = sem("y_added")
        gm_full, gm_done = sem("gm_full"), sem("gm_done")
        vec_for_pe, vec_for_act = sem("vec_for_pe"), sem("vec_for_act")
        act_for_pe, act_for_vec = sem("act_for_pe"), sem("act_for_vec")
        pe_for_act, pe_for_vec = sem("pe_for_act"), sem("pe_for_vec")
        shift_loaded = sem("shift_loaded")
        dve_step = sem("dve_step")
        root_asked, root_done = sem("root_asked"), sem("root_done")
        pool_step = sem("pool_step")
        out_written = sem("out_written")

        def kind_of(layer):
            return layer % 3

        block = ctx.enter_context(nc.Block())

        @block.sync
        def _(sp):
            free = Tally(slots_used, ahead=RING)
            place = [0]

            def slot():
                if free.due():
                    sp.wait_ge(slots_used, free.value())
                s = place[0] % RING
                place[0] += 1
                return s

            def load(s, lo, hi, src):
                dst = ring[:, s, lo:hi]
                if len(src.shape) == 3:
                    dst = dst.rearrange("p (k n) -> p k n", k=src.shape[1])
                sp.dma_start(dst, src).then_inc(slot_full[s], 16)

            def load_linear(w):
                K, N = w.shape
                per = min(4, K // P)
                for c, n in chunks_of(N):
                    for k in range(0, K // P, per):
                        load(slot(), 0, per * n,
                             w[k * P:(k + per) * P, c:c + n].rearrange("(k p) n -> p k n", p=P))

            def rows(v):
                return v.partition_broadcast(P)

            def load_ln(g, b):
                s = slot()
                load(s, 0, D, rows(g))
                load(s, D, 2 * D, rows(b))

            def load_ffn(gate_up, down):
                def unit(u):
                    f = u * 2 * P
                    load(slot(), 0, SLOT, gate_up[:, bass.ds(f, 2 * P)].rearrange("(k p) n -> p k n", p=P))
                    load(slot(), 0, SLOT, gate_up[:, bass.ds(f + D_FF, 2 * P)].rearrange("(k p) n -> p k n", p=P))
                    load(slot(), 0, SLOT, down[bass.ds(f, 2 * P), :].rearrange("(k p) n -> p k n", p=P))
                units = D_FF // (2 * P)
                with rounds(sp, units // 4, {free: RING}) as i:
                    for u in range(4):
                        unit(i * 4 + u)
                place[0] += (units // 4 - 1) * RING
                for u in range(units // 4 * 4, units):
                    unit(u)

            def load_moe(layer):
                s = slot()
                v = ring[:, s, 0:KD * 36].rearrange("p (k n) -> p k n", k=KD)
                for lo, hi, name in ((0, GROUPS, "moe_w_group_2"), (GROUPS, 36, "moe_w_expert_2")):
                    sp.dma_start(v[:, :, lo:hi], A[name][layer].rearrange("(k p) n -> p k n", p=P)).then_inc(slot_full[s], 16)
                load(s, 512, 516, rows(A["moe_b_group_2"][layer]))
                load(s, 516, 548, rows(A["moe_b_expert_2"][layer]))
                at_n = CONST_AT["numbers"][0]
                load(s, 640, 640 + EXPERTS + P, A["consts"][:, at_n:at_n + EXPERTS + P])

                def expert(e):
                    for name in ("moe_w_gate_2", "moe_w_up_2"):
                        for k in range(2):
                            load(slot(), 0, SLOT, A[name][layer, e, k * 512:(k + 1) * 512, :].rearrange("(k p) n -> p k n", p=P))
                    for f in range(2):
                        load(slot(), 0, SLOT, A["moe_w_down_2"][layer, e, f * 256:(f + 1) * 256, :].rearrange("(k p) n -> p k n", p=P))
                with rounds(sp, EXPERTS // 2, {free: RING}) as i:
                    for e in range(2):
                        expert(i * 2 + e)
                place[0] += (EXPERTS // 2 - 1) * RING

            def const(name):
                a, n = CONST_AT[name]
                return A["consts"][:, a:a + n]

            def first(dst, src):
                sp.dma_start(dst, src).then_inc(input_loaded, 16)
            first(ident[:, :], const("ident"))
            first(causal[:, :, :].rearrange("p t k -> p (t k)"), const("causal"))
            first(inv_freq, const("inv_freq"))
            first(ints[:, 0:NT].bitcast(I32), A["positions"])
            first(x[:, :, :], A["x"][0].rearrange("(t p) d -> p t d", p=P))
            first(memrows, A["mem"][0].rearrange("(t p) d -> p t d", p=P))
            load_ln(A["mem_ln_g"], A["mem_ln_b"])
            for layer in range(FIRST_LAYERS):
                kind, j = kind_of(layer), layer // 3
                w_in = (A["w_in_a"], A["w_in_b"], A["w_in_c"])[kind][j]
                load_linear(w_in)
                load_linear(A["w_mem_kv"][layer])
                if kind == 0:
                    s = slot()
                    load(s, 0, DH, rows(A["idx_kn_g"][j]))
                    load(s, DH, 2 * DH, rows(A["idx_kn_b"][j]))
                if kind == 1:
                    s = slot()
                    load(s, 0, 3 * NT * SEQ, const("dilated"))
                load_linear(A["w_out"][layer])
                load_ln(A["ln1_g"][layer], A["ln1_b"][layer])
                load_ffn(A["w_gate_up"][layer], A["w_down"][layer])
                load_ln(A["ln2_g"][layer], A["ln2_b"][layer])

            for layer in range(SECOND_LAYERS):
                j = layer // 2
                if layer % 2 == 0:
                    load_linear(A["ab_w_in_2"][j])
                    s = slot()
                    load(s, 0, RW_SHIFT, rows(A["ab_mu_2"][j]))
                    s = slot()
                    for n, name in enumerate(("rw_w0_2", "rw_a0_2", "rw_k_k_2", "rw_k_a_2")):
                        load(s, 512 * n, 512 * n + 512, rows(A[name][j]))
                    s = slot()
                    load(s, 0, 512, rows(A["rw_r_k_2"][j].rearrange("h d -> (h d)")))
                    load(s, 512, 1024, rows(A["rw_gn_g_2"][j]))
                    load(s, 1024, 1536, rows(A["rw_gn_b_2"][j]))
                    s = slot()
                    sp.dma_start(ring[0:64, s, 0:512], A["rw_w2_2"][j]).then_inc(slot_full[s], 16)
                    sp.dma_start(ring[64:128, s, 0:512], A["rw_a2_2"][j]).then_inc(slot_full[s], 16)
                    load(s, 512, 1024, A["rw_g2_2"][j])
                    load(s, 1024, 1536, A["sg_ws_2"][j].rearrange("g t s -> t g s"))
                    load(s, 1536, 1536 + SG_GROUPS, A["sg_b_2"][j])
                    s = slot()
                    load(s, 0, 512, rows(A["sg_ln_g_2"][j].rearrange("g d -> (g d)")))
                    load(s, 512, 1024, rows(A["sg_ln_b_2"][j].rearrange("g d -> (g d)")))
                    s = slot()
                    lo, hi = CONST_AT["rw_masks"][0], sum(CONST_AT["sg_mask"])
                    load(s, 0, hi - lo, A["consts"][:, lo:hi])
                    load_linear(A["ab_w_out_2"][j])
                else:
                    load_linear(A["mla_w_in_2"][j])
                    s = slot()
                    load(s, 0, 256, rows(A["mla_q_norm_2"][j]))
                    load(s, 256, 512, rows(A["mla_kv_norm_2"][j]))
                    lo = CONST_AT["rope2_cos"][0]
                    load(s, 512, 576, A["consts"][:, lo:lo + 64])
                    load_linear(A["mla_wq_b_2"][j])
                    load_linear(A["mla_wkv_b_2"][j])
                    load_linear(A["mla_w_out_2"][j])
                load_ln(A["ln1_g_2"][layer], A["ln1_b_2"][layer])
                if layer == 0:
                    load(slot(), 0, SLOT, A["mem_2"][0].rearrange("(t p) d -> p t d", p=P))
                load_linear(A["xa_wq_2"][layer])
                load_linear(A["xa_wkv_2"][layer])
                load_linear(A["xa_wo_2"][layer])
                load_ln(A["ln2_g_2"][layer], A["ln2_b_2"][layer])
                load_moe(layer)
                load_ln(A["ln3_g_2"][layer], A["ln3_b_2"][layer])

            sp.wait_ge(ln_done, NT * LAYER_NORMS)
            sp.dma_start(out[0].rearrange("(t p) d -> p t d", p=P), x[:, :, :]).then_inc(out_written, 16)
            sp.wait_ge(out_written, 16)

        @block.tensor
        def _(pe):
            full = [Tally(s) for s in slot_full]
            place = [0]
            t_proj = Tally(proj_done, ahead=2)
            t_tr = Tally(tr_done, ahead=2)
            t_ln = Tally(ln_done)
            t_rope = Tally(rope_done)
            t_logit_free = Tally(logit_free, ahead=2)
            t_p, t_pt = Tally(p_done), Tally(pt_done)
            t_pv = Tally(pv_done, ahead=2)
            t_dots = Tally(dots_done, ahead=2)
            t_h = Tally(h_done)
            t_gu_free = Tally(h_done, ahead=2)
            t_y = Tally(y_added)
            t_gm = Tally(gm_done, ahead=2)
            t_vec, t_act = Tally(vec_for_pe), Tally(act_for_pe)
            tr_items = [0]
            lin_items = [0]
            logit_items = [0]

            def slot(loads=1):
                s = place[0] % RING
                place[0] += 1
                pe.wait_ge(slot_full[s], full[s].next(16 * loads))
                return s

            def hold(loads):
                full[place[0] % RING].skip(16 * loads)
                place[0] += 1

            def mm(o, lhsT, rhs, start=True, stop=True):
                return nc.tensor.matmul(o, lhsT, rhs, start=start, stop=stop)

            def linear(srcT, K, N, drained=True, free_slots=0):
                kt = K // P
                per = min(4, kt)
                for c, (_, n) in enumerate(chunks_of(N)):
                    pair = 2 * (lin_items[0] % 2)
                    if drained:
                        lin_items[0] += 1
                        if t_proj.due():
                            pe.wait_ge(proj_done, t_proj.value())
                    for k0 in range(0, kt, per):
                        s = slot()
                        w = ring[:, s, 0:per * n].rearrange("p (k n) -> p k n", k=per)
                        for t in range(NT):
                            for k in range(per):
                                bank = pair + t if drained else 2 * t + c
                                last = mm(lin[:, bank, 0:n], srcT[:, k0 + k, t * P:(t + 1) * P], w[:, k, :],
                                          start=k0 + k == 0, stop=k0 + k == kt - 1)
                                if free_slots:
                                    last.then_inc(slots_used, 1)
                                    free_slots -= 1
                        last.then_inc(slots_used, 1)

            def transposes(pieces, free_slots=0):
                b = tr_items[0] % 2
                tr_items[0] += 1
                if t_tr.due():
                    pe.wait_ge(tr_done, t_tr.value())
                for j, src in enumerate(pieces):
                    ins = nc.tensor.transpose(trp[0:src.free_size(), b, j * P:(j + 1) * P], src, ident[:, :])
                    if j == len(pieces) - 1:
                        ins.then_inc(tr_full, 1)
                    elif free_slots:
                        ins.then_inc(slots_used, 1)
                        free_slots -= 1
                assert not free_slots

            def rows_to_columns(src, ready, free_slots=1):
                for t in range(NT):
                    pe.wait_ge(ln_done, ready.next())
                    for b in range(0, KD, 4):
                        last = t == NT - 1 and b == 0
                        transposes([src(t, b + j) for j in range(4)], free_slots if last else 0)

            def await_transposes():
                pe.wait_ge(tr_done, tr_items[0])

            def scores(parts):
                for o in parts:
                    b = logit_items[0] % 2
                    logit_items[0] += 1
                    if t_logit_free.due():
                        pe.wait_ge(logit_free, t_logit_free.value())
                    for t in range(NT):
                        for n, (qT, kT) in enumerate(o):
                            last = mm(sco[:, b, t * SEQ:(t + 1) * SEQ], qT[:, t * P:(t + 1) * P], kT,
                                      start=n == 0, stop=n == len(o) - 1)
                    last.then_inc(logit_full, 1)

            def attend(units):
                for parts, _ in units[:2]:
                    scores(parts)
                for h, (_, pieces) in enumerate(units):
                    pe.wait_ge(p_done, t_p.next())
                    for t in range(NT):
                        for k in range(NT):
                            last = nc.tensor.transpose(trp[:, h % 2, k * SEQ + t * P:k * SEQ + (t + 1) * P],
                                                       Pn[:, h % 2, t, k * P:(k + 1) * P], ident[:, :])
                    last.then_inc(pt_full, 1)
                    if h + 2 < len(units):
                        scores(units[h + 2][0])
                    pe.wait_ge(pt_done, t_pt.next())
                    for blk, lo, width, v in pieces:
                        if lo == 0:
                            if t_pv.due():
                                pe.wait_ge(pv_done, t_pv.value())
                        for k in range(NT):
                            last = mm(lin[lo:lo + width, blk % 2, 0:SEQ], v[k], PT[:, h % 2, k, :],
                                      start=k == 0, stop=k == NT - 1)
                        if lo + width == P:
                            last.then_inc(pv_full, 1)

            def first_block_units(kind, proj):
                def qk(qb, kb, odd):
                    r = slice(64 * odd, 64 * odd + 64)
                    return [(qkT[r, qb, :], qkT[r, kb, :])]

                def piece(j, v):
                    return (j // 2, 64 * (j % 2), 64, v)
                units = []
                if kind == 1:
                    for h in range(4):
                        parts = [qk((4 * g + h) // 2, 6 + (4 * g + h) // 2, h % 2) for g in range(3)]
                        units.append((parts, [piece(3 * h + j, [proj[:, k, 1536 + 64 * (3 * h + j):1600 + 64 * (3 * h + j)] for k in range(NT)])
                                              for j in range(3)]))
                else:
                    for h in range(HEADS):
                        units.append(([qk(h // 2, 6 + h // 2, h % 2)],
                                      [piece(h, [proj[:, k, 1536 + 64 * h:1600 + 64 * h] for k in range(NT)])]))
                mem_units = [([qk(17 + h // 2, 19 + h // 2, h % 2)],
                              [piece(12 + h, [mkv[:, k, 256 + 64 * h:320 + 64 * h] for k in range(NT)])])
                             for h in range(MEM_HEADS)]
                return units, mem_units

            def ffn():
                units = D_FF // (2 * P)
                y_of = lambda t, n: lin[:, 2 * t + n, :]

                def unit(u, start, stop):
                    gate, up = slot(), slot()
                    for f in range(2):
                        if t_gu_free.due():
                            pe.wait_ge(h_done, t_gu_free.value())
                        for s, lo in ((gate, 0), (up, SEQ)):
                            w = ring[:, s, :].rearrange("p (k n) -> p k n", k=KD)
                            for k in range(KD):
                                last = mm(sco[:, f, lo:lo + SEQ], w[:, k, f * P:(f + 1) * P], xT[:, k, :],
                                          start=k == 0, stop=k == KD - 1)
                            if f == 1:
                                last.then_inc(slots_used, 1)
                        if f == 0:
                            last.then_inc(gu_full, 1)
                    s = slot()
                    w = ring[:, s, :].rearrange("p (k n) -> p k n", k=2)
                    for f in range(2):
                        pe.wait_ge(h_done, t_h.next())
                        for t in range(NT):
                            for n in range(2):
                                last = mm(y_of(t, n), hT[:, u % 2, f, t * P:(t + 1) * P], w[:, f, n * 512:(n + 1) * 512],
                                          start=start and f == 0, stop=stop and f == 1)
                    last.then_inc(slots_used, 1)

                for u in range(units - units // 4 * 4):
                    unit(u, u == 0, False)
                per = {t_gu_free: 8, t_h: 8}
                for s in range(RING):
                    per[full[s]] = 16
                with rounds(pe, units // 4 - 1, per) as i:
                    for u in range(4):
                        unit(u + units % 4, False, False)
                place[0] += (units // 4 - 2) * RING
                for u in range(4):
                    unit(u + units % 4, False, u == 3)

            def linear_columns(srcT, chunks, free_slots=0):
                for _ in range(chunks):
                    pair = 2 * (lin_items[0] % 2)
                    lin_items[0] += 1
                    if t_proj.due():
                        pe.wait_ge(proj_done, t_proj.value())
                    w = []
                    for _ in range(2):
                        w.append(ring[:, slot(), :].rearrange("p (k n) -> p k n", k=4))
                    for blk in range(4):
                        o = lin[:, pair + blk // 2, blk % 2 * SEQ:(blk % 2 + 1) * SEQ]
                        for k in range(KD):
                            last = mm(o, w[k // 4][:, k % 4, blk * P:(blk + 1) * P], srcT[:, k, :], start=k == 0, stop=k == KD - 1)
                            if free_slots:
                                last.then_inc(slots_used, 1)
                                free_slots -= 1
                            if blk == 3 and k % 4 == 3:
                                last.then_inc(slots_used, 1)

            def mixer_ab():
                linear(xT, D, AB_IN)
                for n in RW_SLOTS[:3]:
                    hold(n)
                lora = slot(RW_SLOTS[3])
                hold(RW_SLOTS[4])
                const = slot(RW_SLOTS[5])
                strict, upto = ring[:, const, 0:P], ring[:, const, P:2 * P]
                chunk_of = ring[:, const, 10 * P:10 * P + 2]
                pe.wait_ge(vec_for_pe, t_vec.next())
                transposes([ring[:, lora, 1024 + g * P:1024 + (g + 1) * P] for g in range(SG_GROUPS)])
                await_transposes()
                pe.wait_ge(vec_for_pe, t_vec.next())
                for t in range(NT):
                    for g in range(SG_GROUPS):
                        last = mm(lin[:, t, g * P:(g + 1) * P], wmT[:, g, :], p_ab[:, t, 2304 + g * P:2304 + (g + 1) * P])
                last.then_inc(pe_for_vec, 1)
                for t in range(NT):
                    pe.wait_ge(act_for_pe, t_act.next())
                    transposes([p_ab[:, t, 1536:1664], p_ab[:, t, 1664:1792]])
                    await_transposes()
                    if t == 0:
                        pe.wait_ge(vec_for_pe, t_vec.next())
                    mm(lin[:, 0, :], loraT[0:64, 0, :], ring[0:64, lora, 0:512])
                    mm(lin[:, 1, :], loraT[64:128, 0, :], ring[64:128, lora, 0:512])
                    mm(lin[:, 2, :], loraT[:, 1, :], ring[:, lora, 512:1024]).then_inc(pe_for_vec, 1)
                    pe.wait_ge(vec_for_pe, t_vec.next())
                    mm(lin[:, 3, :], upto, rw_lw)
                    mm(lin[:, 2, :], strict, rw_lw)
                    for pair in range(4):
                        last = mm(sco[:, 0, 2 * pair:2 * pair + 2], rw_lw[:, pair * P:(pair + 1) * P], chunk_of)
                    last.then_inc(pe_for_act, 1)
                    pe.wait_ge(vec_for_pe, t_vec.next())
                    for pair in range(4):
                        transposes([v[:, pair * P:(pair + 1) * P] for v in (rw_kk, rw_r, rw_b, rw_k)])
                    await_transposes()
                    for h in range(RW_HEADS):
                        r = slice(64 * (h % 2), 64 * (h % 2) + 64)
                        if t_gm.due():
                            pe.wait_ge(gm_done, t_gm.value())
                        queries = rwT[r, h // 2, 0:2, :].rearrange("p a b -> p (a b)")
                        mm(sco[:, h % 2, 0:2 * P], rwT[r, h // 2, 2, :], queries)
                        mm(sco[:, h % 2, 2 * P:4 * P], rwT[r, h // 2, 3, :], queries).then_inc(gm_full, 1)
                    for level in range(6):
                        pe.wait_ge(vec_for_pe, t_vec.next())
                        for h in range(RW_HEADS):
                            last = mm(lin[:, h // 4, h % 4 * P:(h % 4 + 1) * P], rw_BT[:, h, :], rw_X[:, h, :])
                        last.then_inc(pe_for_act, 1)
                        pe.wait_ge(act_for_pe, t_act.next())
                        for h in range(RW_HEADS):
                            last = mm(lin[:, 2 + h // 4, h % 4 * P:(h % 4 + 1) * P], rw_T1[:, h, :], rw_XT[:, h, :])
                        if level < 5:
                            for h in range(RW_HEADS):
                                last = mm(sco[:, h // 4, h % 4 * P:(h % 4 + 1) * P], rw_XT[:, h, :], rw_T1[:, h, :])
                        last.then_inc(pe_for_vec, 1)
                    for half in range(2):
                        rs = slice(64 * half, 64 * half + 64)
                        pe.wait_ge(vec_for_pe, t_vec.next())
                        v = p_ab[rs, t, 1024:1536]
                        for h in range(RW_HEADS):
                            r, c = slice(64 * (h % 2), 64 * (h % 2) + 64), slice(64 * h, 64 * h + 64)
                            mm(lin[rs, h % 2, c], rwT[r, h // 2, 0, rs], rw_state[r, h // 2, :])
                        for h in range(RW_HEADS):
                            c = slice(64 * h, 64 * h + 64)
                            last = mm(lin[rs, 2, c], rw_G[rs, h, 2 * P + 64 * half:2 * P + 64 * half + 64], v[:, c])
                        last.then_inc(pe_for_vec, 1)
                        pe.wait_ge(vec_for_pe, t_vec.next())
                        for h in range(RW_HEADS):
                            c = slice(64 * h, 64 * h + 64)
                            last = mm(lin[rs, 3, c], rw_XT[rs, h, rs], rw_U[rs, c])
                        last.then_inc(pe_for_act, 1)
                        for h in range(RW_HEADS):
                            r, c = slice(64 * (h % 2), 64 * (h % 2) + 64), slice(64 * h, 64 * h + 64)
                            mm(sco[rs, h % 2, c], rwT[r, h // 2, 1, rs], rw_state[r, h // 2, :])
                        pe.wait_ge(act_for_pe, t_act.next())
                        for h in range(RW_HEADS):
                            c = slice(64 * h, 64 * h + 64)
                            mm(lin[rs, 2, c], rw_G[rs, h, P + 64 * half:P + 64 * half + 64], rw_SA[rs, c], stop=False)
                            mm(lin[rs, 2, c], rw_G[rs, h, 3 * P + 64 * half:3 * P + 64 * half + 64], v[:, c], start=False)
                        for h in range(RW_HEADS):
                            r, c = slice(64 * (h % 2), 64 * (h % 2) + 64), slice(64 * h, 64 * h + 64)
                            o = lin[r, 0, 64 * (h // 2):64 * (h // 2) + 64]
                            mm(o, rw_b[rs, c], rw_SA[rs, c], stop=False)
                            last = mm(o, rw_k[rs, c], v[:, c], start=False)
                        last.then_inc(pe_for_vec, 1)
                    pe.wait_ge(vec_for_pe, t_vec.next())
                column = lambda b: slice(b * P, (b + 1) * P) if b < 4 else slice(2304 + (b - 4) * P, 2304 + (b - 3) * P)
                pe.wait_ge(vec_for_pe, t_vec.next())
                for t in range(NT):
                    for b in range(0, KD, 4):
                        transposes([p_ab[:, t, column(b + j)] for j in range(4)], 3 if t == NT - 1 else 0)
                await_transposes()
                linear(mixT, D, D, drained=False)

            def mla():
                linear(xT, D, MLA_IN)
                hold(3)
                pe.wait_ge(vec_for_pe, t_vec.next())
                for b0 in range(0, 4, 2):
                    transposes([mla_p[:, t, (b0 + b) * P:(b0 + b + 1) * P] for b in range(2) for t in range(NT)], 1 if b0 == 0 else 0)
                await_transposes()
                linear(latentT[:, 0:2, :], 256, MLA_HEADS * 96)
                linear(latentT[:, 2:4, :], 256, MLA_HEADS * P)
                pe.wait_ge(vec_for_pe, t_vec.next())
                q_src = lambda t, b: mla_qn[:, t, 2 * b:2 * b + 2, :].rearrange("p h d -> p (h d)")
                k_src = lambda t, b: mla_kn[t][:, 2 * b:2 * b + 2, :].rearrange("p h d -> p (h d)")
                for src in (q_src, k_src):
                    for b0 in range(0, 8, 2):
                        transposes([src(t, b0 + b) for b in range(2) for t in range(NT)])
                transposes([mla_kpe[:, t, :, :].rearrange("p a b -> p (a b)") for t in range(NT)])
                for b0 in range(0, 8, 2):
                    transposes([mla_qpe[:, t, 2 * (b0 + b):2 * (b0 + b) + 2, :, :].rearrange("p h a b -> p (h a b)")
                                for b in range(2) for t in range(NT)])
                await_transposes()
                units = []
                for h in range(MLA_HEADS):
                    r, b = slice(64 * (h % 2), 64 * (h % 2) + 64), h // 2
                    qpe = mlaT[r, 17 + b, :] if b < 4 else mlaT_more[r, b - 4, :]
                    units.append(([[(mlaT[r, b, :], mlaT[r, 8 + b, :]), (qpe, mlaT[r, 16, :])]],
                                  [(b, 64 * (h % 2), 64, [mla_kv[:, k, h, 64:128] for k in range(NT)])]))
                attend(units)
                pe.wait_ge(pv_done, t_pv.n + 2)
                linear(mixT, D, D, drained=False)

            def memory_attention(free_slots):
                linear_columns(xT, 2, free_slots)
                linear_columns(memT, 2)
                linear(memT, D, D)
                pe.wait_ge(proj_done, t_proj.n + 2)
                attend([([[(xa_qT[:, 2 * h + b, :], xa_kT[:, 2 * h + b, :]) for b in range(2)]],
                         [(2 * h + b, 0, P, [xa_v[:, k, 256 * h + P * b:256 * h + P * b + P] for k in range(NT)]) for b in range(2)])
                        for h in range(XA_HEADS)])
                pe.wait_ge(pv_done, t_pv.n + 2)
                linear(mixT, D, D, drained=False)

            def moe():
                s = slot(5)
                w = ring[:, s, 0:KD * 36].rearrange("p (k n) -> p k n", k=KD)
                pe.wait_ge(vec_for_pe, t_vec.next())
                for t in range(NT):
                    o = sco[:, 0, t * 64:t * 64 + 36]
                    for k in range(KD):
                        mm(o, xT[:, k, t * P:(t + 1) * P], w[:, k, :], start=k == 0, stop=False)
                    last = mm(o, ring[:, s, 672:672 + P], ring[:, s, 512:548], start=False)
                last.then_inc(slots_used, 1)
                pe.wait_ge(vec_for_pe, t_vec.next())

                def expert(j):
                    gate = [slot(), slot()]
                    up = [slot(), slot()]
                    for f in range(4):
                        if t_gu_free.due():
                            pe.wait_ge(h_done, t_gu_free.value())
                        for slots, lo in ((gate, 0), (up, SEQ)):
                            for k in range(KD):
                                wk = ring[:, slots[k // 4], :].rearrange("p (k n) -> p k n", k=4)
                                last = mm(sco[:, f % 2, lo:lo + SEQ], wk[:, k % 4, f * P:(f + 1) * P], xT[:, k, :],
                                          start=k == 0, stop=k == KD - 1)
                                if f == 3 and k % 4 == 3:
                                    last.then_inc(slots_used, 1)
                        if f < 3:
                            last.then_inc(gu_full, 1)
                    pe.wait_ge(y_added, t_y.next())
                    for half in range(2):
                        wd = ring[:, slot(), :].rearrange("p (k n) -> p k n", k=2)
                        for f in range(2):
                            pe.wait_ge(h_done, t_h.next())
                            for t in range(NT):
                                for n in range(2):
                                    last = mm(lin[:, 2 * t + n, :], hT[:, j, 2 * half + f, t * P:(t + 1) * P], wd[:, f, n * 512:(n + 1) * 512],
                                              start=half + f == 0, stop=half + f == 2)
                        last.then_inc(slots_used, 1)

                per = {t_gu_free: 8, t_h: 8, t_y: 2}
                for s in range(RING):
                    per[full[s]] = 16
                with rounds(pe, EXPERTS // 2, per):
                    for j in range(2):
                        expert(j)
                place[0] += (EXPERTS // 2 - 1) * RING
                t_y.skip(1)

            pe.wait_ge(input_loaded, 16 * 6)
            hold(2)
            rows_to_columns(lambda t, b: memrows[:, t, b * P:(b + 1) * P], t_ln)
            for t in range(NT):
                for b in range(0, KD, 4):
                    transposes([x[:, t, (b + j) * P:(b + j + 1) * P] for j in range(4)])
            for layer in range(FIRST_LAYERS):
                kind = kind_of(layer)
                proj = projA if kind == 0 else projBC
                width = WIDTH_A if kind == 0 else WIDTH_BC
                await_transposes()
                linear(xT, D, width)
                linear(memT, D, 512)
                pe.wait_ge(proj_done, t_proj.n + 2)
                qm = width - MEM_HEADS * DH
                for t in range(1):
                    transposes([proj[:, t2, qm + b * P:qm + (b + 1) * P] for b in range(2) for t2 in range(NT)])
                    transposes([mkv[:, t2, b * P:(b + 1) * P] for b in range(2) for t2 in range(NT)])
                if kind < 2:
                    hold(2 if kind == 0 else 1)
                pe.wait_ge(rope_done, t_rope.next())
                for b0 in range(0, 12, 2):
                    transposes([proj[:, t, (b0 + b) * P:(b0 + b + 1) * P] for b in range(2) for t in range(NT)],
                               1 if b0 == 0 and kind == 0 else 0)
                if kind == 0:
                    for b0 in range(0, 4, 2):
                        transposes([proj[:, t, 2304 + (b0 + b) * P:2304 + (b0 + b + 1) * P] for b in range(2) for t in range(NT)])
                    transposes([ki2[:, t, :, :].rearrange("p a d -> p (a d)") for t in range(NT)])
                await_transposes()
                if kind == 0:
                    for t in range(NT):
                        for h in range(0, IDX_HEADS, 4):
                            for step in range(2):
                                for o in range(2):
                                    if step == 0:
                                        if t_dots.due():
                                            pe.wait_ge(dots_done, t_dots.value())
                                    r = slice(64 * o, 64 * o + 64)
                                    last = mm(sco[:, o, step * SEQ:(step + 1) * SEQ], qkT[r, 12 + h // 2 + step, t * P:(t + 1) * P], qkT[r, 16, :])
                                    if step == 1:
                                        last.then_inc(dots_full, 1)
                    pe.wait_ge(dots_done, t_dots.n + 2)
                units, mem_units = first_block_units(kind, proj)
                attend(mem_units)
                attend(units)
                pe.wait_ge(pv_done, t_pv.n + 2)
                linear(mixT, D, D, drained=False, free_slots=1 if kind == 1 else 0)
                hold(2)
                rows_to_columns(lambda t, b: x[:, t, b * P:(b + 1) * P], t_ln)
                await_transposes()
                ffn()
                hold(2)
                rows_to_columns(lambda t, b: x[:, t, b * P:(b + 1) * P], t_ln)
            for layer in range(SECOND_LAYERS):
                await_transposes()
                if layer % 2 == 0:
                    mixer_ab()
                else:
                    mla()
                hold(2)
                rows_to_columns(lambda t, b: x[:, t, b * P:(b + 1) * P], t_ln)
                if layer == 0:
                    s = slot()
                    for t in range(NT):
                        for b in range(0, KD, 4):
                            transposes([ring[:, s, t * D + (b + j) * P:t * D + (b + j + 1) * P] for j in range(4)])
                await_transposes()
                memory_attention(1 if layer == 0 else 0)
                hold(2)
                rows_to_columns(lambda t, b: x[:, t, b * P:(b + 1) * P], t_ln)
                await_transposes()
                moe()
                hold(2)
                if layer + 1 < SECOND_LAYERS:
                    rows_to_columns(lambda t, b: x[:, t, b * P:(b + 1) * P], t_ln)

        @block.scalar
        def _(act):
            used = Tally(slots_used)
            t_tr, t_smax, t_pt, t_pv = Tally(tr_full), Tally(smax_done), Tally(pt_full), Tally(pv_full)
            t_dots, t_added = Tally(dots_full), Tally(score_added, ahead=2)
            t_gu, t_h = Tally(gu_full), Tally(h_done, ahead=2)
            t_vec, t_pe = Tally(vec_for_act), Tally(pe_for_act)
            tr_items = [0]
            lin_items = [0]
            proj_items = [0]

            def evacuate_linear(K, N, dst):
                for lo, n in chunks_of(N):
                    act.wait_ge(slots_used, used.next(max(1, K // 512)))
                    pair = 2 * (lin_items[0] % 2)
                    lin_items[0] += 1
                    proj_items[0] += 1
                    nc.scalar.activation(dst[:, :, lo:lo + n], lin[:, pair:pair + 2, 0:n],
                                         ACT.Copy).then_inc(proj_done, 1)

            def evacuate_transposes(dst, rows=P):
                b = tr_items[0] % 2
                tr_items[0] += 1
                act.wait_ge(tr_full, t_tr.next())
                shape = dst.shape
                n = shape[1] * shape[2]
                nc.scalar.activation(dst, trp[0:rows, b, 0:n].rearrange("p (a b) -> p a b", a=shape[1]),
                                     ACT.Copy).then_inc(tr_done, 1)

            def columns(dstT):
                for t in range(NT):
                    for b in range(0, KD, 4):
                        evacuate_transposes(dstT[:, b:b + 4, t * P:(t + 1) * P])

            def attend(n_units, groups, blocks_after, first_block):
                S = S1 if groups == 1 else S3

                def exps(h):
                    act.wait_ge(smax_done, t_smax.next())
                    for t in range(NT):
                        s = S[:, h % 2, t, :, :].rearrange("p g k -> p (g k)")
                        last = nc.scalar.activation(s, s, ACT.Exp, bias=negmax[:, h % 2, t:t + 1],
                                                    accum_out=rowsum[:, h % 2, t:t + 1])
                    last.then_inc(exp_done, 1)
                exps(0)
                blk = first_block
                for h in range(n_units):
                    if h + 1 < n_units:
                        exps(h + 1)
                    act.wait_ge(pt_full, t_pt.next())
                    nc.scalar.activation(PT[:, h % 2, :, :].rearrange("p k q -> p (k q)"), trp[:, h % 2, :],
                                         ACT.Copy).then_inc(pt_done, 1)
                    while blk < blocks_after(h):
                        act.wait_ge(pv_full, t_pv.next())
                        nc.scalar.activation(mixT[:, blk, :], lin[:, blk % 2, 0:SEQ], ACT.Copy).then_inc(pv_done, 1)
                        blk += 1

            def ffn():
                units = D_FF // (2 * P)

                def unit():
                    for f in range(2):
                        if f == 0:
                            act.wait_ge(gu_full, t_gu.next())
                        else:
                            act.wait_ge(slots_used, used.next(2))
                        if t_h.due():
                            act.wait_ge(h_done, t_h.value())
                        nc.scalar.activation(silu_g[:, f, :], sco[:, f, 0:SEQ], ACT.Silu).then_inc(silu_done, 1)
                    used.skip(1)
                unit()
                with rounds(act, units - 1, {t_gu: 1, used: 3, t_h: 2}):
                    unit()

            def mixer_ab():
                evacuate_linear(D, AB_IN, p_ab)
                used.skip(len(RW_SLOTS))
                act.wait_ge(proj_done, proj_items[0])
                act.dma_start(shifted[1:P, :, :], p_ab[0:P - 1, :, 0:RW_SHIFT]).then_inc(shift_loaded, 16)
                act.dma_start(shifted[0:1, 1, :], p_ab[P - 1:P, 0, 0:RW_SHIFT]).then_inc(shift_loaded, 16)
                gated = p_ab[:, :, RW_SHIFT:AB_IN]
                nc.scalar.activation(gated, gated, ACT.Gelu_apprx_tanh).then_inc(act_for_vec, 1)
                evacuate_transposes(wmT)
                for t in range(NT):
                    if t == 0:
                        act.wait_ge(vec_for_act, t_vec.next())
                    nc.scalar.activation(p_ab[:, t, 1536:1600], p_ab[:, t, 1536:1600], ACT.Tanh)
                    nc.scalar.activation(p_ab[:, t, 1664:1792], p_ab[:, t, 1664:1792], ACT.Sigmoid).then_inc(act_for_pe, 1)
                    evacuate_transposes(loraT)
                    act.wait_ge(vec_for_act, t_vec.next())
                    nc.scalar.activation(rw_tmp, rw_tmp, ACT.Sigmoid)
                    nc.scalar.activation(rw_a, rw_a, ACT.Sigmoid).then_inc(act_for_vec, 1)
                    act.wait_ge(pe_for_act, t_pe.next())
                    nc.scalar.activation(rw_r, lin[:, 3, :], ACT.Exp)
                    nc.scalar.activation(rw_pinv, lin[:, 3, :], ACT.Exp, scale=-1.0)
                    nc.scalar.activation(rw_pexc, lin[:, 2, :], ACT.Exp)
                    nc.scalar.activation(rw_decay.rearrange("p a b -> p (a b)"), sco[:, 0, 0:8], ACT.Exp).then_inc(act_for_vec, 1)
                    for pair in range(4):
                        evacuate_transposes(rwT[:, pair, :, :])
                    for _ in range(6):
                        act.wait_ge(pe_for_act, t_pe.next())
                        nc.scalar.activation(rw_T1.rearrange("p h k -> p (h k)"), lin[:, 0:2, :].rearrange("p a b -> p (a b)"),
                                             ACT.Copy).then_inc(act_for_pe, 1)
                    for half in range(2):
                        rs = slice(64 * half, 64 * half + 64)
                        act.wait_ge(pe_for_act, t_pe.next())
                        nc.scalar.activation(rw_SA[rs, :], lin[rs, 3, :], ACT.Copy, scale=-1.0).then_inc(act_for_pe, 1)
                columns(mixT)

            def mla():
                evacuate_linear(D, MLA_IN, mla_p)
                used.skip(1)
                for b in range(0, 4, 2):
                    evacuate_transposes(latentT[:, b:b + 2, :])
                evacuate_linear(256, MLA_HEADS * 96, mla_q.rearrange("p t h d -> p t (h d)"))
                evacuate_linear(256, MLA_HEADS * P, mla_kv.rearrange("p t h d -> p t (h d)"))
                for b in range(0, 16, 2):
                    evacuate_transposes(mlaT[:, b:b + 2, :])
                evacuate_transposes(mlaT[:, 16:17, :])
                for b in range(0, 4, 2):
                    evacuate_transposes(mlaT[:, 17 + b:19 + b, :])
                for b in range(0, 4, 2):
                    evacuate_transposes(mlaT_more[:, b:b + 2, :])
                attend(MLA_HEADS, 1, lambda h: (h + 1) // 2, 0)

            def memory_attention():
                for dst in (xa_qT, xa_kT):
                    for c in range(2):
                        act.wait_ge(slots_used, used.next(2))
                        pair = 2 * (lin_items[0] % 2)
                        lin_items[0] += 1
                        proj_items[0] += 1
                        nc.scalar.activation(dst[:, 4 * c:4 * c + 4, :].rearrange("p a b -> p (a b)"),
                                             lin[:, pair:pair + 2, :].rearrange("p a b -> p (a b)"), ACT.Copy).then_inc(proj_done, 1)
                evacuate_linear(D, D, xa_v)
                attend(XA_HEADS, 1, lambda h: 2 * (h + 1), 0)

            def moe():
                used.skip(1)
                act.wait_ge(vec_for_act, t_vec.next())
                for t in range(NT):
                    nc.scalar.activation(hot[:, t, 0:GROUPS], logits36[:, t, 0:GROUPS], ACT.Exp, bias=router[:, t, 8:9],
                                         accum_out=router[:, t, 9:10])
                    last = nc.scalar.activation(router[:, t, 11:12], router[:, t, 10:11], ACT.Exp)
                last.then_inc(act_for_vec, 1)
                with rounds(act, EXPERTS // 2, {t_gu: 6, used: RING, t_h: 8}):
                    for j in range(2):
                        for f in range(4):
                            if f < 3:
                                act.wait_ge(gu_full, t_gu.next())
                            else:
                                act.wait_ge(slots_used, used.next(4))
                            if t_h.due():
                                act.wait_ge(h_done, t_h.value())
                            nc.scalar.activation(silu_g[:, f % 2, :], sco[:, f % 2, 0:SEQ], ACT.Silu).then_inc(silu_done, 1)
                        used.skip(2)

            act.wait_ge(input_loaded, 16 * 6)
            used.skip(1)
            columns(memT)
            columns(xT)
            act.wait_ge(vec_for_act, t_vec.next())
            nc.scalar.activation(small[:, 0:32], small[:, 96:128], ACT.Sin).then_inc(act_for_vec, 1)
            for layer in range(FIRST_LAYERS):
                kind = kind_of(layer)
                proj = projA if kind == 0 else projBC
                evacuate_linear(D, WIDTH_A if kind == 0 else WIDTH_BC, proj)
                evacuate_linear(D, 512, mkv)
                evacuate_transposes(qkT[:, 17:19, :])
                evacuate_transposes(qkT[:, 19:21, :])
                for b in range(0, 16 if kind == 0 else 12, 2):
                    evacuate_transposes(qkT[:, b:b + 2, :])
                if kind == 0:
                    used.skip(1)
                    evacuate_transposes(qkT[:, 16:17, :])
                    for n in range(NT * IDX_HEADS // 2):
                        act.wait_ge(dots_full, t_dots.next())
                        if t_added.due():
                            act.wait_ge(score_added, t_added.value())
                        nc.scalar.activation(idx_relu[:, n % 2, :, :].rearrange("p o k -> p (o k)"), sco[:, n % 2, :],
                                             ACT.Relu).then_inc(dots_done, 1)
                attend(MEM_HEADS, 1, lambda h: 6 + (h + 1) // 2, 6)
                if kind == 1:
                    attend(4, 3, lambda h: 3 * (h + 1) // 2, 0)
                else:
                    attend(HEADS, 1, lambda h: (h + 1) // 2, 0)
                if kind == 1:
                    used.skip(1)
                used.skip(4 + 1)
                columns(xT)
                ffn()
                used.skip(1)
                columns(xT)
            for layer in range(SECOND_LAYERS):
                if layer % 2 == 0:
                    mixer_ab()
                else:
                    mla()
                used.skip(4 + 1)
                columns(xT)
                if layer == 0:
                    used.skip(1)
                    columns(memT)
                memory_attention()
                used.skip(4 + 1)
                columns(xT)
                moe()
                used.skip(1)
                if layer + 1 < SECOND_LAYERS:
                    columns(xT)

        @block.gpsimd
        def _(pool):
            asked = Tally(root_asked)
            nc.gpsimd.memset(root_in, 1.0)
            nc.gpsimd.memset(root_power, -0.5).then_inc(pool_step, 1)
            pool.wait_ge(pool_step, 1)
            with rounds(pool, ROOTS // 2, {asked: 2}):
                for b in range(2):
                    pool.wait_ge(root_asked, asked.next())
                    nc.gpsimd.tensor_tensor(root_out[:, b, :], root_in[:, b, :], root_power, ALU.pow).then_inc(root_done, 1)

        @block.vector
        def _(dve):
            used = Tally(slots_used)
            t_step = Tally(dve_step)
            t_proj = Tally(proj_done)
            t_act, t_pe = Tally(act_for_vec), Tally(pe_for_vec)
            t_logit, t_logit_free = Tally(logit_full), Tally(logit_free)
            t_exp, t_pt = Tally(exp_done), Tally(pt_full, ahead=2)
            t_dots, t_added = Tally(dots_done), Tally(score_added)
            t_gu, t_silu, t_h = Tally(gu_full), Tally(silu_done), Tally(h_done)
            t_root = Tally(root_done)
            logit_items = [0]
            t_gm, t_gm_done = Tally(gm_full), Tally(gm_done)
            t_y = Tally(y_added)
            root_items = [0]
            shifts = [0]
            V = nc.vector


            ring_fill = [0] * RING
            place = [0]

            def passed(n, loads=1):
                for _ in range(n):
                    ring_fill[place[0] % RING] += 16 * loads
                    place[0] += 1
                used.skip(n)

            def own_slot(loads):
                s = place[0] % RING
                passed(1, loads)
                dve.wait_ge(slot_full[s], ring_fill[s])
                return s

            def rsqrt(v, op, c):
                b, n = root_items[0] % 2, v.shape[1]
                root_items[0] += 1
                V.tensor_scalar(root_in[:, b, 0:n], v, c, None, op).then_inc(root_asked, 1)
                dve.wait_ge(root_done, t_root.next())
                return root_out[:, b, 0:n]

            def normalise(rows, t, s):
                for h in range(2):
                    last = V.bn_stats(bn[:, t, h * 6:h * 6 + 6], rows[:, t, h * 512:(h + 1) * 512])
                last.then_inc(dve_step, 1)
                dve.wait_ge(dve_step, t_step.next())
                V.bn_aggr(mean_var[:, t, :], bn[:, t, :]).then_inc(dve_step, 1)
                dve.wait_ge(dve_step, t_step.next())
                rstd = rsqrt(mean_var[:, t, 1:2], ALU.add, LN_EPS)
                V.scalar_tensor_tensor(rows[:, t, :], rows[:, t, :], mean_var[:, t, 0:1], ring[:, s, 0:D], ALU.subtract, ALU.mult).then_inc(dve_step, 1)
                dve.wait_ge(dve_step, t_step.next())
                V.scalar_tensor_tensor(rows[:, t, :], rows[:, t, :], rstd, ring[:, s, D:2 * D],
                                       ALU.mult, ALU.add).then_inc(ln_done, 1)

            def add_and_normalise(alpha):
                s = own_slot(2)
                for t in range(NT):
                    V.scalar_tensor_tensor(x[:, t, :], x[:, t, :], alpha, lin[:, 2 * t:2 * t + 2, :].rearrange("p a b -> p (a b)"),
                                           ALU.mult, ALU.add).then_inc(dve_step, 1)
                    dve.wait_ge(dve_step, t_step.next())
                    normalise(x, t, s)

            def rotate(heads, cos, sin, half, scratch=rope_tmp):
                n = heads.shape[1]
                a, b = heads[:, :, 0:half], heads[:, :, half:2 * half]
                c = cos.unsqueeze(1).to_broadcast([P, n, half])
                s = sin.unsqueeze(1).to_broadcast([P, n, half])
                tmp = [scratch[:, j, 0:n * half].rearrange("p (n f) -> p n f", n=n) for j in range(4)]
                V.tensor_tensor(tmp[0], a, c, ALU.mult)
                V.tensor_tensor(tmp[1], b, s, ALU.mult)
                V.tensor_tensor(tmp[2], b, c, ALU.mult)
                V.tensor_tensor(tmp[3], a, s, ALU.mult).then_inc(dve_step, 1)
                dve.wait_ge(dve_step, t_step.next())
                V.tensor_tensor(a, tmp[0], tmp[1], ALU.subtract)
                return V.tensor_tensor(b, tmp[2], tmp[3], ALU.add)

            def attend(n_units, groups, mask_of, scale):
                S = S1 if groups == 1 else S3

                def maxima(h):
                    for g in range(groups):
                        bank = logit_items[0] % 2
                        logit_items[0] += 1
                        dve.wait_ge(logit_full, t_logit.next())
                        src = sco[:, bank, :].rearrange("p (t k) -> p t k", t=NT)
                        mask = mask_of(g)
                        if mask is None:
                            ins = V.tensor_scalar(S[:, h % 2, :, g, :], src, scale, None, ALU.mult)
                        else:
                            ins = V.scalar_tensor_tensor(S[:, h % 2, :, g, :], src, scale, mask, ALU.mult, ALU.add)
                        ins.then_inc(logit_free, 1)
                        dve.wait_ge(logit_free, t_logit_free.next())
                    V.tensor_reduce(negmax[:, h % 2, :], S[:, h % 2, :, :, :].rearrange("p t g k -> p t (g k)"), AX.X, ALU.max,
                                    negate=True).then_inc(smax_done, 1)
                maxima(0)
                for h in range(n_units):
                    if h + 1 < n_units:
                        maxima(h + 1)
                    dve.wait_ge(exp_done, t_exp.next())
                    V.reciprocal(rinv[:, h % 2, :], rowsum[:, h % 2, :]).then_inc(dve_step, 1)
                    dve.wait_ge(dve_step, t_step.next())
                    for g in range(1, groups):
                        V.tensor_tensor(S[:, h % 2, :, 0, :], S[:, h % 2, :, 0, :], S[:, h % 2, :, g, :], ALU.add).then_inc(dve_step, 1)
                        dve.wait_ge(dve_step, t_step.next())
                    if t_pt.due():
                        dve.wait_ge(pt_full, t_pt.value())
                    for t in range(NT):
                        last = V.tensor_scalar(Pn[:, h % 2, t, :], S[:, h % 2, t, 0, :], rinv[:, h % 2, t:t + 1], None, ALU.mult)
                    last.then_inc(p_done, 1)

            def select_keys(proj):
                n = 0
                for t in range(NT):
                    for i, h in enumerate((0, 2, 1, 3, 4, 6, 5, 7)):
                        if i % 2 == 0:
                            dve.wait_ge(dots_done, t_dots.next())
                        prev = causal[:, t, :] if i == 0 else idx_score[:, t, :]
                        ins = V.scalar_tensor_tensor(idx_score[:, t, :], idx_relu[:, n % 2, i % 2, :], proj[:, t, 2816 + h:2817 + h], prev,
                                                     ALU.mult, ALU.add)
                        if i % 2:
                            ins.then_inc(score_added, 1)
                            dve.wait_ge(score_added, t_added.next())
                            n += 1
                        else:
                            ins.then_inc(dve_step, 1)
                            dve.wait_ge(dve_step, t_step.next())
                for t in range(NT):
                    for _ in range(TOPK // 8):
                        V.max(top_score, idx_score[:, t, :]).then_inc(dve_step, 1)
                        dve.wait_ge(dve_step, t_step.next())
                        V.match_replace(idx_score[:, t, :], top_score, idx_score[:, t, :], TAKEN).then_inc(dve_step, 1)
                        dve.wait_ge(dve_step, t_step.next())
                    V.tensor_scalar(dsa_mask[:, t, :], idx_score[:, t, :], TAKEN, 1.0, ALU.is_equal, ALU.subtract).then_inc(dve_step, 1)
                    dve.wait_ge(dve_step, t_step.next())
                    V.scalar_tensor_tensor(dsa_mask[:, t, :], dsa_mask[:, t, :], -MASKED, causal[:, t, :], ALU.mult, ALU.add).then_inc(dve_step, 1)
                    dve.wait_ge(dve_step, t_step.next())

            def ffn():
                units = D_FF // (2 * P)

                def unit(u):
                    for f in range(2):
                        dve.wait_ge(silu_done, t_silu.next())
                        V.tensor_tensor(hT[:, u % 2, f, :], silu_g[:, f, :], sco[:, f, SEQ:2 * SEQ], ALU.mult).then_inc(h_done, 1)
                per = {t_silu: 4}
                unit(0)
                with rounds(dve, (units - 1) // 2, per):
                    unit(1)
                    unit(0)

            def spread(v, n):
                return v.unsqueeze(2).to_broadcast([P, v.shape[1], n])

            def centre_and_scale(v, sq, n, eps):
                m = v.shape[1]
                s = stat8[:, 0:m]
                V.tensor_reduce(s, v, AX.X, ALU.add).then_inc(dve_step, 1)
                dve.wait_ge(dve_step, t_step.next())
                V.tensor_scalar(s, s, 1.0 / n, None, ALU.mult).then_inc(dve_step, 1)
                dve.wait_ge(dve_step, t_step.next())
                V.tensor_tensor(v, v, spread(s, n), ALU.subtract).then_inc(dve_step, 1)
                dve.wait_ge(dve_step, t_step.next())
                V.tensor_tensor(sq, v, v, ALU.mult).then_inc(dve_step, 1)
                dve.wait_ge(dve_step, t_step.next())
                V.tensor_reduce(s, sq, AX.X, ALU.add).then_inc(dve_step, 1)
                dve.wait_ge(dve_step, t_step.next())
                V.tensor_scalar(s, s, 1.0 / n, None, ALU.mult).then_inc(dve_step, 1)
                dve.wait_ge(dve_step, t_step.next())
                V.tensor_tensor(v, v, spread(rsqrt(s, ALU.add, eps), n), ALU.mult).then_inc(dve_step, 1)
                dve.wait_ge(dve_step, t_step.next())

            def mixer_ab():
                n_chunks = len(chunks_of(AB_IN))
                V.memset(shifted[0:1, 0, :], 0.0).then_inc(dve_step, 1)
                dve.wait_ge(dve_step, t_step.next())
                passed(2 * n_chunks)
                mu, p0, p1, lora, sg, const = [own_slot(n) for n in RW_SLOTS]
                w0, a0, k_k, k_a = [ring[:, p0, 512 * n:512 * n + 512] for n in range(4)]
                r_k, gn_g, gn_b = [ring[:, p1, 512 * n:512 * n + 512] for n in range(3)]
                groups = lambda v: v.rearrange("p (g d) -> p g d", g=SG_GROUPS)
                heads = lambda v: v.rearrange("p (h d) -> p h d", h=RW_HEADS)
                ws = groups(ring[:, lora, 1024:1536])
                V.tensor_tensor(ws, ws, ring[:, const, 10 * P + 2:11 * P + 2].unsqueeze(1).to_broadcast([P, SG_GROUPS, P]),
                                ALU.mult).then_inc(vec_for_pe, 1)
                dve.wait_ge(proj_done, t_proj.next(n_chunks))
                dve.wait_ge(shift_loaded, 32 * (1 + shifts[0]))
                shifts[0] += 1
                for t in range(NT):
                    ps = p_ab[:, t, 0:RW_SHIFT]
                    V.tensor_tensor(shifted[:, t, :], shifted[:, t, :], ps, ALU.subtract).then_inc(dve_step, 1)
                    dve.wait_ge(dve_step, t_step.next())
                    V.tensor_tensor(shifted[:, t, :], shifted[:, t, :], ring[:, mu, 0:RW_SHIFT], ALU.mult).then_inc(dve_step, 1)
                    dve.wait_ge(dve_step, t_step.next())
                    ins = V.tensor_tensor(ps, ps, shifted[:, t, :], ALU.add)
                    if t == NT - 1:
                        ins.then_inc(vec_for_act, 1)
                    else:
                        ins.then_inc(dve_step, 1)
                        dve.wait_ge(dve_step, t_step.next())
                dve.wait_ge(act_for_vec, t_act.next())
                for t in range(NT):
                    z = p_ab[:, t, 2304:2816]
                    centre_and_scale(groups(z), groups(rw_y), P, LN_EPS)
                    V.tensor_tensor(z, z, ring[:, sg, 0:512], ALU.mult).then_inc(dve_step, 1)
                    dve.wait_ge(dve_step, t_step.next())
                    ins = V.tensor_tensor(z, z, ring[:, sg, 512:1024], ALU.add)
                    if t == NT - 1:
                        ins.then_inc(vec_for_pe, 1)
                    else:
                        ins.then_inc(dve_step, 1)
                        dve.wait_ge(dve_step, t_step.next())
                dve.wait_ge(pe_for_vec, t_pe.next())
                for t in range(NT):
                    for g in range(SG_GROUPS):
                        c = slice(P * g, P * g + P)
                        last = V.scalar_tensor_tensor(groups(p_ab[:, t, 2304:2816])[:, g, :], lin[:, t, c], ring[:, lora, 1536 + g:1537 + g],
                                                      p_ab[:, t, 1792 + P * g:1792 + P * g + P], ALU.add, ALU.mult)
                last.then_inc(vec_for_pe, 1)
                V.memset(rw_state, 0.0).then_inc(dve_step, 1)
                dve.wait_ge(dve_step, t_step.next())
                for t in range(NT):
                    r, k, v = [p_ab[:, t, 512 * n:512 * n + 512] for n in range(3)]
                    V.tensor_tensor(rw_kk, k, k_k, ALU.mult).then_inc(dve_step, 1)
                    dve.wait_ge(dve_step, t_step.next())
                    V.tensor_tensor(rw_pexc, rw_kk, rw_kk, ALU.mult).then_inc(dve_step, 1)
                    dve.wait_ge(dve_step, t_step.next())
                    V.tensor_reduce(stat8, heads(rw_pexc), AX.X, ALU.add).then_inc(dve_step, 1)
                    dve.wait_ge(dve_step, t_step.next())
                    V.tensor_tensor(heads(rw_kk), heads(rw_kk), spread(rsqrt(stat8, ALU.max, 1e-24), 64), ALU.mult).then_inc(dve_step, 1)
                    dve.wait_ge(dve_step, t_step.next())
                    dve.wait_ge(pe_for_vec, t_pe.next())
                    V.tensor_tensor(rw_tmp, lin[:, 0, :], w0, ALU.add)
                    V.tensor_copy(rw_g, lin[:, 2, :])
                    V.tensor_tensor(rw_a, lin[:, 1, :], a0, ALU.add).then_inc(vec_for_act, 1)
                    dve.wait_ge(act_for_vec, t_act.next())
                    V.tensor_scalar(rw_lw, rw_tmp, -math.exp(-0.5), None, ALU.mult).then_inc(vec_for_pe, 1)
                    V.tensor_tensor(rw_b, rw_kk, rw_a, ALU.mult)
                    V.scalar_tensor_tensor(rw_k, rw_a, 1.0, k_a, ALU.subtract, ALU.mult).then_inc(dve_step, 1)
                    dve.wait_ge(dve_step, t_step.next())
                    V.scalar_tensor_tensor(k, rw_k, 1.0, k, ALU.add, ALU.mult).then_inc(dve_step, 1)
                    dve.wait_ge(dve_step, t_step.next())
                    dve.wait_ge(act_for_vec, t_act.next())
                    V.tensor_tensor(rw_kk, rw_kk, rw_pexc, ALU.mult)
                    V.tensor_tensor(rw_r, rw_r, r, ALU.mult)
                    V.tensor_tensor(rw_b, rw_b, rw_pinv, ALU.mult)
                    V.tensor_tensor(rw_k, k, rw_pinv, ALU.mult).then_inc(vec_for_pe, 1)
                    eye = ident[:, :].unsqueeze(1).to_broadcast([P, RW_HEADS, P])
                    V.tensor_copy(rw_X, eye)
                    V.tensor_copy(rw_XT, eye)
                    for h in range(RW_HEADS):
                        dve.wait_ge(gm_full, t_gm.next())
                        V.tensor_tensor(rw_G[:, h, :], sco[:, h % 2, :], ring[:, const, 0:4 * P], ALU.mult).then_inc(gm_done, 1)
                        t_gm_done.skip(1)
                    dve.wait_ge(gm_done, t_gm_done.n)
                    flat = lambda v: v.rearrange("p h k -> p (h k)")
                    for level in range(7):
                        if level:
                            dve.wait_ge(pe_for_vec, t_pe.next())
                            ins = V.tensor_tensor(flat(rw_XT), flat(rw_XT), lin[:, 2:4, :].rearrange("p a b -> p (a b)"), ALU.subtract)
                        if 0 < level < 6:
                            V.tensor_tensor(flat(rw_X), flat(rw_X), sco[:, :, :].rearrange("p a b -> p (a b)"), ALU.subtract)
                        if level < 6:
                            mask = ring[:, const, (4 + level) * P:(5 + level) * P].unsqueeze(1).to_broadcast([P, RW_HEADS, P])
                            ins = V.tensor_tensor(rw_BT, rw_G[:, :, 0:P], mask, ALU.mult)
                        ins.then_inc(vec_for_pe, 1)
                    pairs = lambda a: a.rearrange("p (h o d) -> p h o d", o=2, d=64)
                    for half in range(2):
                        rs = slice(64 * half, 64 * half + 64)
                        dve.wait_ge(pe_for_vec, t_pe.next())
                        V.tensor_copy(rw_U[rs, :], lin[rs, 2, :]).then_inc(dve_step, 1)
                        dve.wait_ge(dve_step, t_step.next())
                        for o in range(2):
                            ins = V.tensor_tensor(pairs(rw_U[rs, :])[:, :, o, :], pairs(rw_U[rs, :])[:, :, o, :], pairs(lin[rs, o, :])[:, :, o, :], ALU.add)
                        ins.then_inc(vec_for_pe, 1)
                        dve.wait_ge(pe_for_vec, t_pe.next())
                        V.tensor_copy(rw_y[rs, :], lin[rs, 2, :]).then_inc(dve_step, 1)
                        dve.wait_ge(dve_step, t_step.next())
                        for o in range(2):
                            V.tensor_tensor(pairs(rw_y[rs, :])[:, :, o, :], pairs(rw_y[rs, :])[:, :, o, :], pairs(sco[rs, o, :])[:, :, o, :], ALU.add)
                        V.tensor_tensor(rw_state, rw_state, lin[:, 0, 0:256].rearrange("p (a d) -> p a d", a=4), ALU.add).then_inc(dve_step, 1)
                        dve.wait_ge(dve_step, t_step.next())
                        V.tensor_tensor(rw_state, rw_state, rw_decay[:, :, half].unsqueeze(2).to_broadcast([P, 4, 64]), ALU.mult).then_inc(vec_for_pe, 1)
                    dve.wait_ge(dve_step, t_step.n)
                    y = heads(rw_y)
                    V.tensor_tensor(rw_tmp, r, k, ALU.mult).then_inc(dve_step, 1)
                    dve.wait_ge(dve_step, t_step.next())
                    centre_and_scale(y, heads(rw_pexc), 64, RW_GN_EPS)
                    V.tensor_tensor(rw_y, rw_y, gn_g, ALU.mult).then_inc(dve_step, 1)
                    dve.wait_ge(dve_step, t_step.next())
                    V.tensor_tensor(rw_y, rw_y, gn_b, ALU.add).then_inc(dve_step, 1)
                    dve.wait_ge(dve_step, t_step.next())
                    V.tensor_tensor(rw_tmp, rw_tmp, r_k, ALU.mult).then_inc(dve_step, 1)
                    dve.wait_ge(dve_step, t_step.next())
                    V.tensor_reduce(stat8, heads(rw_tmp), AX.X, ALU.add).then_inc(dve_step, 1)
                    dve.wait_ge(dve_step, t_step.next())
                    V.tensor_tensor(heads(rw_tmp), heads(v), spread(stat8, 64), ALU.mult).then_inc(dve_step, 1)
                    dve.wait_ge(dve_step, t_step.next())
                    V.tensor_tensor(rw_y, rw_y, rw_tmp, ALU.add).then_inc(dve_step, 1)
                    dve.wait_ge(dve_step, t_step.next())
                    ins = V.tensor_tensor(r, rw_y, rw_g, ALU.mult)
                    if t == NT - 1:
                        ins.then_inc(vec_for_pe, 1)
                    else:
                        ins.then_inc(dve_step, 1)
                        dve.wait_ge(dve_step, t_step.next())

            def mla():
                V.memset(mla_qpe, 0.0)
                passed(4)
                s = own_slot(3)
                V.tensor_copy(rope2, ring[:, s, 512:576]).then_inc(dve_step, 1)
                dve.wait_ge(dve_step, t_step.next())
                cos, sin = [rope2[:, 32 * n:32 * n + 32].rearrange("p (t f) -> p t f", t=NT) for n in range(2)]
                dve.wait_ge(proj_done, t_proj.next(2))
                for t in range(NT):
                    sq = mla_tmp[:, 0:2, :]
                    latents = mla_p[:, t, 0:512].rearrange("p (c d) -> p c d", c=2)
                    V.tensor_tensor(sq, latents, latents, ALU.mult).then_inc(dve_step, 1)
                    dve.wait_ge(dve_step, t_step.next())
                    V.tensor_reduce(bn[:, t, 0:2], sq, AX.X, ALU.add).then_inc(dve_step, 1)
                    dve.wait_ge(dve_step, t_step.next())
                    V.tensor_scalar(bn[:, t, 0:2], bn[:, t, 0:2], 1.0 / 256, None, ALU.mult).then_inc(dve_step, 1)
                    dve.wait_ge(dve_step, t_step.next())
                    root = rsqrt(bn[:, t, 0:2], ALU.add, RMS_EPS)
                    for c in range(2):
                        V.scalar_tensor_tensor(latents[:, c, :], latents[:, c, :], root[:, c:c + 1], ring[:, s, 256 * c:256 * c + 256], ALU.mult, ALU.mult)
                    key = mla_p[:, t, 512:544].unsqueeze(1)
                    rotate(key, cos[:, t, :], sin[:, t, :], 16, mla_tmp).then_inc(dve_step, 1)
                    dve.wait_ge(dve_step, t_step.next())
                    ins = V.tensor_copy(mla_kpe[:, t, :, :], key.to_broadcast([P, 4, 32]))
                    if t == NT - 1:
                        ins.then_inc(vec_for_pe, 1)
                    else:
                        ins.then_inc(dve_step, 1)
                        dve.wait_ge(dve_step, t_step.next())
                dve.wait_ge(proj_done, t_proj.next(3 + 4))
                passed(3 + 4)
                for t in range(NT):
                    queries = mla_q[:, t, :, 64:96]
                    V.tensor_copy(mla_qn[:, t, :, :], mla_q[:, t, :, 0:64])
                    V.tensor_copy(mla_kn[t], mla_kv[:, t, :, 0:64])
                    rotate(queries, cos[:, t, :], sin[:, t, :], 16, mla_tmp).then_inc(dve_step, 1)
                    dve.wait_ge(dve_step, t_step.next())
                    ins = V.tensor_copy(mla_qpe[:, t, :, 0, :], queries)
                    if t == NT - 1:
                        ins.then_inc(vec_for_pe, 1)
                    else:
                        ins.then_inc(dve_step, 1)
                        dve.wait_ge(dve_step, t_step.next())
                attend(MLA_HEADS, 1, lambda g: causal[:, :, :], 96 ** -0.5)

            def route():
                s = own_slot(5)
                V.memset(group8, MASKED)
                V.tensor_copy(numbers, ring[:, s, 640:640 + EXPERTS]).then_inc(vec_for_pe, 1)
                dve.wait_ge(slots_used, used.n)
                V.tensor_scalar(x[:, :, :], x[:, :, :], ALPHA_2, None, ALU.mult).then_inc(y_added, 1)
                V.tensor_copy(logits36, sco[:, 0, 0:128].rearrange("p (t n) -> p t n", t=NT)[:, :, 0:36]).then_inc(vec_for_pe, 1)
                V.memset(router, 0.0).then_inc(dve_step, 1)
                dve.wait_ge(dve_step, t_step.next())
                V.tensor_copy(group8[:, :, 0:GROUPS], logits36[:, :, 0:GROUPS]).then_inc(dve_step, 1)
                dve.wait_ge(dve_step, t_step.next())
                for t in range(NT):
                    index = ints[:, 8 * t:8 * t + 8]
                    V.max(top8[:, t, :], group8[:, t, :]).then_inc(dve_step, 1)
                    dve.wait_ge(dve_step, t_step.next())
                    V.max_index(index, top8[:, t, :], group8[:, t, :]).then_inc(dve_step, 1)
                    dve.wait_ge(dve_step, t_step.next())
                    V.tensor_scalar(router[:, t, 8:9], top8[:, t, 0:1], -1.0, None, ALU.mult)
                    V.tensor_copy(router[:, t, 0:1], index[:, 0:1]).then_inc(dve_step, 1)
                    dve.wait_ge(dve_step, t_step.next())
                    V.tensor_scalar(group_hot[:, t, :], numbers[:, 0:GROUPS], router[:, t, 0:1], 1.0, ALU.is_equal, ALU.subtract).then_inc(dve_step, 1)
                    dve.wait_ge(dve_step, t_step.next())
                    V.tensor_scalar(group_hot[:, t, :], group_hot[:, t, :], -MASKED, None, ALU.mult).then_inc(dve_step, 1)
                    dve.wait_ge(dve_step, t_step.next())
                    V.tensor_tensor(picked[:, t, :, :], logits36[:, t, GROUPS:36].rearrange("p (g e) -> p g e", g=GROUPS),
                                    spread(group_hot[:, t, :], PER_GROUP), ALU.add).then_inc(dve_step, 1)
                    dve.wait_ge(dve_step, t_step.next())
                    experts = picked[:, t, :, :].rearrange("p g e -> p (g e)")
                    V.max(top8[:, t, :], experts).then_inc(dve_step, 1)
                    dve.wait_ge(dve_step, t_step.next())
                    V.max_index(index, top8[:, t, :], experts).then_inc(dve_step, 1)
                    dve.wait_ge(dve_step, t_step.next())
                    V.tensor_copy(router[:, t, 0:2], index[:, 0:2])
                    ins = V.tensor_tensor(router[:, t, 10:11], top8[:, t, 1:2], top8[:, t, 0:1], ALU.subtract)
                    if t == NT - 1:
                        ins.then_inc(vec_for_act, 1)
                    else:
                        ins.then_inc(dve_step, 1)
                        dve.wait_ge(dve_step, t_step.next())
                dve.wait_ge(act_for_vec, t_act.next())
                for t in range(NT):
                    e2, total = router[:, t, 11:12], router[:, t, 9:10]
                    V.scalar_tensor_tensor(router[:, t, 12:13], e2, 1.0, total, ALU.add, ALU.mult).then_inc(dve_step, 1)
                    dve.wait_ge(dve_step, t_step.next())
                    V.reciprocal(router[:, t, 13:14], router[:, t, 12:13]).then_inc(dve_step, 1)
                    dve.wait_ge(dve_step, t_step.next())
                    V.tensor_tensor(router[:, t, 14:15], router[:, t, 13:14], e2, ALU.mult).then_inc(dve_step, 1)
                    dve.wait_ge(dve_step, t_step.next())
                    V.tensor_scalar(hot[:, t, :], numbers, router[:, t, 0:1], router[:, t, 13:14], ALU.is_equal, ALU.mult)
                    V.tensor_scalar(gates[:, t, :], numbers, router[:, t, 1:2], router[:, t, 14:15], ALU.is_equal, ALU.mult).then_inc(dve_step, 1)
                    dve.wait_ge(dve_step, t_step.next())
                    V.tensor_tensor(gates[:, t, :], gates[:, t, :], hot[:, t, :], ALU.add).then_inc(dve_step, 1)
                    dve.wait_ge(dve_step, t_step.next())

            def moe():
                route()
                with rounds(dve, EXPERTS // 2, {t_silu: 8, used: RING, t_y: 2}) as i:
                    for j in range(2):
                        for f in range(4):
                            dve.wait_ge(silu_done, t_silu.next())
                            V.tensor_tensor(hT[:, j, f, :], silu_g[:, f % 2, :], sco[:, f % 2, SEQ:2 * SEQ], ALU.mult).then_inc(h_done, 1)
                        dve.wait_ge(slots_used, used.next(6))
                        dve.wait_ge(y_added, t_y.next())
                        for t in range(NT):
                            ins = V.scalar_tensor_tensor(x[:, t, :], lin[:, 2 * t:2 * t + 2, :].rearrange("p a b -> p (a b)"),
                                                         gates[:, t, bass.ds(i * 2 + j, 1)], x[:, t, :], ALU.mult, ALU.add)
                        ins.then_inc(y_added, 1)
                used.skip(-EXPERTS * 6)
                passed(EXPERTS * 6)
                s = own_slot(2)
                dve.wait_ge(y_added, t_y.next())
                for t in range(NT):
                    normalise(x, t, s)

            dve.wait_ge(input_loaded, 16 * 6)
            dve.wait_ge(pool_step, 1)
            s = own_slot(2)
            for t in range(NT):
                normalise(memrows, t, s)
            V.tensor_copy(pos_f, ints[:, 0:NT].bitcast(I32)).then_inc(dve_step, 1)
            dve.wait_ge(dve_step, t_step.next())
            for t in range(NT):
                V.tensor_scalar(small[:, 96 + 8 * t:104 + 8 * t], inv_freq, pos_f[:, t:t + 1], None, ALU.mult)
                last = V.tensor_scalar(small[:, 112 + 8 * t:120 + 8 * t], inv_freq, pos_f[:, t:t + 1], None, ALU.mult)
            last.then_inc(dve_step, 1)
            dve.wait_ge(dve_step, t_step.next())
            ROUND = 1.5 * 2.0 ** 23
            TURN = (6.28125, 0.0019340515136718750, 1.2556659146180184e-06)
            whole = [rope_tmp[:, 0, 0:16], rope_tmp[:, 0, 16:32]]
            V.tensor_scalar(whole[0], small[:, 96:112], 1 / (2 * math.pi), 0.25, ALU.mult, ALU.add).then_inc(dve_step, 1)
            dve.wait_ge(dve_step, t_step.next())
            V.tensor_scalar(whole[0], whole[0], ROUND, None, ALU.add).then_inc(dve_step, 1)
            dve.wait_ge(dve_step, t_step.next())
            V.tensor_scalar(whole[1], small[:, 112:128], 1 / (2 * math.pi), ROUND, ALU.mult, ALU.add).then_inc(dve_step, 1)
            dve.wait_ge(dve_step, t_step.next())
            V.tensor_scalar(rope_tmp[:, 0, 0:32], rope_tmp[:, 0, 0:32], ROUND, None, ALU.subtract).then_inc(dve_step, 1)
            dve.wait_ge(dve_step, t_step.next())
            for c in TURN:
                V.scalar_tensor_tensor(small[:, 96:128], rope_tmp[:, 0, 0:32], -c, small[:, 96:128], ALU.mult, ALU.add).then_inc(dve_step, 1)
                dve.wait_ge(dve_step, t_step.next())
            V.tensor_scalar(small[:, 96:112], small[:, 96:112], math.pi / 2, None, ALU.add).then_inc(dve_step, 1)
            dve.wait_ge(dve_step, t_step.next())
            V.tensor_scalar(small[:, 96:128], small[:, 96:128], 3.1415925, -3.1415925, ALU.min, ALU.max).then_inc(vec_for_act, 1)
            dve.wait_ge(act_for_vec, t_act.next())
            for layer in range(FIRST_LAYERS):
                kind = kind_of(layer)
                proj = projA if kind == 0 else projBC
                width = WIDTH_A if kind == 0 else WIDTH_BC
                n_chunks = len(chunks_of(width))
                dve.wait_ge(proj_done, t_proj.next(n_chunks + 1))
                passed(2 * n_chunks + 2)
                for t in range(NT):
                    last = rotate(proj[:, t, 0:2 * MIX].rearrange("p (h d) -> p h d", d=DH), rope_cos[:, t, :], rope_sin[:, t, :], ROPE_HALF)
                    if kind == 0:
                        last.then_inc(dve_step, 1)
                        dve.wait_ge(dve_step, t_step.next())
                        last = rotate(proj[:, t, 2304:2816].rearrange("p (h d) -> p h d", d=DH), rope_cos[:, t, :], rope_sin[:, t, :], ROPE_HALF)
                    if t < NT - 1 or kind == 0:
                        last.then_inc(dve_step, 1)
                        dve.wait_ge(dve_step, t_step.next())
                if kind == 0:
                    s = own_slot(2)
                    for t in range(NT):
                        ki = proj[:, t, 2824:2888]
                        V.tensor_scalar(proj[:, t, 2816:2824], proj[:, t, 2816:2824], (IDX_HEADS * DH) ** -0.5, None, ALU.mult)
                        V.bn_stats(bn[:, t, 0:6], ki).then_inc(dve_step, 1)
                        dve.wait_ge(dve_step, t_step.next())
                        V.bn_aggr(mean_var[:, t, :], bn[:, t, 0:6]).then_inc(dve_step, 1)
                        dve.wait_ge(dve_step, t_step.next())
                        rstd = rsqrt(mean_var[:, t, 1:2], ALU.add, LN_EPS)
                        V.scalar_tensor_tensor(ki, ki, mean_var[:, t, 0:1], ring[:, s, 0:DH], ALU.subtract, ALU.mult).then_inc(dve_step, 1)
                        dve.wait_ge(dve_step, t_step.next())
                        V.scalar_tensor_tensor(ki, ki, rstd, ring[:, s, DH:2 * DH], ALU.mult, ALU.add).then_inc(dve_step, 1)
                        dve.wait_ge(dve_step, t_step.next())
                        rotate(ki.unsqueeze(1), rope_cos[:, t, :], rope_sin[:, t, :], ROPE_HALF).then_inc(dve_step, 1)
                        dve.wait_ge(dve_step, t_step.next())
                        V.tensor_copy(ki2[:, t, 0, :], ki)
                        last = V.tensor_copy(ki2[:, t, 1, :], ki)
                        if t < NT - 1:
                            last.then_inc(dve_step, 1)
                            dve.wait_ge(dve_step, t_step.next())
                last.then_inc(rope_done, 1)
                if kind == 0:
                    select_keys(proj)
                attend(MEM_HEADS, 1, lambda g: None, DH ** -0.5)
                if kind == 0:
                    attend(HEADS, 1, lambda g: dsa_mask, DH ** -0.5)
                elif kind == 1:
                    s = own_slot(1)
                    masks = ring[:, s, 0:3 * NT * SEQ].rearrange("p (g t k) -> p g t k", g=3, t=NT)
                    attend(4, 3, lambda g: masks[:, g, :, :], DH ** -0.5)
                else:
                    attend(HEADS, 1, lambda g: causal[:, :, :], DH ** -0.5)
                passed(4)
                dve.wait_ge(slots_used, used.n)
                add_and_normalise(ALPHA)
                ffn()
                passed(3 * (D_FF // (2 * P)))
                dve.wait_ge(slots_used, used.n)
                add_and_normalise(ALPHA)
            for layer in range(SECOND_LAYERS):
                if layer % 2 == 0:
                    mixer_ab()
                else:
                    mla()
                passed(4)
                dve.wait_ge(slots_used, used.n)
                add_and_normalise(ALPHA_2)
                if layer == 0:
                    passed(1)
                passed(4 + 8)
                t_proj.skip(2 + 4)
                attend(XA_HEADS, 1, lambda g: None, (D // XA_HEADS) ** -0.5)
                passed(4)
                dve.wait_ge(slots_used, used.n)
                add_and_normalise(ALPHA_2)
                moe()


_INS = ["x", "mem", "positions", "mem_ln_g", "mem_ln_b", "w_in_a", "idx_kn_g", "idx_kn_b", "w_in_b", "w_in_c", "w_mem_kv",
        "w_out", "ln1_g", "ln1_b", "w_gate_up", "w_down", "ln2_g", "ln2_b", "mem_2", "ab_w_in_2", "ab_mu_2", "rw_w0_2",
        "rw_w2_2", "rw_a0_2", "rw_a2_2", "rw_g2_2", "rw_k_k_2", "rw_k_a_2", "rw_r_k_2", "rw_gn_g_2", "rw_gn_b_2",
        "sg_ln_g_2", "sg_ln_b_2", "sg_ws_2", "sg_b_2", "ab_w_out_2", "mla_w_in_2", "mla_q_norm_2", "mla_kv_norm_2",
        "mla_wq_b_2", "mla_wkv_b_2", "mla_w_out_2", "ln1_g_2", "ln1_b_2", "xa_wq_2", "xa_wkv_2", "xa_wo_2", "ln2_g_2",
        "ln2_b_2", "moe_w_group_2", "moe_b_group_2", "moe_w_expert_2", "moe_b_expert_2", "moe_w_gate_2",
        "moe_w_up_2", "moe_w_down_2", "ln3_g_2", "ln3_b_2"]


def kernel(**inputs):
    import concourse.bacc as _bacc
    from concourse.bass_utils import run_bass_kernel_spmd as _run

    nc = _bacc.Bacc("TRN2", target_bir_lowering=False, num_devices=1)
    arrays, args = {}, {}
    for name in _INS + ["consts"]:
        a = shape_constants() if name == "consts" else np.ascontiguousarray(inputs[name])
        if name == "positions":
            a = np.ascontiguousarray(a.reshape(NT, P).T)
        if name == "sg_b_2":
            a = np.ascontiguousarray(a.transpose(0, 2, 1))
        arrays[f"in_{name}"] = a
        args[name] = nc.dram_tensor(f"in_{name}", a.shape, mybir.dt.from_np(a.dtype), kind="ExternalInput").ap()
    o = nc.dram_tensor("out_0", (1, SEQ, D), F32, kind="ExternalOutput").ap()
    build(nc, args, o)
    r = _run(nc, [arrays], core_ids=[0])
    return r.results[0]["out_0"]
```

```python
import math
from contextlib import ExitStack, contextmanager

import numpy as np

import concourse.bass as bass
from concourse import mybir

ALU = mybir.AluOpType
ACT = mybir.ActivationFunctionType
AX = mybir.AxisListType
F32 = mybir.dt.float32
I32 = mybir.dt.int32
U32 = mybir.dt.uint32

P = 128
D = 1024
SEQ = 256
NT = SEQ // P
KD = D // P
MASKED = -1.0e30
TAKEN = -2.0e30
LN_EPS = 1e-5

DEPTH = 4
HEADS, DH = 12, 64
MIX = HEADS * DH
MEM_HEADS = 4
ROPE_HALF = DH // 8
ROPE_THETA = 500000.0
IDX_HEADS = 8
TOPK = SEQ // 4
WIDTH_A = 3 * MIX + IDX_HEADS * DH + IDX_HEADS + DH + MEM_HEADS * DH
WIDTH_BC = 3 * MIX + MEM_HEADS * DH
D_FF = -(-8 * D // (3 * 256)) * 256
ALPHA = (2 * DEPTH) ** 0.25
DILATIONS = (1, 4, 16)
DIL_WINDOW = 128

DEPTH_2 = 2
ALPHA_2 = (2 * DEPTH_2) ** 0.25
RW_HEADS, RW_DIM = 8, 512
RW_CHUNK = 64
RW_SHIFT = 3 * RW_DIM + 64 + 64 + 128
RW_GN_EPS = 64e-5
SG_GROUPS = 4
AB_IN = RW_SHIFT + 1024
MLA_HEADS = 16
MLA_IN = 256 + 256 + 32
RMS_EPS = 1e-6
XA_HEADS = 4
GROUPS, PER_GROUP = 4, 8
EXPERTS = GROUPS * PER_GROUP
MOE_FF = 512
PAIRS = EXPERTS // 2
PLACES = P // 2
COLUMNS = EXPERTS + 2

RING = 12
SLOT = 2048

FIRST_LAYERS = DEPTH
SECOND_LAYERS = DEPTH_2
ROOTS = NT * (1 + 2 * FIRST_LAYERS + len(range(0, FIRST_LAYERS, 3)) + 3 * SECOND_LAYERS
              + 3 * len(range(0, SECOND_LAYERS, 2)) + len(range(1, SECOND_LAYERS, 2)))
LAYER_NORMS = 1 + 2 * FIRST_LAYERS + 3 * SECOND_LAYERS
RW_SLOTS = (1, 4, 3, 5, 2, 1)

CONST_PARTS = [("ident", P), ("causal", NT * SEQ), ("dilated", 3 * NT * SEQ), ("inv_freq", ROPE_HALF),
               ("rw_masks", 4 * P), ("rw_levels", 6 * P), ("rw_chunk", 2), ("sg_mask", P),
               ("rope2_cos", NT * 16), ("rope2_sin", NT * 16), ("numbers", EXPERTS), ("places", PLACES), ("one", P),
               ("earlier", P), ("all", P)]
CONST_AT = {}
for _name, _size in CONST_PARTS:
    CONST_AT[_name] = (sum(n for _, n in CONST_PARTS[:len(CONST_AT)]), _size)
CONST_WIDTH = sum(n for _, n in CONST_PARTS)
ROUTER_PARTS = ("numbers", "places", "one", "earlier", "all")
ROUTER_CONST = 640


def router_const(name):
    lo = ROUTER_CONST + CONST_AT[name][0] - CONST_AT["numbers"][0]
    return slice(lo, lo + CONST_AT[name][1])


def shape_constants():
    c = np.zeros((P, CONST_WIDTH), np.float32)

    def put(name, a):
        at, n = CONST_AT[name]
        c[:, at:at + n] = np.asarray(a, np.float32).reshape(P, n)

    p = np.arange(P)
    q = p[:, None, None] + P * np.arange(NT)[None, :, None]
    k = np.arange(SEQ)[None, None, :]
    put("ident", np.eye(P))
    put("causal", np.where(k <= q, 0.0, MASKED))
    put("dilated", np.stack([np.where((k <= q) & ((q - k) % r == 0) & (q - k <= r * DIL_WINDOW), 0.0, MASKED)
                             for r in DILATIONS], axis=1))
    put("inv_freq", np.tile(np.float32(ROPE_THETA) ** (-np.arange(ROPE_HALF, dtype=np.float32) / ROPE_HALF), (P, 1)))
    row, col = p[:, None], p[None, :]
    same = row // RW_CHUNK == col // RW_CHUNK
    strict, upto = same & (row < col), same & (row <= col)
    put("rw_masks", np.concatenate([strict, upto, strict, upto], axis=1))
    put("rw_levels", np.concatenate([(row // s + 1 == col // s) & (col // s % 2 == 1)
                                     for s in (1, 2, 4, 8, 16, 32)], axis=1))
    put("rw_chunk", p[:, None] // RW_CHUNK == np.arange(2)[None, :])
    put("sg_mask", col <= row)
    inv2 = np.float32(10000.0) ** (-np.arange(16, dtype=np.float32) / 16)
    ang = (p[:, None] + P * np.arange(NT)[None, :]).astype(np.float32)[..., None] * inv2
    put("rope2_cos", np.cos(ang))
    put("rope2_sin", np.sin(ang))
    put("numbers", np.tile(np.arange(EXPERTS), (P, 1)))
    put("places", np.tile(np.arange(PLACES), (P, 1)))
    put("one", np.broadcast_to(row == 0, (P, P)))
    put("earlier", row < col)
    put("all", np.ones((P, P)))
    return c


class Tally:

    def __init__(self, sem, ahead=0):
        self.sem = sem
        self.n = -ahead
        self.turn = None

    def skip(self, k=1):
        self.n += k

    def next(self, k=1):
        self.n += k
        return self.value()

    def due(self):
        self.n += 1
        return self.turn is not None or self.n > 0

    def value(self):
        if self.turn is None:
            return self.n
        i, per = self.turn
        assert self.n > 0
        return i * per + self.n


@contextmanager
def rounds(eng, count, per):
    first = {t: t.n for t in per}
    with eng.Fori(0, count) as i:
        for t, k in per.items():
            t.turn = (i, k)
        yield i
        for t, k in per.items():
            assert t.n - first[t] == k, (t.sem, t.n - first[t], k)
            t.turn = None
            t.n = first[t] + k * count


def chunks_of(width):
    return [(c, min(512, width - c)) for c in range(0, width, 512)]


def build(nc, A, out):
    ctx = ExitStack()
    with ctx:
        def sem(name):
            return ctx.enter_context(nc.semaphore(name))

        def psum(name, banks):
            return ctx.enter_context(nc.psum_tensor(name, [P, banks, 512], F32))

        ring = ctx.enter_context(nc.sbuf_tensor("ring", [P, RING, SLOT], F32))
        x = ctx.enter_context(nc.sbuf_tensor("x", [P, NT, D], F32))
        ident = ctx.enter_context(nc.sbuf_tensor("ident", [P, P], F32))
        causal = ctx.enter_context(nc.sbuf_tensor("causal", [P, NT, SEQ], F32))
        small = ctx.enter_context(nc.sbuf_tensor("small", [P, 128], F32))
        ints = ctx.enter_context(nc.sbuf_tensor("ints", [P, 16 + SECOND_LAYERS], U32))
        roots = ctx.enter_context(nc.sbuf_tensor("roots", [P, 5, 8], F32))
        ARENA = 25056
        arena = ctx.enter_context(nc.sbuf_tensor("arena", [P, ARENA], F32))

        def at(offset, *dims):
            n = math.prod(dims)
            assert offset + n <= ARENA, (offset, dims)
            v = arena[:, offset:offset + n]
            if len(dims) == 1:
                return v
            names = "abcde"[:len(dims)]
            return v.rearrange(f"p ({' '.join(names)}) -> p {' '.join(names)}",
                               **dict(zip(names, dims)))

        xT = at(0, KD, SEQ)
        mixT = at(2048, KD, SEQ)
        memT = at(4096, KD, SEQ)
        PROJ = 6144
        projA = at(PROJ, NT, WIDTH_A)
        projBC = at(PROJ, NT, WIDTH_BC)
        dilated12 = at(PROJ + NT * WIDTH_BC, 2, NT, SEQ)
        QKT = PROJ + NT * WIDTH_A
        qkT = at(QKT, 21, SEQ)
        memrows = at(QKT, NT, D)
        mkv = at(QKT + 21 * SEQ, NT, 512)
        ATT = QKT + 21 * SEQ + NT * 512
        S1 = at(ATT, 2, NT, 1, SEQ)
        S3 = at(ATT, 2, NT, 3, SEQ)
        Pn = at(ATT + 3072, 2, NT, SEQ)
        PT = at(ATT + 4096, 2, NT, SEQ)
        dsa_mask = at(ATT + 5120, NT, SEQ)
        dilated0 = dsa_mask
        idx_relu = at(ATT + 2048, 2, 2, SEQ)
        idx_score = at(ATT + 1024, NT, SEQ)
        ki2 = at(ATT, NT, 2, DH)
        rope_tmp = at(ATT + 3072, 4, 24 * ROPE_HALF)
        silu_g = at(PROJ, 2, SEQ)
        hT = at(PROJ + 512, 2, 4, SEQ)
        GATE = PROJ + 512 + 2048
        gates = at(GATE, NT, COLUMNS)
        logits36 = at(GATE + 80, NT, GROUPS + EXPERTS)
        picked = at(GATE + 160, NT, GROUPS, PER_GROUP)
        group_hot = at(GATE + 224, NT, GROUPS)
        group8 = at(GATE + 240, NT, 8)
        top8 = at(GATE + 256, NT, 8)
        router = at(GATE + 272, NT, 16)
        hot = at(GATE + 304, NT, EXPERTS)
        numbers = at(GATE + 368, EXPERTS)
        chosen = at(GATE + 400, NT, COLUMNS)
        place_of = at(GATE + 480, NT, COLUMNS)
        late_gates = at(GATE + 560, NT, EXPERTS)
        most = at(GATE + 624, 8)
        places = at(GATE + 640, PLACES)
        PAIR = GATE + 768
        rowsT = at(PAIR, KD, P)
        pair_silu = at(PAIR + 1024, MOE_FF)
        pair_h = at(PAIR + 1536, MOE_FF)
        pair_hT = at(PAIR + 2048, 4, P)
        spreadT = at(PAIR + 2560, NT, P)
        pair_y = at(PAIR + 2816, D)
        gathering = at(PAIR + 3840, NT, P)
        gated = at(PAIR + 4096, NT, P)
        moe_sum = at(2048, NT, D)
        p_ab = at(PROJ, NT, AB_IN)
        RW = PROJ + NT * AB_IN
        shifted = at(RW, NT, RW_SHIFT)
        rw_a, rw_kk, rw_b, rw_k, rw_r, rw_pinv, rw_pexc, rw_tmp, rw_g, rw_lw = [at(RW + 512 * j, 512) for j in range(10)]
        rwT = at(RW + 5120, 4, 4, P)
        rw_G = at(RW + 7168, RW_HEADS, 4 * P)
        rw_X = at(RW + 11264, RW_HEADS, P)
        rw_XT = at(0, RW_HEADS, P)
        rw_T1 = at(1024, RW_HEADS, P)
        rw_BT = at(4096, RW_HEADS, P)
        loraT = at(5120, 2, P)
        rw_state = at(5376, 4, 64)
        rw_U = at(5632, 512)
        rw_SA = at(RW + 12288, 512)
        rw_decay = at(RW + 12800, 4, 2)
        stat8 = at(RW + 12816, 8)
        wmT = at(2048, SG_GROUPS, P)
        rw_y = at(2560, 512)
        mla_q = at(PROJ, NT, MLA_HEADS, 96)
        mla_kv = at(PROJ + 3072, NT, MLA_HEADS, P)
        mlaT = at(PROJ + 7168, 21, SEQ)
        mlaT_more = at(0, 4, SEQ)
        mla_p = at(ATT, NT, MLA_IN)
        mla_qpe = at(ATT + 1088, NT, MLA_HEADS, 2, 32)
        mla_tmp = at(ATT + 3200, 4, 256)
        rope2 = at(ATT + 4480, 64)
        mla_kpe = at(ATT + 4224, NT, 4, 32)
        mla_qn = at(2048, NT, MLA_HEADS, 64)
        mla_kn = [at(1024, MLA_HEADS, 64), at(ATT + 5120, MLA_HEADS, 64)]
        latentT = at(2304, 4, SEQ)
        xa_v = at(PROJ, NT, D)
        xa_qT = at(PROJ + 2048, KD, SEQ)
        xa_kT = at(PROJ + 4096, KD, SEQ)
        root_in, root_out, root_power = roots[:, 0:2, :], roots[:, 2:4, :], roots[:, 4, :]
        rope_cos = small[:, 0:16].rearrange("p (t f) -> p t f", t=NT)
        rope_sin = small[:, 16:32].rearrange("p (t f) -> p t f", t=NT)
        bn = small[:, 32:56].rearrange("p (t f) -> p t f", t=NT)
        mean_var = small[:, 56:60].rearrange("p (t f) -> p t f", t=NT)
        negmax = small[:, 64:68].rearrange("p (b t) -> p b t", b=2)
        rowsum = small[:, 68:72].rearrange("p (b t) -> p b t", b=2)
        rinv = small[:, 72:76].rearrange("p (b t) -> p b t", b=2)
        pos_f = small[:, 76:78]
        inv_freq = small[:, 80:88]
        top_score = small[:, 88:96]
        angle = small[:, 96:112].rearrange("p (t f) -> p t f", t=NT)
        turns = small[:, 112:128].rearrange("p (t f) -> p t f", t=NT)

        lin = psum("lin", 4)
        trp = psum("trp", 2)
        sco = psum("sco", 2)

        slot_full = [sem(f"slot_full{s}") for s in range(RING)]
        slots_used = sem("slots_used")
        x_loaded, input_loaded = sem("x_loaded"), sem("input_loaded")
        proj_done = sem("proj_done")
        tr_full, tr_done = sem("tr_full"), sem("tr_done")
        ln_done = sem("ln_done")
        rope_done = sem("rope_done")
        logit_full, logit_free = sem("logit_full"), sem("logit_free")
        smax_done, exp_done, p_done = sem("smax_done"), sem("exp_done"), sem("p_done")
        pt_full, pt_done = sem("pt_full"), sem("pt_done")
        pv_full, pv_done = sem("pv_full"), sem("pv_done")
        dots_full, dots_done, score_added = sem("dots_full"), sem("dots_done"), sem("score_added")
        gu_full, silu_done, h_done = sem("gu_full"), sem("silu_done"), sem("h_done")
        selected, selection_used = sem("selected"), sem("selection_used")
        pair_out, combined, y_added = sem("pair_out"), sem("combined"), sem("y_added")
        overflow_known = sem("overflow_known")
        rest_loaded = [sem(f"rest_loaded{n}") for n in range(SECOND_LAYERS)]
        rest_gate_up = [sem(f"rest_gate_up{n}") for n in range(SECOND_LAYERS)]
        rest_silu = [sem(f"rest_silu{n}") for n in range(SECOND_LAYERS)]
        rest_hidden = [sem(f"rest_hidden{n}") for n in range(SECOND_LAYERS)]
        rest_output = [sem(f"rest_output{n}") for n in range(SECOND_LAYERS)]
        rest_added = [sem(f"rest_added{n}") for n in range(SECOND_LAYERS)]
        gm_full, gm_done = sem("gm_full"), sem("gm_done")
        vec_for_pe, vec_for_act = sem("vec_for_pe"), sem("vec_for_act")
        act_for_pe, act_for_vec = sem("act_for_pe"), sem("act_for_vec")
        pe_for_act, pe_for_vec = sem("pe_for_act"), sem("pe_for_vec")
        shift_loaded = sem("shift_loaded")
        dve_step = sem("dve_step")
        root_asked, root_done = sem("root_asked"), sem("root_done")
        pool_step = sem("pool_step")
        out_written = sem("out_written")

        def kind_of(layer):
            return layer % 3

        block = ctx.enter_context(nc.Block())

        @block.sync
        def _(sp):
            free = Tally(slots_used, ahead=RING)
            place = [0]

            def slot():
                if free.due():
                    sp.wait_ge(slots_used, free.value())
                s = place[0] % RING
                place[0] += 1
                return s

            def load(s, lo, hi, src):
                dst = ring[:, s, lo:hi]
                if len(src.shape) == 3:
                    dst = dst.rearrange("p (k n) -> p k n", k=src.shape[1])
                sp.dma_start(dst, src).then_inc(slot_full[s], 16)

            def load_linear(w):
                K, N = w.shape
                per = min(4, K // P)
                for c, n in chunks_of(N):
                    for k in range(0, K // P, per):
                        load(slot(), 0, per * n,
                             w[k * P:(k + per) * P, c:c + n].rearrange("(k p) n -> p k n", p=P))

            def rows(v):
                return v.partition_broadcast(P)

            def load_ln(g, b):
                s = slot()
                load(s, 0, D, rows(g))
                load(s, D, 2 * D, rows(b))

            def load_ffn(gate_up, down):
                def unit(u):
                    f = u * 2 * P
                    load(slot(), 0, SLOT, gate_up[:, bass.ds(f, 2 * P)].rearrange("(k p) n -> p k n", p=P))
                    load(slot(), 0, SLOT, gate_up[:, bass.ds(f + D_FF, 2 * P)].rearrange("(k p) n -> p k n", p=P))
                    load(slot(), 0, SLOT, down[bass.ds(f, 2 * P), :].rearrange("(k p) n -> p k n", p=P))
                units = D_FF // (2 * P)
                with rounds(sp, units // 4, {free: RING}) as i:
                    for u in range(4):
                        unit(i * 4 + u)
                place[0] += (units // 4 - 1) * RING
                for u in range(units // 4 * 4, units):
                    unit(u)

            def load_moe(layer):
                s = slot()
                v = ring[:, s, 0:KD * 36].rearrange("p (k n) -> p k n", k=KD)
                for lo, hi, name in ((0, GROUPS, "moe_w_group_2"), (GROUPS, 36, "moe_w_expert_2")):
                    sp.dma_start(v[:, :, lo:hi], A[name][layer].rearrange("(k p) n -> p k n", p=P)).then_inc(slot_full[s], 16)
                load(s, 512, 516, rows(A["moe_b_group_2"][layer]))
                load(s, 516, 548, rows(A["moe_b_expert_2"][layer]))
                lo, hi = CONST_AT[ROUTER_PARTS[0]][0], sum(CONST_AT[ROUTER_PARTS[-1]])
                load(s, ROUTER_CONST, ROUTER_CONST + hi - lo, A["consts"][:, lo:hi])

                def pieces(e):
                    for name in ("moe_w_gate_2", "moe_w_up_2"):
                        for k in range(2):
                            yield A[name][layer, e, k * 512:(k + 1) * 512, :].rearrange("(k p) n -> p k n", p=P)
                    for f in range(2):
                        yield A["moe_w_down_2"][layer, e, f * 256:(f + 1) * 256, :].rearrange("(k p) n -> p k n", p=P)

                with rounds(sp, PAIRS, {free: RING}) as i:
                    first, second = list(pieces(i * 2)), list(pieces(i * 2 + 1))
                    for both in zip(first, second):
                        for src in both:
                            load(slot(), 0, SLOT, src)
                place[0] += (PAIRS - 1) * RING

                sp.wait_ge(overflow_known, layer + 1)
                overflow = sp.value_load(ints[0:1, 16 + layer:17 + layer], min_val=0, max_val=1)
                t_added = Tally(rest_added[layer])
                with sp.If(overflow):
                    sp.wait_ge(slots_used, place[0])
                    with rounds(sp, EXPERTS, {t_added: 1}) as i:
                        sp.wait_ge(rest_added[layer], t_added.next())
                        for n, src in enumerate(pieces(i)):
                            dst = ring[:, n, :].rearrange("p (k n) -> p k n", k=src.shape[1])
                            sp.dma_start(dst, src).then_inc(rest_loaded[layer], 16)
                    sp.wait_ge(rest_added[layer], t_added.next())

            def const(name):
                a, n = CONST_AT[name]
                return A["consts"][:, a:a + n]

            sp.dma_start(ident[:, :], const("ident")).then_inc(x_loaded, 16)
            sp.dma_start(x[:, :, :], A["x"][0].rearrange("(t p) d -> p t d", p=P)).then_inc(x_loaded, 16)
            sp.dma_start(memrows, A["mem"][0].rearrange("(t p) d -> p t d", p=P)).then_inc(input_loaded, 16)
            sp.dma_start(causal[:, :, :].rearrange("p t k -> p (t k)"), const("causal")).then_inc(input_loaded, 16)
            sp.dma_start(inv_freq, const("inv_freq")).then_inc(input_loaded, 16)
            sp.dma_start(ints[:, 0:NT].bitcast(I32), A["positions"]).then_inc(input_loaded, 16)
            for layer in range(FIRST_LAYERS):
                kind, j = kind_of(layer), layer // 3
                w_in = (A["w_in_a"], A["w_in_b"], A["w_in_c"])[kind][j]
                load_linear(w_in)
                if layer == 0:
                    load_ln(A["mem_ln_g"], A["mem_ln_b"])
                load_linear(A["w_mem_kv"][layer])
                if kind == 0:
                    s = slot()
                    load(s, 0, DH, rows(A["idx_kn_g"][j]))
                    load(s, DH, 2 * DH, rows(A["idx_kn_b"][j]))
                if kind == 1:
                    s = slot()
                    load(s, 0, 3 * NT * SEQ, const("dilated"))
                load_linear(A["w_out"][layer])
                load_ln(A["ln1_g"][layer], A["ln1_b"][layer])
                load_ffn(A["w_gate_up"][layer], A["w_down"][layer])
                load_ln(A["ln2_g"][layer], A["ln2_b"][layer])

            for layer in range(SECOND_LAYERS):
                j = layer // 2
                if layer % 2 == 0:
                    load_linear(A["ab_w_in_2"][j])
                    s = slot()
                    load(s, 0, RW_SHIFT, rows(A["ab_mu_2"][j]))
                    s = slot()
                    for n, name in enumerate(("rw_w0_2", "rw_a0_2", "rw_k_k_2", "rw_k_a_2")):
                        load(s, 512 * n, 512 * n + 512, rows(A[name][j]))
                    s = slot()
                    load(s, 0, 512, rows(A["rw_r_k_2"][j].rearrange("h d -> (h d)")))
                    load(s, 512, 1024, rows(A["rw_gn_g_2"][j]))
                    load(s, 1024, 1536, rows(A["rw_gn_b_2"][j]))
                    s = slot()
                    sp.dma_start(ring[0:64, s, 0:512], A["rw_w2_2"][j]).then_inc(slot_full[s], 16)
                    sp.dma_start(ring[64:128, s, 0:512], A["rw_a2_2"][j]).then_inc(slot_full[s], 16)
                    load(s, 512, 1024, A["rw_g2_2"][j])
                    load(s, 1024, 1536, A["sg_ws_2"][j].rearrange("g t s -> t g s"))
                    load(s, 1536, 1536 + SG_GROUPS, A["sg_b_2"][j])
                    s = slot()
                    load(s, 0, 512, rows(A["sg_ln_g_2"][j].rearrange("g d -> (g d)")))
                    load(s, 512, 1024, rows(A["sg_ln_b_2"][j].rearrange("g d -> (g d)")))
                    s = slot()
                    lo, hi = CONST_AT["rw_masks"][0], sum(CONST_AT["sg_mask"])
                    load(s, 0, hi - lo, A["consts"][:, lo:hi])
                    load_linear(A["ab_w_out_2"][j])
                else:
                    load_linear(A["mla_w_in_2"][j])
                    s = slot()
                    load(s, 0, 256, rows(A["mla_q_norm_2"][j]))
                    load(s, 256, 512, rows(A["mla_kv_norm_2"][j]))
                    lo = CONST_AT["rope2_cos"][0]
                    load(s, 512, 576, A["consts"][:, lo:lo + 64])
                    load_linear(A["mla_wq_b_2"][j])
                    load_linear(A["mla_wkv_b_2"][j])
                    load_linear(A["mla_w_out_2"][j])
                load_ln(A["ln1_g_2"][layer], A["ln1_b_2"][layer])
                if layer == 0:
                    load(slot(), 0, SLOT, A["mem_2"][0].rearrange("(t p) d -> p t d", p=P))
                load_linear(A["xa_wq_2"][layer])
                load_linear(A["xa_wkv_2"][layer])
                load_linear(A["xa_wo_2"][layer])
                load_ln(A["ln2_g_2"][layer], A["ln2_b_2"][layer])
                load_moe(layer)
                load_ln(A["ln3_g_2"][layer], A["ln3_b_2"][layer])

            sp.wait_ge(ln_done, NT * LAYER_NORMS)
            sp.dma_start(out[0].rearrange("(t p) d -> p t d", p=P), x[:, :, :]).then_inc(out_written, 16)
            sp.wait_ge(out_written, 16)

        @block.tensor
        def _(pe):
            full = [Tally(s) for s in slot_full]
            place = [0]
            t_proj = Tally(proj_done, ahead=2)
            t_tr = Tally(tr_done, ahead=2)
            t_ln = Tally(ln_done)
            t_rope = Tally(rope_done)
            t_logit_free = Tally(logit_free, ahead=2)
            t_p, t_pt = Tally(p_done), Tally(pt_done)
            t_pv = Tally(pv_done, ahead=2)
            t_dots = Tally(dots_done, ahead=2)
            t_h = Tally(h_done)
            t_gu_free = Tally(h_done, ahead=2)
            t_y = Tally(y_added)
            t_selected, t_out = Tally(selected), Tally(pair_out)
            t_gm = Tally(gm_done, ahead=2)
            t_vec, t_act = Tally(vec_for_pe), Tally(act_for_pe)
            tr_items = [0]
            lin_items = [0]
            logit_items = [0]

            def slot(loads=1):
                s = place[0] % RING
                place[0] += 1
                pe.wait_ge(slot_full[s], full[s].next(16 * loads))
                return s

            def hold(loads):
                full[place[0] % RING].skip(16 * loads)
                place[0] += 1

            def mm(o, lhsT, rhs, start=True, stop=True):
                return nc.tensor.matmul(o, lhsT, rhs, start=start, stop=stop)

            def output_linear(srcT, free_slots=0):
                w = []
                for t in range(NT):
                    for c in range(2):
                        for half in range(2):
                            if t == 0:
                                w.append(ring[:, slot(), :].rearrange("p (k n) -> p k n", k=4))
                            for k in range(4):
                                last = mm(lin[:, 2 * t + c, :], srcT[:, 4 * half + k, t * P:(t + 1) * P], w[2 * c + half][:, k, :],
                                          start=half + k == 0, stop=half == 1 and k == 3)
                                if free_slots:
                                    last.then_inc(slots_used, 1)
                                    free_slots -= 1
                            if t == NT - 1:
                                last.then_inc(slots_used, 1)
                    if t == 0:
                        last.then_inc(pe_for_vec, 1)

            def linear(srcT, K, N):
                kt = K // P
                per = min(4, kt)
                for _, n in chunks_of(N):
                    pair = 2 * (lin_items[0] % 2)
                    lin_items[0] += 1
                    if t_proj.due():
                        pe.wait_ge(proj_done, t_proj.value())
                    for k0 in range(0, kt, per):
                        s = slot()
                        w = ring[:, s, 0:per * n].rearrange("p (k n) -> p k n", k=per)
                        for t in range(NT):
                            for k in range(per):
                                last = mm(lin[:, pair + t, 0:n], srcT[:, k0 + k, t * P:(t + 1) * P], w[:, k, :],
                                          start=k0 + k == 0, stop=k0 + k == kt - 1)
                        last.then_inc(slots_used, 1)

            def transposes(pieces, free_slots=0):
                b = tr_items[0] % 2
                tr_items[0] += 1
                if t_tr.due():
                    pe.wait_ge(tr_done, t_tr.value())
                for j, src in enumerate(pieces):
                    ins = nc.tensor.transpose(trp[0:src.free_size(), b, j * P:(j + 1) * P], src, ident[:, :])
                    if j == len(pieces) - 1:
                        ins.then_inc(tr_full, 1)
                    elif free_slots:
                        ins.then_inc(slots_used, 1)
                        free_slots -= 1
                assert not free_slots

            def rows_to_columns(src, ready, free_slots=1):
                for t in range(NT):
                    pe.wait_ge(ln_done, ready.next())
                    for b in range(0, KD, 4):
                        last = t == NT - 1 and b == 0
                        transposes([src(t, b + j) for j in range(4)], free_slots if last else 0)

            def await_transposes():
                pe.wait_ge(tr_done, tr_items[0])

            def scores(parts):
                for o in parts:
                    b = logit_items[0] % 2
                    logit_items[0] += 1
                    if t_logit_free.due():
                        pe.wait_ge(logit_free, t_logit_free.value())
                    for t in range(NT):
                        for n, (qT, kT) in enumerate(o):
                            last = mm(sco[:, b, t * SEQ:(t + 1) * SEQ], qT[:, t * P:(t + 1) * P], kT,
                                      start=n == 0, stop=n == len(o) - 1)
                    last.then_inc(logit_full, 1)

            def attend(units):
                def values(h):
                    pe.wait_ge(pt_done, t_pt.next())
                    for blk, lo, width, v in units[h][1]:
                        if lo == 0:
                            if t_pv.due():
                                pe.wait_ge(pv_done, t_pv.value())
                        for k in range(NT):
                            last = mm(lin[lo:lo + width, blk % 2, 0:SEQ], v[k], PT[:, h % 2, k, :],
                                      start=k == 0, stop=k == NT - 1)
                        if lo + width == P:
                            last.then_inc(pv_full, 1)

                for parts, _ in units[:2]:
                    scores(parts)
                for h in range(len(units)):
                    pe.wait_ge(p_done, t_p.next())
                    for t in range(NT):
                        for k in range(NT):
                            last = nc.tensor.transpose(trp[:, h % 2, k * SEQ + t * P:k * SEQ + (t + 1) * P],
                                                       Pn[:, h % 2, t, k * P:(k + 1) * P], ident[:, :])
                    last.then_inc(pt_full, 1)
                    if h + 2 < len(units):
                        scores(units[h + 2][0])
                    if h > 0:
                        values(h - 1)
                values(len(units) - 1)

            def first_block_units(kind, proj):
                def qk(qb, kb, odd):
                    r = slice(64 * odd, 64 * odd + 64)
                    return [(qkT[r, qb, :], qkT[r, kb, :])]

                def piece(j, v):
                    return (j // 2, 64 * (j % 2), 64, v)
                units = []
                if kind == 1:
                    for h in range(4):
                        parts = [qk((4 * g + h) // 2, 6 + (4 * g + h) // 2, h % 2) for g in range(3)]
                        units.append((parts, [piece(3 * h + j, [proj[:, k, 1536 + 64 * (3 * h + j):1600 + 64 * (3 * h + j)] for k in range(NT)])
                                              for j in range(3)]))
                else:
                    for h in range(HEADS):
                        units.append(([qk(h // 2, 6 + h // 2, h % 2)],
                                      [piece(h, [proj[:, k, 1536 + 64 * h:1600 + 64 * h] for k in range(NT)])]))
                mem_units = [([qk(17 + h // 2, 19 + h // 2, h % 2)],
                              [piece(12 + h, [mkv[:, k, 256 + 64 * h:320 + 64 * h] for k in range(NT)])])
                             for h in range(MEM_HEADS)]
                return units, mem_units

            def ffn():
                units = D_FF // (2 * P)
                y_of = lambda t, n: lin[:, 2 * t + n, :]

                def unit(u, start, stop):
                    gate, up = slot(), slot()
                    for f in range(2):
                        if t_gu_free.due():
                            pe.wait_ge(h_done, t_gu_free.value())
                        for s, lo in ((gate, 0), (up, SEQ)):
                            w = ring[:, s, :].rearrange("p (k n) -> p k n", k=KD)
                            for k in range(KD):
                                last = mm(sco[:, f, lo:lo + SEQ], w[:, k, f * P:(f + 1) * P], xT[:, k, :],
                                          start=k == 0, stop=k == KD - 1)
                            if f == 1:
                                last.then_inc(slots_used, 1)
                        if f == 0:
                            last.then_inc(gu_full, 1)
                    s = slot()
                    w = ring[:, s, :].rearrange("p (k n) -> p k n", k=2)

                    def product(f, t, n):
                        return mm(y_of(t, n), hT[:, u % 2, f, t * P:(t + 1) * P], w[:, f, n * 512:(n + 1) * 512],
                                  start=start and f == 0, stop=stop and f == 1)
                    pe.wait_ge(h_done, t_h.next())
                    if not stop:
                        for t in range(NT):
                            for n in range(2):
                                product(0, t, n)
                    pe.wait_ge(h_done, t_h.next())
                    for t in range(NT):
                        for n in range(2):
                            if stop:
                                product(0, t, n)
                            last = product(1, t, n)
                        if stop and t == 0:
                            last.then_inc(pe_for_vec, 1)
                    last.then_inc(slots_used, 1)

                for u in range(units - units // 4 * 4):
                    unit(u, u == 0, False)
                per = {t_gu_free: 8, t_h: 8}
                for s in range(RING):
                    per[full[s]] = 16
                with rounds(pe, units // 4 - 1, per) as i:
                    for u in range(4):
                        unit(u + units % 4, False, False)
                place[0] += (units // 4 - 2) * RING
                for u in range(4):
                    unit(u + units % 4, False, u == 3)

            def linear_columns(srcT, chunks, free_slots=0):
                for _ in range(chunks):
                    pair = 2 * (lin_items[0] % 2)
                    lin_items[0] += 1
                    if t_proj.due():
                        pe.wait_ge(proj_done, t_proj.value())
                    w = []
                    for _ in range(2):
                        w.append(ring[:, slot(), :].rearrange("p (k n) -> p k n", k=4))
                    for blk in range(4):
                        o = lin[:, pair + blk // 2, blk % 2 * SEQ:(blk % 2 + 1) * SEQ]
                        for k in range(KD):
                            last = mm(o, w[k // 4][:, k % 4, blk * P:(blk + 1) * P], srcT[:, k, :], start=k == 0, stop=k == KD - 1)
                            if free_slots:
                                last.then_inc(slots_used, 1)
                                free_slots -= 1
                            if blk == 3 and k % 4 == 3:
                                last.then_inc(slots_used, 1)

            def mixer_ab():
                linear(xT, D, AB_IN)
                for n in RW_SLOTS[:3]:
                    hold(n)
                lora = slot(RW_SLOTS[3])
                hold(RW_SLOTS[4])
                const = slot(RW_SLOTS[5])
                strict, upto = ring[:, const, 0:P], ring[:, const, P:2 * P]
                chunk_of = ring[:, const, 10 * P:10 * P + 2]
                pe.wait_ge(vec_for_pe, t_vec.next())
                transposes([ring[:, lora, 1024 + g * P:1024 + (g + 1) * P] for g in range(SG_GROUPS)])
                await_transposes()
                pe.wait_ge(vec_for_pe, t_vec.next())
                for t in range(NT):
                    for g in range(SG_GROUPS):
                        last = mm(lin[:, t, g * P:(g + 1) * P], wmT[:, g, :], p_ab[:, t, 2304 + g * P:2304 + (g + 1) * P])
                last.then_inc(pe_for_vec, 1)
                for t in range(NT):
                    pe.wait_ge(act_for_pe, t_act.next())
                    transposes([p_ab[:, t, 1536:1664], p_ab[:, t, 1664:1792]])
                    await_transposes()
                    if t == 0:
                        pe.wait_ge(vec_for_pe, t_vec.next())
                    mm(lin[:, 0, :], loraT[0:64, 0, :], ring[0:64, lora, 0:512])
                    mm(lin[:, 1, :], loraT[64:128, 0, :], ring[64:128, lora, 0:512])
                    mm(lin[:, 2, :], loraT[:, 1, :], ring[:, lora, 512:1024]).then_inc(pe_for_vec, 1)
                    pe.wait_ge(vec_for_pe, t_vec.next())
                    mm(lin[:, 3, :], upto, rw_lw)
                    mm(lin[:, 2, :], strict, rw_lw)
                    for pair in range(4):
                        last = mm(sco[:, 0, 2 * pair:2 * pair + 2], rw_lw[:, pair * P:(pair + 1) * P], chunk_of)
                    last.then_inc(pe_for_act, 1)
                    pe.wait_ge(vec_for_pe, t_vec.next())
                    for pair in range(4):
                        transposes([v[:, pair * P:(pair + 1) * P] for v in (rw_kk, rw_r, rw_b, rw_k)])
                    await_transposes()
                    for h in range(RW_HEADS):
                        r = slice(64 * (h % 2), 64 * (h % 2) + 64)
                        if t_gm.due():
                            pe.wait_ge(gm_done, t_gm.value())
                        queries = rwT[r, h // 2, 0:2, :].rearrange("p a b -> p (a b)")
                        mm(sco[:, h % 2, 0:2 * P], rwT[r, h // 2, 2, :], queries)
                        mm(sco[:, h % 2, 2 * P:4 * P], rwT[r, h // 2, 3, :], queries).then_inc(gm_full, 1)
                    for level in range(6):
                        pe.wait_ge(vec_for_pe, t_vec.next())
                        for h in range(RW_HEADS):
                            last = mm(lin[:, h // 4, h % 4 * P:(h % 4 + 1) * P], rw_BT[:, h, :], rw_X[:, h, :])
                        last.then_inc(pe_for_act, 1)
                        pe.wait_ge(act_for_pe, t_act.next())
                        for h in range(RW_HEADS):
                            last = mm(lin[:, 2 + h // 4, h % 4 * P:(h % 4 + 1) * P], rw_T1[:, h, :], rw_XT[:, h, :])
                        if level < 5:
                            for h in range(RW_HEADS):
                                last = mm(sco[:, h // 4, h % 4 * P:(h % 4 + 1) * P], rw_XT[:, h, :], rw_T1[:, h, :])
                        last.then_inc(pe_for_vec, 1)
                    for half in range(2):
                        rs = slice(64 * half, 64 * half + 64)
                        pe.wait_ge(vec_for_pe, t_vec.next())
                        v = p_ab[rs, t, 1024:1536]
                        for h in range(RW_HEADS):
                            r, c = slice(64 * (h % 2), 64 * (h % 2) + 64), slice(64 * h, 64 * h + 64)
                            mm(lin[rs, h % 2, c], rwT[r, h // 2, 0, rs], rw_state[r, h // 2, :])
                        for h in range(RW_HEADS):
                            c = slice(64 * h, 64 * h + 64)
                            last = mm(lin[rs, 2, c], rw_G[rs, h, 2 * P + 64 * half:2 * P + 64 * half + 64], v[:, c])
                        last.then_inc(pe_for_vec, 1)
                        pe.wait_ge(vec_for_pe, t_vec.next())
                        for h in range(RW_HEADS):
                            c = slice(64 * h, 64 * h + 64)
                            last = mm(lin[rs, 3, c], rw_XT[rs, h, rs], rw_U[rs, c])
                        last.then_inc(pe_for_act, 1)
                        for h in range(RW_HEADS):
                            r, c = slice(64 * (h % 2), 64 * (h % 2) + 64), slice(64 * h, 64 * h + 64)
                            mm(sco[rs, h % 2, c], rwT[r, h // 2, 1, rs], rw_state[r, h // 2, :])
                        pe.wait_ge(act_for_pe, t_act.next())
                        for h in range(RW_HEADS):
                            c = slice(64 * h, 64 * h + 64)
                            mm(lin[rs, 2, c], rw_G[rs, h, P + 64 * half:P + 64 * half + 64], rw_SA[rs, c], stop=False)
                            mm(lin[rs, 2, c], rw_G[rs, h, 3 * P + 64 * half:3 * P + 64 * half + 64], v[:, c], start=False)
                        for h in range(RW_HEADS):
                            r, c = slice(64 * (h % 2), 64 * (h % 2) + 64), slice(64 * h, 64 * h + 64)
                            o = lin[r, 0, 64 * (h // 2):64 * (h // 2) + 64]
                            mm(o, rw_b[rs, c], rw_SA[rs, c], stop=False)
                            last = mm(o, rw_k[rs, c], v[:, c], start=False)
                        last.then_inc(pe_for_vec, 1)
                    pe.wait_ge(vec_for_pe, t_vec.next())
                column = lambda b: slice(b * P, (b + 1) * P) if b < 4 else slice(2304 + (b - 4) * P, 2304 + (b - 3) * P)
                pe.wait_ge(vec_for_pe, t_vec.next())
                for t in range(NT):
                    for b in range(0, KD, 4):
                        transposes([p_ab[:, t, column(b + j)] for j in range(4)], 3 if t == NT - 1 else 0)
                await_transposes()
                output_linear(mixT)

            def mla():
                linear(xT, D, MLA_IN)
                hold(3)
                pe.wait_ge(vec_for_pe, t_vec.next())
                for b0 in range(0, 4, 2):
                    transposes([mla_p[:, t, (b0 + b) * P:(b0 + b + 1) * P] for b in range(2) for t in range(NT)], 1 if b0 == 0 else 0)
                await_transposes()
                linear(latentT[:, 0:2, :], 256, MLA_HEADS * 96)
                linear(latentT[:, 2:4, :], 256, MLA_HEADS * P)
                pe.wait_ge(vec_for_pe, t_vec.next())
                q_src = lambda t, b: mla_qn[:, t, 2 * b:2 * b + 2, :].rearrange("p h d -> p (h d)")
                k_src = lambda t, b: mla_kn[t][:, 2 * b:2 * b + 2, :].rearrange("p h d -> p (h d)")
                for src in (q_src, k_src):
                    for b0 in range(0, 8, 2):
                        transposes([src(t, b0 + b) for b in range(2) for t in range(NT)])
                transposes([mla_kpe[:, t, :, :].rearrange("p a b -> p (a b)") for t in range(NT)])
                for b0 in range(0, 8, 2):
                    transposes([mla_qpe[:, t, 2 * (b0 + b):2 * (b0 + b) + 2, :, :].rearrange("p h a b -> p (h a b)")
                                for b in range(2) for t in range(NT)])
                await_transposes()
                units = []
                for h in range(MLA_HEADS):
                    r, b = slice(64 * (h % 2), 64 * (h % 2) + 64), h // 2
                    qpe = mlaT[r, 17 + b, :] if b < 4 else mlaT_more[r, b - 4, :]
                    units.append(([[(mlaT[r, b, :], mlaT[r, 8 + b, :]), (qpe, mlaT[r, 16, :])]],
                                  [(b, 64 * (h % 2), 64, [mla_kv[:, k, h, 64:128] for k in range(NT)])]))
                attend(units)
                pe.wait_ge(pv_done, t_pv.n + 2)
                output_linear(mixT)

            def memory_attention(free_slots):
                linear_columns(xT, 2, free_slots)
                linear_columns(memT, 2)
                linear(memT, D, D)
                pe.wait_ge(proj_done, t_proj.n + 2)
                attend([([[(xa_qT[:, 2 * h + b, :], xa_kT[:, 2 * h + b, :]) for b in range(2)]],
                         [(2 * h + b, 0, P, [xa_v[:, k, 256 * h + P * b:256 * h + P * b + P] for k in range(NT)]) for b in range(2)])
                        for h in range(XA_HEADS)])
                pe.wait_ge(pv_done, t_pv.n + 2)
                output_linear(mixT)

            def moe(layer):
                s = slot(5)
                w = ring[:, s, 0:KD * 36].rearrange("p (k n) -> p k n", k=KD)
                for t in range(NT):
                    o = sco[:, 0, t * 64:t * 64 + 36]
                    for k in range(KD):
                        mm(o, xT[:, k, t * P:(t + 1) * P], w[:, k, :], start=k == 0, stop=False)
                    last = mm(o, ring[:, s, router_const("one")], ring[:, s, 512:548], start=False)
                last.then_inc(pe_for_vec, 1)
                pe.wait_ge(vec_for_pe, t_vec.next())
                earlier, every = ring[:, s, router_const("earlier")], ring[:, s, router_const("all")]
                mm(sco[:, 1, 0:COLUMNS], earlier, chosen[:, 0, :])
                mm(sco[:, 1, 64:64 + COLUMNS], every, chosen[:, 0, :], stop=False)
                mm(sco[:, 1, 64:64 + COLUMNS], earlier, chosen[:, 1, :], start=False)
                mm(sco[:, 1, 128:128 + COLUMNS], every, chosen[:, 0, :], stop=False)
                mm(sco[:, 1, 128:128 + COLUMNS], every, chosen[:, 1, :], start=False).then_inc(slots_used, 1)

                banks = [tr_items[0] % 2, 1 - tr_items[0] % 2]
                t_columns = Tally(tr_done)
                t_columns.skip(tr_items[0])
                expert_rows = [slice(0, PLACES), slice(PLACES, 2 * PLACES)]

                def gather():
                    pe.wait_ge(selected, t_selected.next())
                    for half in range(2):
                        for j in range(4):
                            b = 4 * half + j
                            for t in range(NT):
                                last = mm(trp[:, banks[half], j * P:(j + 1) * P], x[:, t, b * P:(b + 1) * P], gathering[:, t, :],
                                          start=t == 0, stop=t == NT - 1)
                        last.then_inc(tr_full, 1)

                def combine():
                    pe.wait_ge(pair_out, t_out.next())
                    for t in range(NT):
                        for n in range(2):
                            last = mm(lin[:, 2 * (1 - t) + n, :], spreadT[:, t, :], pair_y[:, n * 512:(n + 1) * 512])
                        last.then_inc(combined, 1)

                gather()
                per = {t_selected: 1, t_columns: 4, t_h: 1, t_y: 2, t_out: 1}
                for s in range(RING):
                    per[full[s]] = 16
                t_y.skip(NT)
                with rounds(pe, PAIRS, per):
                    pe.wait_ge(tr_done, t_columns.next(2))
                    for gate_or_up in range(2):
                        for half in range(2):
                            both = [ring[:, slot(), :].rearrange("p (k n) -> p k n", k=4) for _ in range(2)]
                            for k in range(4):
                                for r, wk in zip(expert_rows, both):
                                    last = mm(sco[r, gate_or_up, :], rowsT[:, 4 * half + k, r], wk[:, k, :],
                                              start=half + k == 0, stop=half == 1 and k == 3)
                                    if k == 3:
                                        last.then_inc(slots_used, 1)
                    combine()
                    pe.wait_ge(h_done, t_h.next())
                    for f in range(4):
                        last = nc.tensor.transpose(trp[:, banks[0], f * P:(f + 1) * P], pair_h[:, f * P:(f + 1) * P], ident[:, :])
                    last.then_inc(tr_full, 1)
                    for t in range(NT):
                        last = nc.tensor.transpose(trp[:, banks[1], t * P:(t + 1) * P], gated[:, t, :], ident[:, :])
                    last.then_inc(tr_full, 1)
                    pe.wait_ge(y_added, t_y.next(2))
                    pe.wait_ge(tr_done, t_columns.next(2))
                    for half in range(2):
                        both = [ring[:, slot(), :].rearrange("p (k n) -> p k n", k=2) for _ in range(2)]
                        for f in range(2):
                            for n in range(2):
                                for r, wd in zip(expert_rows, both):
                                    last = mm(lin[r, n, :], pair_hT[:, 2 * half + f, r], wd[:, f, n * 512:(n + 1) * 512],
                                              start=half + f == 0, stop=half + f == 2)
                                    if f + n == 2:
                                        last.then_inc(slots_used, 1)
                                    elif half + f + n == 0 and r == expert_rows[0]:
                                        last.then_inc(selection_used, 1)
                        if half == 0:
                            gather()
                place[0] += (PAIRS - 1) * RING
                combine()
                t_y.skip(NT)
                tr_items[0] += 4 * PAIRS + 2
                t_tr.skip(4 * PAIRS + 2)

                pe.wait_ge(overflow_known, layer + 1)
                overflow = pe.value_load(ints[0:1, 16 + layer:17 + layer], min_val=0, max_val=1)
                t_loaded, t_hidden, t_added = Tally(rest_loaded[layer]), Tally(rest_hidden[layer]), Tally(rest_added[layer])
                with pe.If(overflow):
                    pe.wait_ge(y_added, t_y.value())
                    with rounds(pe, EXPERTS, {t_loaded: 96, t_hidden: 4, t_added: 1}):
                        pe.wait_ge(rest_loaded[layer], t_loaded.next(96))
                        for f in range(4):
                            for slots, lo in (((0, 1), 0), ((2, 3), SEQ)):
                                for k in range(KD):
                                    wk = ring[:, slots[k // 4], :].rearrange("p (k n) -> p k n", k=4)
                                    last = mm(sco[:, 0, lo:lo + SEQ], wk[:, k % 4, f * P:(f + 1) * P], xT[:, k, :],
                                              start=k == 0, stop=k == KD - 1)
                            last.then_inc(rest_gate_up[layer], 1)
                            pe.wait_ge(rest_hidden[layer], t_hidden.next())
                        pe.wait_ge(rest_added[layer], t_added.next())
                        for f in range(4):
                            wd = ring[:, 4 + f // 2, :].rearrange("p (k n) -> p k n", k=2)
                            for t in range(NT):
                                for n in range(2):
                                    last = mm(lin[:, 2 * t + n, :], hT[:, 0, f, t * P:(t + 1) * P], wd[:, f % 2, n * 512:(n + 1) * 512],
                                              start=f == 0, stop=f == 3)
                        last.then_inc(rest_output[layer], 1)

            pe.wait_ge(x_loaded, 16 * 2)
            for t in range(NT):
                for b in range(0, KD, 4):
                    transposes([x[:, t, (b + j) * P:(b + j + 1) * P] for j in range(4)])
            for layer in range(FIRST_LAYERS):
                kind = kind_of(layer)
                proj = projA if kind == 0 else projBC
                width = WIDTH_A if kind == 0 else WIDTH_BC
                await_transposes()
                linear(xT, D, width)
                if layer == 0:
                    hold(2)
                    rows_to_columns(lambda t, b: memrows[:, t, b * P:(b + 1) * P], t_ln)
                    await_transposes()
                linear(memT, D, 512)
                pe.wait_ge(proj_done, t_proj.n + 2)
                qm = width - MEM_HEADS * DH
                for t in range(1):
                    transposes([proj[:, t2, qm + b * P:qm + (b + 1) * P] for b in range(2) for t2 in range(NT)])
                    transposes([mkv[:, t2, b * P:(b + 1) * P] for b in range(2) for t2 in range(NT)])
                if kind < 2:
                    hold(2 if kind == 0 else 1)
                pe.wait_ge(rope_done, t_rope.next())
                for b0 in range(0, 12, 2):
                    transposes([proj[:, t, (b0 + b) * P:(b0 + b + 1) * P] for b in range(2) for t in range(NT)],
                               1 if b0 == 0 and kind == 0 else 0)
                if kind == 0:
                    for b0 in range(0, 4, 2):
                        transposes([proj[:, t, 2304 + (b0 + b) * P:2304 + (b0 + b + 1) * P] for b in range(2) for t in range(NT)])
                    transposes([ki2[:, t, :, :].rearrange("p a d -> p (a d)") for t in range(NT)])
                await_transposes()
                if kind == 0:
                    for t in range(NT):
                        for h in range(0, IDX_HEADS, 4):
                            for step in range(2):
                                for o in range(2):
                                    if step == 0:
                                        if t_dots.due():
                                            pe.wait_ge(dots_done, t_dots.value())
                                    r = slice(64 * o, 64 * o + 64)
                                    last = mm(sco[:, o, step * SEQ:(step + 1) * SEQ], qkT[r, 12 + h // 2 + step, t * P:(t + 1) * P], qkT[r, 16, :])
                                    if step == 1:
                                        last.then_inc(dots_full, 1)
                    pe.wait_ge(dots_done, t_dots.n + 2)
                units, mem_units = first_block_units(kind, proj)
                attend(mem_units)
                attend(units)
                pe.wait_ge(pv_done, t_pv.n + 2)
                output_linear(mixT, 1 if kind == 1 else 0)
                hold(2)
                rows_to_columns(lambda t, b: x[:, t, b * P:(b + 1) * P], t_ln)
                await_transposes()
                ffn()
                hold(2)
                rows_to_columns(lambda t, b: x[:, t, b * P:(b + 1) * P], t_ln)
            for layer in range(SECOND_LAYERS):
                await_transposes()
                if layer % 2 == 0:
                    mixer_ab()
                else:
                    mla()
                hold(2)
                rows_to_columns(lambda t, b: x[:, t, b * P:(b + 1) * P], t_ln)
                if layer == 0:
                    s = slot()
                    for t in range(NT):
                        for b in range(0, KD, 4):
                            transposes([ring[:, s, t * D + (b + j) * P:t * D + (b + j + 1) * P] for j in range(4)])
                await_transposes()
                memory_attention(1 if layer == 0 else 0)
                hold(2)
                rows_to_columns(lambda t, b: x[:, t, b * P:(b + 1) * P], t_ln)
                await_transposes()
                moe(layer)
                hold(2)
                if layer + 1 < SECOND_LAYERS:
                    rows_to_columns(lambda t, b: x[:, t, b * P:(b + 1) * P], t_ln)

        @block.scalar
        def _(act):
            used = Tally(slots_used)
            t_tr, t_smax, t_pt, t_pv = Tally(tr_full), Tally(smax_done), Tally(pt_full), Tally(pv_full)
            t_dots, t_added = Tally(dots_full), Tally(score_added, ahead=2)
            t_gu, t_h = Tally(gu_full), Tally(h_done, ahead=2)
            t_vec, t_pe = Tally(vec_for_act), Tally(pe_for_act)
            tr_items = [0]
            lin_items = [0]
            proj_items = [0]

            def evacuate_linear(K, N, dst):
                for lo, n in chunks_of(N):
                    act.wait_ge(slots_used, used.next(max(1, K // 512)))
                    pair = 2 * (lin_items[0] % 2)
                    lin_items[0] += 1
                    proj_items[0] += 1
                    nc.scalar.activation(dst[:, :, lo:lo + n], lin[:, pair:pair + 2, 0:n],
                                         ACT.Copy).then_inc(proj_done, 1)

            def evacuate_transposes(dst, rows=P):
                b = tr_items[0] % 2
                tr_items[0] += 1
                act.wait_ge(tr_full, t_tr.next())
                shape = dst.shape
                n = shape[1] * shape[2]
                nc.scalar.activation(dst, trp[0:rows, b, 0:n].rearrange("p (a b) -> p a b", a=shape[1]),
                                     ACT.Copy).then_inc(tr_done, 1)

            def columns(dstT):
                for t in range(NT):
                    for b in range(0, KD, 4):
                        evacuate_transposes(dstT[:, b:b + 4, t * P:(t + 1) * P])

            def attend(n_units, groups, blocks_after, first_block):
                S = S1 if groups == 1 else S3

                def exps(h):
                    act.wait_ge(smax_done, t_smax.next())
                    for t in range(NT):
                        s = S[:, h % 2, t, :, :].rearrange("p g k -> p (g k)")
                        last = nc.scalar.activation(s, s, ACT.Exp, bias=negmax[:, h % 2, t:t + 1],
                                                    accum_out=rowsum[:, h % 2, t:t + 1])
                    last.then_inc(exp_done, 1)
                blocks = [first_block]

                def outputs(h):
                    while blocks[0] < blocks_after(h):
                        act.wait_ge(pv_full, t_pv.next())
                        nc.scalar.activation(mixT[:, blocks[0], :], lin[:, blocks[0] % 2, 0:SEQ], ACT.Copy).then_inc(pv_done, 1)
                        blocks[0] += 1

                exps(0)
                for h in range(n_units):
                    if h + 1 < n_units:
                        exps(h + 1)
                    act.wait_ge(pt_full, t_pt.next())
                    nc.scalar.activation(PT[:, h % 2, :, :].rearrange("p k q -> p (k q)"), trp[:, h % 2, :],
                                         ACT.Copy).then_inc(pt_done, 1)
                    if h > 0:
                        outputs(h - 1)
                outputs(n_units - 1)

            def ffn():
                units = D_FF // (2 * P)

                def unit():
                    for f in range(2):
                        if f == 0:
                            act.wait_ge(gu_full, t_gu.next())
                        else:
                            act.wait_ge(slots_used, used.next(2))
                        if t_h.due():
                            act.wait_ge(h_done, t_h.value())
                        nc.scalar.activation(silu_g[:, f, :], sco[:, f, 0:SEQ], ACT.Silu).then_inc(silu_done, 1)
                    used.skip(1)
                unit()
                with rounds(act, units - 1, {t_gu: 1, used: 3, t_h: 2}):
                    unit()

            def mixer_ab():
                evacuate_linear(D, AB_IN, p_ab)
                used.skip(len(RW_SLOTS))
                act.wait_ge(proj_done, proj_items[0])
                act.dma_start(shifted[1:P, :, :], p_ab[0:P - 1, :, 0:RW_SHIFT]).then_inc(shift_loaded, 16)
                act.dma_start(shifted[0:1, 1, :], p_ab[P - 1:P, 0, 0:RW_SHIFT]).then_inc(shift_loaded, 16)
                gated = p_ab[:, :, RW_SHIFT:AB_IN]
                nc.scalar.activation(gated, gated, ACT.Gelu_apprx_tanh).then_inc(act_for_vec, 1)
                evacuate_transposes(wmT)
                for t in range(NT):
                    if t == 0:
                        act.wait_ge(vec_for_act, t_vec.next())
                    nc.scalar.activation(p_ab[:, t, 1536:1600], p_ab[:, t, 1536:1600], ACT.Tanh)
                    nc.scalar.activation(p_ab[:, t, 1664:1792], p_ab[:, t, 1664:1792], ACT.Sigmoid).then_inc(act_for_pe, 1)
                    evacuate_transposes(loraT)
                    act.wait_ge(vec_for_act, t_vec.next())
                    nc.scalar.activation(rw_tmp, rw_tmp, ACT.Sigmoid)
                    nc.scalar.activation(rw_a, rw_a, ACT.Sigmoid).then_inc(act_for_vec, 1)
                    act.wait_ge(pe_for_act, t_pe.next())
                    nc.scalar.activation(rw_r, lin[:, 3, :], ACT.Exp)
                    nc.scalar.activation(rw_pinv, lin[:, 3, :], ACT.Exp, scale=-1.0)
                    nc.scalar.activation(rw_pexc, lin[:, 2, :], ACT.Exp)
                    nc.scalar.activation(rw_decay.rearrange("p a b -> p (a b)"), sco[:, 0, 0:8], ACT.Exp).then_inc(act_for_vec, 1)
                    for pair in range(4):
                        evacuate_transposes(rwT[:, pair, :, :])
                    for _ in range(6):
                        act.wait_ge(pe_for_act, t_pe.next())
                        nc.scalar.activation(rw_T1.rearrange("p h k -> p (h k)"), lin[:, 0:2, :].rearrange("p a b -> p (a b)"),
                                             ACT.Copy).then_inc(act_for_pe, 1)
                    for half in range(2):
                        rs = slice(64 * half, 64 * half + 64)
                        act.wait_ge(pe_for_act, t_pe.next())
                        nc.scalar.activation(rw_SA[rs, :], lin[rs, 3, :], ACT.Copy, scale=-1.0).then_inc(act_for_pe, 1)
                columns(mixT)

            def mla():
                evacuate_linear(D, MLA_IN, mla_p)
                used.skip(1)
                for b in range(0, 4, 2):
                    evacuate_transposes(latentT[:, b:b + 2, :])
                evacuate_linear(256, MLA_HEADS * 96, mla_q.rearrange("p t h d -> p t (h d)"))
                evacuate_linear(256, MLA_HEADS * P, mla_kv.rearrange("p t h d -> p t (h d)"))
                for b in range(0, 16, 2):
                    evacuate_transposes(mlaT[:, b:b + 2, :])
                evacuate_transposes(mlaT[:, 16:17, :])
                for b in range(0, 4, 2):
                    evacuate_transposes(mlaT[:, 17 + b:19 + b, :])
                for b in range(0, 4, 2):
                    evacuate_transposes(mlaT_more[:, b:b + 2, :])
                attend(MLA_HEADS, 1, lambda h: (h + 1) // 2, 0)

            def memory_attention():
                for dst in (xa_qT, xa_kT):
                    for c in range(2):
                        act.wait_ge(slots_used, used.next(2))
                        pair = 2 * (lin_items[0] % 2)
                        lin_items[0] += 1
                        proj_items[0] += 1
                        nc.scalar.activation(dst[:, 4 * c:4 * c + 4, :].rearrange("p a b -> p (a b)"),
                                             lin[:, pair:pair + 2, :].rearrange("p a b -> p (a b)"), ACT.Copy).then_inc(proj_done, 1)
                evacuate_linear(D, D, xa_v)
                attend(XA_HEADS, 1, lambda h: 2 * (h + 1), 0)

            def moe(layer):
                used.skip(1)
                act.wait_ge(vec_for_act, t_vec.next())
                for t in range(NT):
                    nc.scalar.activation(hot[:, t, 0:GROUPS], logits36[:, t, 0:GROUPS], ACT.Exp, bias=router[:, t, 8:9],
                                         accum_out=router[:, t, 9:10])
                    last = nc.scalar.activation(router[:, t, 11:12], router[:, t, 10:11], ACT.Exp)
                last.then_inc(act_for_vec, 1)
                banks = [tr_items[0] % 2, 1 - tr_items[0] % 2]

                def gathered():
                    for half in range(2):
                        act.wait_ge(tr_full, t_tr.next())
                        nc.scalar.activation(rowsT[:, 4 * half:4 * half + 4, :].rearrange("p a b -> p (a b)"), trp[:, banks[half], :],
                                             ACT.Copy).then_inc(tr_done, 1)

                gathered()
                with rounds(act, PAIRS, {t_tr: 4, used: RING}):
                    act.wait_ge(slots_used, used.next(4))
                    nc.scalar.activation(pair_silu, sco[:, 0, :], ACT.Silu).then_inc(silu_done, 1)
                    used.skip(4)
                    act.wait_ge(tr_full, t_tr.next())
                    nc.scalar.activation(pair_hT.rearrange("p a b -> p (a b)"), trp[:, banks[0], :], ACT.Copy).then_inc(tr_done, 1)
                    act.wait_ge(tr_full, t_tr.next())
                    nc.scalar.activation(spreadT.rearrange("p a b -> p (a b)"), trp[:, banks[1], 0:NT * P], ACT.Copy).then_inc(tr_done, 1)
                    gathered()
                    act.wait_ge(slots_used, used.next(4))
                    nc.scalar.activation(pair_y, lin[:, 0:2, :].rearrange("p a b -> p (a b)"), ACT.Copy).then_inc(pair_out, 1)
                tr_items[0] += 4 * PAIRS + 2

                act.wait_ge(overflow_known, layer + 1)
                overflow = act.value_load(ints[0:1, 16 + layer:17 + layer], min_val=0, max_val=1)
                t_gate_up = Tally(rest_gate_up[layer])
                with act.If(overflow):
                    with rounds(act, EXPERTS, {t_gate_up: 4}):
                        for f in range(4):
                            act.wait_ge(rest_gate_up[layer], t_gate_up.next())
                            nc.scalar.activation(silu_g[:, 0, :], sco[:, 0, 0:SEQ], ACT.Silu).then_inc(rest_silu[layer], 1)

            columns(xT)
            for layer in range(FIRST_LAYERS):
                kind = kind_of(layer)
                proj = projA if kind == 0 else projBC
                evacuate_linear(D, WIDTH_A if kind == 0 else WIDTH_BC, proj)
                if layer == 0:
                    used.skip(1)
                    columns(memT)
                    act.wait_ge(vec_for_act, t_vec.next())
                    nc.scalar.activation(small[:, 0:32], small[:, 96:128], ACT.Sin).then_inc(act_for_vec, 1)
                evacuate_linear(D, 512, mkv)
                evacuate_transposes(qkT[:, 17:19, :])
                evacuate_transposes(qkT[:, 19:21, :])
                for b in range(0, 16 if kind == 0 else 12, 2):
                    evacuate_transposes(qkT[:, b:b + 2, :])
                if kind == 0:
                    used.skip(1)
                    evacuate_transposes(qkT[:, 16:17, :])
                    for n in range(NT * IDX_HEADS // 2):
                        act.wait_ge(dots_full, t_dots.next())
                        if t_added.due():
                            act.wait_ge(score_added, t_added.value())
                        nc.scalar.activation(idx_relu[:, n % 2, :, :].rearrange("p o k -> p (o k)"), sco[:, n % 2, :],
                                             ACT.Relu).then_inc(dots_done, 1)
                attend(MEM_HEADS, 1, lambda h: 6 + (h + 1) // 2, 6)
                if kind == 1:
                    attend(4, 3, lambda h: 3 * (h + 1) // 2, 0)
                else:
                    attend(HEADS, 1, lambda h: (h + 1) // 2, 0)
                if kind == 1:
                    used.skip(1)
                used.skip(4 + 1)
                columns(xT)
                ffn()
                used.skip(1)
                columns(xT)
            for layer in range(SECOND_LAYERS):
                if layer % 2 == 0:
                    mixer_ab()
                else:
                    mla()
                used.skip(4 + 1)
                columns(xT)
                if layer == 0:
                    used.skip(1)
                    columns(memT)
                memory_attention()
                used.skip(4 + 1)
                columns(xT)
                moe(layer)
                used.skip(1)
                if layer + 1 < SECOND_LAYERS:
                    columns(xT)

        @block.gpsimd
        def _(pool):
            asked = Tally(root_asked)
            nc.gpsimd.memset(root_in, 1.0)
            nc.gpsimd.memset(root_power, -0.5).then_inc(pool_step, 1)
            pool.wait_ge(pool_step, 1)
            with rounds(pool, ROOTS // 2, {asked: 2}):
                for b in range(2):
                    pool.wait_ge(root_asked, asked.next())
                    nc.gpsimd.tensor_tensor(root_out[:, b, :], root_in[:, b, :], root_power, ALU.pow).then_inc(root_done, 1)

        @block.vector
        def _(dve):
            used = Tally(slots_used)
            t_step = Tally(dve_step)
            t_proj = Tally(proj_done)
            t_act, t_pe = Tally(act_for_vec), Tally(pe_for_vec)
            t_logit, t_logit_free = Tally(logit_full), Tally(logit_free)
            t_exp, t_pt = Tally(exp_done), Tally(pt_full, ahead=2)
            t_dots, t_added = Tally(dots_done), Tally(score_added)
            t_gu, t_silu, t_h = Tally(gu_full), Tally(silu_done), Tally(h_done)
            t_root = Tally(root_done)
            logit_items = [0]
            t_gm, t_gm_done = Tally(gm_full), Tally(gm_done)
            t_y = Tally(y_added)
            t_combined, t_selection = Tally(combined), Tally(selection_used)
            root_items = [0]
            shifts = [0]
            V = nc.vector


            ring_fill = [0] * RING
            place = [0]

            def passed(n, loads=1):
                for _ in range(n):
                    ring_fill[place[0] % RING] += 16 * loads
                    place[0] += 1
                used.skip(n)

            def own_slot(loads):
                s = place[0] % RING
                passed(1, loads)
                dve.wait_ge(slot_full[s], ring_fill[s])
                return s

            def ask_root(v, op, c):
                b, n = root_items[0] % 2, v.shape[1]
                root_items[0] += 1
                V.tensor_scalar(root_in[:, b, 0:n], v, c, None, op).then_inc(root_asked, 1)
                return root_out[:, b, 0:n]

            def rsqrt(v, op, c):
                answer = ask_root(v, op, c)
                dve.wait_ge(root_done, t_root.next())
                return answer

            def normalise(rows, t, s, dst=None):
                dst = rows if dst is None else dst
                for h in range(2):
                    last = V.bn_stats(bn[:, t, h * 6:h * 6 + 6], rows[:, t, h * 512:(h + 1) * 512])
                last.then_inc(dve_step, 1)
                dve.wait_ge(dve_step, t_step.next())
                V.bn_aggr(mean_var[:, t, :], bn[:, t, :]).then_inc(dve_step, 1)
                dve.wait_ge(dve_step, t_step.next())
                rstd = ask_root(mean_var[:, t, 1:2], ALU.add, LN_EPS)
                V.scalar_tensor_tensor(dst[:, t, :], rows[:, t, :], mean_var[:, t, 0:1], ring[:, s, 0:D], ALU.subtract, ALU.mult).then_inc(dve_step, 1)
                dve.wait_ge(dve_step, t_step.next())
                dve.wait_ge(root_done, t_root.next())
                V.scalar_tensor_tensor(dst[:, t, :], dst[:, t, :], rstd, ring[:, s, D:2 * D],
                                       ALU.mult, ALU.add).then_inc(ln_done, 1)

            def add_and_normalise(alpha):
                complete = used.n
                s = own_slot(2)
                for t in range(NT):
                    if t == 0:
                        dve.wait_ge(pe_for_vec, t_pe.next())
                    else:
                        dve.wait_ge(slots_used, complete)
                    V.scalar_tensor_tensor(x[:, t, :], x[:, t, :], alpha, lin[:, 2 * t:2 * t + 2, :].rearrange("p a b -> p (a b)"),
                                           ALU.mult, ALU.add).then_inc(dve_step, 1)
                    dve.wait_ge(dve_step, t_step.next())
                    normalise(x, t, s)

            def rotate(heads, cos, sin, half, scratch=rope_tmp):
                n = heads.shape[1]
                a, b = heads[:, :, 0:half], heads[:, :, half:2 * half]
                c = cos.unsqueeze(1).to_broadcast([P, n, half])
                s = sin.unsqueeze(1).to_broadcast([P, n, half])
                tmp = [scratch[:, j, 0:n * half].rearrange("p (n f) -> p n f", n=n) for j in range(4)]
                V.tensor_tensor(tmp[0], a, c, ALU.mult)
                V.tensor_tensor(tmp[1], b, s, ALU.mult)
                V.tensor_tensor(tmp[2], b, c, ALU.mult)
                V.tensor_tensor(tmp[3], a, s, ALU.mult).then_inc(dve_step, 1)
                dve.wait_ge(dve_step, t_step.next())
                V.tensor_tensor(a, tmp[0], tmp[1], ALU.subtract)
                return V.tensor_tensor(b, tmp[2], tmp[3], ALU.add)

            def attend(n_units, groups, mask_of, scale):
                S = S1 if groups == 1 else S3

                def maxima(h):
                    for g in range(groups):
                        bank = logit_items[0] % 2
                        logit_items[0] += 1
                        dve.wait_ge(logit_full, t_logit.next())
                        src = sco[:, bank, :].rearrange("p (t k) -> p t k", t=NT)
                        mask = mask_of(g)
                        if mask is None:
                            ins = V.tensor_scalar(S[:, h % 2, :, g, :], src, scale, None, ALU.mult)
                        else:
                            ins = V.scalar_tensor_tensor(S[:, h % 2, :, g, :], src, scale, mask, ALU.mult, ALU.add)
                        ins.then_inc(logit_free, 1)
                        dve.wait_ge(logit_free, t_logit_free.next())
                    V.tensor_reduce(negmax[:, h % 2, :], S[:, h % 2, :, :, :].rearrange("p t g k -> p t (g k)"), AX.X, ALU.max,
                                    negate=True).then_inc(smax_done, 1)
                maxima(0)
                for h in range(n_units):
                    if h + 1 < n_units:
                        maxima(h + 1)
                    dve.wait_ge(exp_done, t_exp.next())
                    V.reciprocal(rinv[:, h % 2, :], rowsum[:, h % 2, :]).then_inc(dve_step, 1)
                    dve.wait_ge(dve_step, t_step.next())
                    for g in range(1, groups):
                        V.tensor_tensor(S[:, h % 2, :, 0, :], S[:, h % 2, :, 0, :], S[:, h % 2, :, g, :], ALU.add).then_inc(dve_step, 1)
                        dve.wait_ge(dve_step, t_step.next())
                    if t_pt.due():
                        dve.wait_ge(pt_full, t_pt.value())
                    for t in range(NT):
                        last = V.tensor_scalar(Pn[:, h % 2, t, :], S[:, h % 2, t, 0, :], rinv[:, h % 2, t:t + 1], None, ALU.mult)
                    last.then_inc(p_done, 1)

            def select_keys(proj):
                n = 0
                for t in range(NT):
                    for i, h in enumerate((0, 2, 1, 3, 4, 6, 5, 7)):
                        if i % 2 == 0:
                            dve.wait_ge(dots_done, t_dots.next())
                        prev = causal[:, t, :] if i == 0 else idx_score[:, t, :]
                        ins = V.scalar_tensor_tensor(idx_score[:, t, :], idx_relu[:, n % 2, i % 2, :], proj[:, t, 2816 + h:2817 + h], prev,
                                                     ALU.mult, ALU.add)
                        if i % 2:
                            ins.then_inc(score_added, 1)
                            dve.wait_ge(score_added, t_added.next())
                            n += 1
                        else:
                            ins.then_inc(dve_step, 1)
                            dve.wait_ge(dve_step, t_step.next())
                for t in range(NT):
                    for _ in range(TOPK // 8):
                        V.max(top_score, idx_score[:, t, :]).then_inc(dve_step, 1)
                        dve.wait_ge(dve_step, t_step.next())
                        V.match_replace(idx_score[:, t, :], top_score, idx_score[:, t, :], TAKEN).then_inc(dve_step, 1)
                        dve.wait_ge(dve_step, t_step.next())
                    V.tensor_scalar(dsa_mask[:, t, :], idx_score[:, t, :], TAKEN, 1.0, ALU.is_equal, ALU.subtract).then_inc(dve_step, 1)
                    dve.wait_ge(dve_step, t_step.next())
                    V.scalar_tensor_tensor(dsa_mask[:, t, :], dsa_mask[:, t, :], -MASKED, causal[:, t, :], ALU.mult, ALU.add).then_inc(dve_step, 1)
                    dve.wait_ge(dve_step, t_step.next())

            def ffn():
                units = D_FF // (2 * P)

                def unit(u):
                    for f in range(2):
                        dve.wait_ge(silu_done, t_silu.next())
                        V.tensor_tensor(hT[:, u % 2, f, :], silu_g[:, f, :], sco[:, f, SEQ:2 * SEQ], ALU.mult).then_inc(h_done, 1)
                per = {t_silu: 4}
                unit(0)
                with rounds(dve, (units - 1) // 2, per):
                    unit(1)
                    unit(0)

            def spread(v, n):
                return v.unsqueeze(2).to_broadcast([P, v.shape[1], n])

            def centre_and_scale(v, sq, n, eps):
                m = v.shape[1]
                s = stat8[:, 0:m]
                V.tensor_reduce(s, v, AX.X, ALU.add).then_inc(dve_step, 1)
                dve.wait_ge(dve_step, t_step.next())
                V.tensor_scalar(s, s, 1.0 / n, None, ALU.mult).then_inc(dve_step, 1)
                dve.wait_ge(dve_step, t_step.next())
                V.tensor_tensor(v, v, spread(s, n), ALU.subtract).then_inc(dve_step, 1)
                dve.wait_ge(dve_step, t_step.next())
                V.tensor_tensor(sq, v, v, ALU.mult).then_inc(dve_step, 1)
                dve.wait_ge(dve_step, t_step.next())
                V.tensor_reduce(s, sq, AX.X, ALU.add).then_inc(dve_step, 1)
                dve.wait_ge(dve_step, t_step.next())
                V.tensor_scalar(s, s, 1.0 / n, None, ALU.mult).then_inc(dve_step, 1)
                dve.wait_ge(dve_step, t_step.next())
                V.tensor_tensor(v, v, spread(rsqrt(s, ALU.add, eps), n), ALU.mult).then_inc(dve_step, 1)
                dve.wait_ge(dve_step, t_step.next())

            def mixer_ab():
                n_chunks = len(chunks_of(AB_IN))
                V.memset(shifted[0:1, 0, :], 0.0).then_inc(dve_step, 1)
                dve.wait_ge(dve_step, t_step.next())
                passed(2 * n_chunks)
                mu, p0, p1, lora, sg, const = [own_slot(n) for n in RW_SLOTS]
                w0, a0, k_k, k_a = [ring[:, p0, 512 * n:512 * n + 512] for n in range(4)]
                r_k, gn_g, gn_b = [ring[:, p1, 512 * n:512 * n + 512] for n in range(3)]
                groups = lambda v: v.rearrange("p (g d) -> p g d", g=SG_GROUPS)
                heads = lambda v: v.rearrange("p (h d) -> p h d", h=RW_HEADS)
                ws = groups(ring[:, lora, 1024:1536])
                V.tensor_tensor(ws, ws, ring[:, const, 10 * P + 2:11 * P + 2].unsqueeze(1).to_broadcast([P, SG_GROUPS, P]),
                                ALU.mult).then_inc(vec_for_pe, 1)
                dve.wait_ge(proj_done, t_proj.next(n_chunks))
                dve.wait_ge(shift_loaded, 32 * (1 + shifts[0]))
                shifts[0] += 1
                for t in range(NT):
                    ps = p_ab[:, t, 0:RW_SHIFT]
                    V.tensor_tensor(shifted[:, t, :], shifted[:, t, :], ps, ALU.subtract).then_inc(dve_step, 1)
                    dve.wait_ge(dve_step, t_step.next())
                    V.tensor_tensor(shifted[:, t, :], shifted[:, t, :], ring[:, mu, 0:RW_SHIFT], ALU.mult).then_inc(dve_step, 1)
                    dve.wait_ge(dve_step, t_step.next())
                    ins = V.tensor_tensor(ps, ps, shifted[:, t, :], ALU.add)
                    if t == NT - 1:
                        ins.then_inc(vec_for_act, 1)
                    else:
                        ins.then_inc(dve_step, 1)
                        dve.wait_ge(dve_step, t_step.next())
                dve.wait_ge(act_for_vec, t_act.next())
                for t in range(NT):
                    z = p_ab[:, t, 2304:2816]
                    centre_and_scale(groups(z), groups(rw_y), P, LN_EPS)
                    V.tensor_tensor(z, z, ring[:, sg, 0:512], ALU.mult).then_inc(dve_step, 1)
                    dve.wait_ge(dve_step, t_step.next())
                    ins = V.tensor_tensor(z, z, ring[:, sg, 512:1024], ALU.add)
                    if t == NT - 1:
                        ins.then_inc(vec_for_pe, 1)
                    else:
                        ins.then_inc(dve_step, 1)
                        dve.wait_ge(dve_step, t_step.next())
                dve.wait_ge(pe_for_vec, t_pe.next())
                for t in range(NT):
                    for g in range(SG_GROUPS):
                        c = slice(P * g, P * g + P)
                        last = V.scalar_tensor_tensor(groups(p_ab[:, t, 2304:2816])[:, g, :], lin[:, t, c], ring[:, lora, 1536 + g:1537 + g],
                                                      p_ab[:, t, 1792 + P * g:1792 + P * g + P], ALU.add, ALU.mult)
                last.then_inc(vec_for_pe, 1)
                V.memset(rw_state, 0.0).then_inc(dve_step, 1)
                dve.wait_ge(dve_step, t_step.next())
                for t in range(NT):
                    r, k, v = [p_ab[:, t, 512 * n:512 * n + 512] for n in range(3)]
                    V.tensor_tensor(rw_kk, k, k_k, ALU.mult).then_inc(dve_step, 1)
                    dve.wait_ge(dve_step, t_step.next())
                    V.tensor_tensor(rw_pexc, rw_kk, rw_kk, ALU.mult).then_inc(dve_step, 1)
                    dve.wait_ge(dve_step, t_step.next())
                    V.tensor_reduce(stat8, heads(rw_pexc), AX.X, ALU.add).then_inc(dve_step, 1)
                    dve.wait_ge(dve_step, t_step.next())
                    V.tensor_tensor(heads(rw_kk), heads(rw_kk), spread(rsqrt(stat8, ALU.max, 1e-24), 64), ALU.mult).then_inc(dve_step, 1)
                    dve.wait_ge(dve_step, t_step.next())
                    dve.wait_ge(pe_for_vec, t_pe.next())
                    V.tensor_tensor(rw_tmp, lin[:, 0, :], w0, ALU.add)
                    V.tensor_copy(rw_g, lin[:, 2, :])
                    V.tensor_tensor(rw_a, lin[:, 1, :], a0, ALU.add).then_inc(vec_for_act, 1)
                    dve.wait_ge(act_for_vec, t_act.next())
                    V.tensor_scalar(rw_lw, rw_tmp, -math.exp(-0.5), None, ALU.mult).then_inc(vec_for_pe, 1)
                    V.tensor_tensor(rw_b, rw_kk, rw_a, ALU.mult)
                    V.scalar_tensor_tensor(rw_k, rw_a, 1.0, k_a, ALU.subtract, ALU.mult).then_inc(dve_step, 1)
                    dve.wait_ge(dve_step, t_step.next())
                    V.scalar_tensor_tensor(k, rw_k, 1.0, k, ALU.add, ALU.mult).then_inc(dve_step, 1)
                    dve.wait_ge(dve_step, t_step.next())
                    dve.wait_ge(act_for_vec, t_act.next())
                    V.tensor_tensor(rw_kk, rw_kk, rw_pexc, ALU.mult)
                    V.tensor_tensor(rw_r, rw_r, r, ALU.mult)
                    V.tensor_tensor(rw_b, rw_b, rw_pinv, ALU.mult)
                    V.tensor_tensor(rw_k, k, rw_pinv, ALU.mult).then_inc(vec_for_pe, 1)
                    eye = ident[:, :].unsqueeze(1).to_broadcast([P, RW_HEADS, P])
                    V.tensor_copy(rw_X, eye)
                    V.tensor_copy(rw_XT, eye)
                    for h in range(RW_HEADS):
                        dve.wait_ge(gm_full, t_gm.next())
                        V.tensor_tensor(rw_G[:, h, :], sco[:, h % 2, :], ring[:, const, 0:4 * P], ALU.mult).then_inc(gm_done, 1)
                        t_gm_done.skip(1)
                    dve.wait_ge(gm_done, t_gm_done.n)
                    flat = lambda v: v.rearrange("p h k -> p (h k)")
                    for level in range(7):
                        if level:
                            dve.wait_ge(pe_for_vec, t_pe.next())
                            ins = V.tensor_tensor(flat(rw_XT), flat(rw_XT), lin[:, 2:4, :].rearrange("p a b -> p (a b)"), ALU.subtract)
                        if 0 < level < 6:
                            V.tensor_tensor(flat(rw_X), flat(rw_X), sco[:, :, :].rearrange("p a b -> p (a b)"), ALU.subtract)
                        if level < 6:
                            mask = ring[:, const, (4 + level) * P:(5 + level) * P].unsqueeze(1).to_broadcast([P, RW_HEADS, P])
                            ins = V.tensor_tensor(rw_BT, rw_G[:, :, 0:P], mask, ALU.mult)
                        ins.then_inc(vec_for_pe, 1)
                    pairs = lambda a: a.rearrange("p (h o d) -> p h o d", o=2, d=64)
                    for half in range(2):
                        rs = slice(64 * half, 64 * half + 64)
                        dve.wait_ge(pe_for_vec, t_pe.next())
                        V.tensor_copy(rw_U[rs, :], lin[rs, 2, :]).then_inc(dve_step, 1)
                        dve.wait_ge(dve_step, t_step.next())
                        for o in range(2):
                            ins = V.tensor_tensor(pairs(rw_U[rs, :])[:, :, o, :], pairs(rw_U[rs, :])[:, :, o, :], pairs(lin[rs, o, :])[:, :, o, :], ALU.add)
                        ins.then_inc(vec_for_pe, 1)
                        dve.wait_ge(pe_for_vec, t_pe.next())
                        V.tensor_copy(rw_y[rs, :], lin[rs, 2, :]).then_inc(dve_step, 1)
                        dve.wait_ge(dve_step, t_step.next())
                        for o in range(2):
                            V.tensor_tensor(pairs(rw_y[rs, :])[:, :, o, :], pairs(rw_y[rs, :])[:, :, o, :], pairs(sco[rs, o, :])[:, :, o, :], ALU.add)
                        V.tensor_tensor(rw_state, rw_state, lin[:, 0, 0:256].rearrange("p (a d) -> p a d", a=4), ALU.add).then_inc(dve_step, 1)
                        dve.wait_ge(dve_step, t_step.next())
                        V.tensor_tensor(rw_state, rw_state, rw_decay[:, :, half].unsqueeze(2).to_broadcast([P, 4, 64]), ALU.mult).then_inc(vec_for_pe, 1)
                    dve.wait_ge(dve_step, t_step.n)
                    y = heads(rw_y)
                    V.tensor_tensor(rw_tmp, r, k, ALU.mult).then_inc(dve_step, 1)
                    dve.wait_ge(dve_step, t_step.next())
                    centre_and_scale(y, heads(rw_pexc), 64, RW_GN_EPS)
                    V.tensor_tensor(rw_y, rw_y, gn_g, ALU.mult).then_inc(dve_step, 1)
                    dve.wait_ge(dve_step, t_step.next())
                    V.tensor_tensor(rw_y, rw_y, gn_b, ALU.add).then_inc(dve_step, 1)
                    dve.wait_ge(dve_step, t_step.next())
                    V.tensor_tensor(rw_tmp, rw_tmp, r_k, ALU.mult).then_inc(dve_step, 1)
                    dve.wait_ge(dve_step, t_step.next())
                    V.tensor_reduce(stat8, heads(rw_tmp), AX.X, ALU.add).then_inc(dve_step, 1)
                    dve.wait_ge(dve_step, t_step.next())
                    V.tensor_tensor(heads(rw_tmp), heads(v), spread(stat8, 64), ALU.mult).then_inc(dve_step, 1)
                    dve.wait_ge(dve_step, t_step.next())
                    V.tensor_tensor(rw_y, rw_y, rw_tmp, ALU.add).then_inc(dve_step, 1)
                    dve.wait_ge(dve_step, t_step.next())
                    ins = V.tensor_tensor(r, rw_y, rw_g, ALU.mult)
                    if t == NT - 1:
                        ins.then_inc(vec_for_pe, 1)
                    else:
                        ins.then_inc(dve_step, 1)
                        dve.wait_ge(dve_step, t_step.next())

            def mla():
                V.memset(mla_qpe, 0.0)
                passed(4)
                s = own_slot(3)
                V.tensor_copy(rope2, ring[:, s, 512:576]).then_inc(dve_step, 1)
                dve.wait_ge(dve_step, t_step.next())
                cos, sin = [rope2[:, 32 * n:32 * n + 32].rearrange("p (t f) -> p t f", t=NT) for n in range(2)]
                dve.wait_ge(proj_done, t_proj.next(2))
                for t in range(NT):
                    sq = mla_tmp[:, 0:2, :]
                    latents = mla_p[:, t, 0:512].rearrange("p (c d) -> p c d", c=2)
                    V.tensor_tensor(sq, latents, latents, ALU.mult).then_inc(dve_step, 1)
                    dve.wait_ge(dve_step, t_step.next())
                    V.tensor_reduce(bn[:, t, 0:2], sq, AX.X, ALU.add).then_inc(dve_step, 1)
                    dve.wait_ge(dve_step, t_step.next())
                    V.tensor_scalar(bn[:, t, 0:2], bn[:, t, 0:2], 1.0 / 256, None, ALU.mult).then_inc(dve_step, 1)
                    dve.wait_ge(dve_step, t_step.next())
                    root = rsqrt(bn[:, t, 0:2], ALU.add, RMS_EPS)
                    for c in range(2):
                        V.scalar_tensor_tensor(latents[:, c, :], latents[:, c, :], root[:, c:c + 1], ring[:, s, 256 * c:256 * c + 256], ALU.mult, ALU.mult)
                    key = mla_p[:, t, 512:544].unsqueeze(1)
                    rotate(key, cos[:, t, :], sin[:, t, :], 16, mla_tmp).then_inc(dve_step, 1)
                    dve.wait_ge(dve_step, t_step.next())
                    ins = V.tensor_copy(mla_kpe[:, t, :, :], key.to_broadcast([P, 4, 32]))
                    if t == NT - 1:
                        ins.then_inc(vec_for_pe, 1)
                    else:
                        ins.then_inc(dve_step, 1)
                        dve.wait_ge(dve_step, t_step.next())
                dve.wait_ge(proj_done, t_proj.next(3 + 4))
                passed(3 + 4)
                for t in range(NT):
                    queries = mla_q[:, t, :, 64:96]
                    V.tensor_copy(mla_qn[:, t, :, :], mla_q[:, t, :, 0:64])
                    V.tensor_copy(mla_kn[t], mla_kv[:, t, :, 0:64])
                    rotate(queries, cos[:, t, :], sin[:, t, :], 16, mla_tmp).then_inc(dve_step, 1)
                    dve.wait_ge(dve_step, t_step.next())
                    ins = V.tensor_copy(mla_qpe[:, t, :, 0, :], queries)
                    if t == NT - 1:
                        ins.then_inc(vec_for_pe, 1)
                    else:
                        ins.then_inc(dve_step, 1)
                        dve.wait_ge(dve_step, t_step.next())
                attend(MLA_HEADS, 1, lambda g: causal[:, :, :], 96 ** -0.5)

            def route():
                s = own_slot(5)
                V.memset(group8, MASKED)
                V.memset(chosen, 0.0)
                V.memset(gates, 0.0)
                V.memset(spreadT, 0.0)
                V.memset(pair_y, 0.0).then_inc(pair_out, 1)
                V.tensor_copy(numbers, ring[:, s, router_const("numbers")])
                V.tensor_copy(places, ring[:, s, router_const("places")])
                dve.wait_ge(pe_for_vec, t_pe.next())
                V.tensor_copy(logits36, sco[:, 0, 0:128].rearrange("p (t n) -> p t n", t=NT)[:, :, 0:36])
                V.memset(router, 0.0).then_inc(dve_step, 1)
                dve.wait_ge(dve_step, t_step.next())
                V.tensor_copy(group8[:, :, 0:GROUPS], logits36[:, :, 0:GROUPS]).then_inc(dve_step, 1)
                dve.wait_ge(dve_step, t_step.next())
                tiles = range(NT)
                for t in tiles:
                    ins = V.max(top8[:, t, :], group8[:, t, :])
                ins.then_inc(dve_step, 1)
                dve.wait_ge(dve_step, t_step.next())
                for t in tiles:
                    V.tensor_scalar(router[:, t, 8:9], top8[:, t, 0:1], -1.0, None, ALU.mult)
                    ins = V.max_index(ints[:, 8 * t:8 * t + 8], top8[:, t, :], group8[:, t, :])
                ins.then_inc(dve_step, 1)
                dve.wait_ge(dve_step, t_step.next())
                for t in tiles:
                    ins = V.tensor_copy(router[:, t, 0:1], ints[:, 8 * t:8 * t + 1])
                ins.then_inc(dve_step, 1)
                dve.wait_ge(dve_step, t_step.next())
                for t in tiles:
                    ins = V.tensor_scalar(group_hot[:, t, :], numbers[:, 0:GROUPS], router[:, t, 0:1], 1.0, ALU.is_equal, ALU.subtract)
                ins.then_inc(dve_step, 1)
                dve.wait_ge(dve_step, t_step.next())
                ins = V.tensor_scalar(group_hot, group_hot, -MASKED, None, ALU.mult)
                ins.then_inc(dve_step, 1)
                dve.wait_ge(dve_step, t_step.next())
                for t in tiles:
                    ins = V.tensor_tensor(picked[:, t, :, :], logits36[:, t, GROUPS:36].rearrange("p (g e) -> p g e", g=GROUPS),
                                          spread(group_hot[:, t, :], PER_GROUP), ALU.add)
                ins.then_inc(dve_step, 1)
                dve.wait_ge(dve_step, t_step.next())
                experts = [picked[:, t, :, :].rearrange("p g e -> p (g e)") for t in tiles]
                for t in tiles:
                    ins = V.max(top8[:, t, :], experts[t])
                ins.then_inc(dve_step, 1)
                dve.wait_ge(dve_step, t_step.next())
                for t in tiles:
                    ins = V.max_index(ints[:, 8 * t:8 * t + 8], top8[:, t, :], experts[t])
                ins.then_inc(dve_step, 1)
                dve.wait_ge(dve_step, t_step.next())
                for t in tiles:
                    ins = V.tensor_copy(router[:, t, 0:2], ints[:, 8 * t:8 * t + 2])
                ins.then_inc(dve_step, 1)
                for t in tiles:
                    ins = V.tensor_tensor(router[:, t, 10:11], top8[:, t, 1:2], top8[:, t, 0:1], ALU.subtract)
                ins.then_inc(vec_for_act, 1)
                dve.wait_ge(dve_step, t_step.next())
                for t in tiles:
                    ins = V.tensor_scalar(chosen[:, t, 0:EXPERTS], numbers, router[:, t, 0:1], None, ALU.is_equal)
                ins.then_inc(dve_step, 1)
                dve.wait_ge(dve_step, t_step.next())
                for t in tiles:
                    ins = V.scalar_tensor_tensor(chosen[:, t, 0:EXPERTS], numbers, router[:, t, 1:2], chosen[:, t, 0:EXPERTS], ALU.is_equal, ALU.add)
                ins.then_inc(vec_for_pe, 1)
                dve.wait_ge(act_for_vec, t_act.next())
                e2, total, norm, first, second = [router[:, :, c:c + 1] for c in (11, 9, 12, 13, 14)]
                for t in tiles:
                    ins = V.scalar_tensor_tensor(norm[:, t, :], e2[:, t, :], 1.0, total[:, t, :], ALU.add, ALU.mult)
                ins.then_inc(dve_step, 1)
                dve.wait_ge(dve_step, t_step.next())
                for t in tiles:
                    ins = V.reciprocal(first[:, t, :], norm[:, t, :])
                ins.then_inc(dve_step, 1)
                dve.wait_ge(dve_step, t_step.next())
                for t in tiles:
                    ins = V.tensor_tensor(second[:, t, :], first[:, t, :], e2[:, t, :], ALU.mult)
                ins.then_inc(dve_step, 1)
                dve.wait_ge(dve_step, t_step.next())
                for t in tiles:
                    V.tensor_scalar(hot[:, t, :], numbers, router[:, t, 0:1], first[:, t, :], ALU.is_equal, ALU.mult)
                    ins = V.tensor_scalar(gates[:, t, 0:EXPERTS], numbers, router[:, t, 1:2], second[:, t, :], ALU.is_equal, ALU.mult)
                ins.then_inc(dve_step, 1)
                dve.wait_ge(dve_step, t_step.next())
                for t in tiles:
                    V.tensor_tensor(gates[:, t, 0:EXPERTS], gates[:, t, 0:EXPERTS], hot[:, t, :], ALU.add)
                dve.wait_ge(slots_used, used.n)
                V.tensor_reduce(most[:, 0:1], sco[:, 1, 128:128 + EXPERTS], AX.X, ALU.max)
                for t in range(NT):
                    ins = V.tensor_copy(place_of[:, t, :], sco[:, 1, 64 * t:64 * t + COLUMNS])
                ins.then_inc(dve_step, 1)
                dve.wait_ge(dve_step, t_step.next())

            def check_overflow(layer):
                V.tensor_scalar(ints[0:1, 16 + layer:17 + layer], most[0:1, 0:1], float(PLACES), None, ALU.is_gt).then_inc(overflow_known, 1)

            def moe(layer):
                route()

                def select(first):
                    for dst, weight in ((gathering, chosen), (gated, gates)):
                        for t in range(NT):
                            for j in range(2):
                                column = bass.ds(first + j, 1)
                                ins = V.tensor_scalar(dst[:, t, PLACES * j:PLACES * j + PLACES], places, place_of[:, t, column],
                                                      weight[:, t, column], ALU.is_equal, ALU.mult)
                    ins.then_inc(selected, 1)

                def add_combined():
                    for t in range(NT):
                        dve.wait_ge(combined, t_combined.next())
                        dve.wait_ge(y_added, t_y.next())
                        V.tensor_tensor(moe_sum[:, t, :], moe_sum[:, t, :], lin[:, 2 * (1 - t):2 * (1 - t) + 2, :].rearrange("p a b -> p (a b)"),
                                        ALU.add).then_inc(y_added, 1)

                select(0)
                check_overflow(layer)
                for t in range(NT):
                    V.tensor_scalar(moe_sum[:, t, :], x[:, t, :], ALPHA_2, None, ALU.mult).then_inc(y_added, 1)
                with rounds(dve, PAIRS, {t_silu: 1, used: RING, t_combined: 2, t_y: 2, t_selection: 1}) as i:
                    dve.wait_ge(silu_done, t_silu.next())
                    dve.wait_ge(slots_used, used.next(8))
                    V.tensor_tensor(pair_h, pair_silu, sco[:, 1, :], ALU.mult).then_inc(h_done, 1)
                    used.skip(4)
                    add_combined()
                    dve.wait_ge(selection_used, t_selection.next())
                    select(i * 2 + 2)
                used.skip(-EXPERTS * 6)
                passed(EXPERTS * 6)
                add_combined()
                dve.wait_ge(y_added, t_y.next(2))

                overflow = dve.value_load(ints[0:1, 16 + layer:17 + layer], min_val=0, max_val=1)
                t_rest_silu, t_output, t_added = Tally(rest_silu[layer]), Tally(rest_output[layer]), Tally(rest_added[layer])
                with dve.If(overflow):
                    for t in range(NT):
                        ins = V.scalar_tensor_tensor(late_gates[:, t, :], place_of[:, t, 0:EXPERTS], float(PLACES), gates[:, t, 0:EXPERTS], ALU.is_ge, ALU.mult)
                    ins.then_inc(rest_added[layer], 1)
                    with rounds(dve, EXPERTS, {t_rest_silu: 4, t_output: 1, t_added: 1}) as i:
                        for f in range(4):
                            dve.wait_ge(rest_silu[layer], t_rest_silu.next())
                            V.tensor_tensor(hT[:, 0, f, :], silu_g[:, 0, :], sco[:, 0, SEQ:2 * SEQ], ALU.mult).then_inc(rest_hidden[layer], 1)
                        dve.wait_ge(rest_output[layer], t_output.next())
                        dve.wait_ge(rest_added[layer], t_added.next())
                        for t in range(NT):
                            ins = V.scalar_tensor_tensor(moe_sum[:, t, :], lin[:, 2 * t:2 * t + 2, :].rearrange("p a b -> p (a b)"),
                                                         late_gates[:, t, bass.ds(i, 1)], moe_sum[:, t, :], ALU.mult, ALU.add)
                        ins.then_inc(rest_added[layer], 1)
                    dve.wait_ge(rest_added[layer], t_added.next())
                s = own_slot(2)
                for t in range(NT):
                    normalise(moe_sum, t, s, x)

            dve.wait_ge(input_loaded, 16 * 4)
            dve.wait_ge(pool_step, 1)
            passed(2 * len(chunks_of(WIDTH_A)))
            s = own_slot(2)
            for t in range(NT):
                normalise(memrows, t, s)
            V.tensor_copy(pos_f, ints[:, 0:NT].bitcast(I32)).then_inc(dve_step, 1)
            dve.wait_ge(dve_step, t_step.next())
            for t in range(NT):
                V.tensor_scalar(small[:, 96 + 8 * t:104 + 8 * t], inv_freq, pos_f[:, t:t + 1], None, ALU.mult)
                last = V.tensor_scalar(small[:, 112 + 8 * t:120 + 8 * t], inv_freq, pos_f[:, t:t + 1], None, ALU.mult)
            last.then_inc(dve_step, 1)
            dve.wait_ge(dve_step, t_step.next())
            ROUND = 1.5 * 2.0 ** 23
            TURN = (6.28125, 0.0019340515136718750, 1.2556659146180184e-06)
            whole = [rope_tmp[:, 0, 0:16], rope_tmp[:, 0, 16:32]]
            V.tensor_scalar(whole[0], small[:, 96:112], 1 / (2 * math.pi), 0.25, ALU.mult, ALU.add).then_inc(dve_step, 1)
            dve.wait_ge(dve_step, t_step.next())
            V.tensor_scalar(whole[0], whole[0], ROUND, None, ALU.add).then_inc(dve_step, 1)
            dve.wait_ge(dve_step, t_step.next())
            V.tensor_scalar(whole[1], small[:, 112:128], 1 / (2 * math.pi), ROUND, ALU.mult, ALU.add).then_inc(dve_step, 1)
            dve.wait_ge(dve_step, t_step.next())
            V.tensor_scalar(rope_tmp[:, 0, 0:32], rope_tmp[:, 0, 0:32], ROUND, None, ALU.subtract).then_inc(dve_step, 1)
            dve.wait_ge(dve_step, t_step.next())
            for c in TURN:
                V.scalar_tensor_tensor(small[:, 96:128], rope_tmp[:, 0, 0:32], -c, small[:, 96:128], ALU.mult, ALU.add).then_inc(dve_step, 1)
                dve.wait_ge(dve_step, t_step.next())
            V.tensor_scalar(small[:, 96:112], small[:, 96:112], math.pi / 2, None, ALU.add).then_inc(dve_step, 1)
            dve.wait_ge(dve_step, t_step.next())
            V.tensor_scalar(small[:, 96:128], small[:, 96:128], 3.1415925, -3.1415925, ALU.min, ALU.max).then_inc(vec_for_act, 1)
            dve.wait_ge(act_for_vec, t_act.next())
            for layer in range(FIRST_LAYERS):
                kind = kind_of(layer)
                proj = projA if kind == 0 else projBC
                width = WIDTH_A if kind == 0 else WIDTH_BC
                n_chunks = len(chunks_of(width))
                dve.wait_ge(proj_done, t_proj.next(n_chunks + 1))
                passed(2 if layer == 0 else 2 * n_chunks + 2)
                for t in range(NT):
                    last = rotate(proj[:, t, 0:2 * MIX].rearrange("p (h d) -> p h d", d=DH), rope_cos[:, t, :], rope_sin[:, t, :], ROPE_HALF)
                    if kind == 0:
                        last.then_inc(dve_step, 1)
                        dve.wait_ge(dve_step, t_step.next())
                        last = rotate(proj[:, t, 2304:2816].rearrange("p (h d) -> p h d", d=DH), rope_cos[:, t, :], rope_sin[:, t, :], ROPE_HALF)
                    if t < NT - 1 or kind == 0:
                        last.then_inc(dve_step, 1)
                        dve.wait_ge(dve_step, t_step.next())
                if kind == 0:
                    s = own_slot(2)
                    for t in range(NT):
                        ki = proj[:, t, 2824:2888]
                        V.tensor_scalar(proj[:, t, 2816:2824], proj[:, t, 2816:2824], (IDX_HEADS * DH) ** -0.5, None, ALU.mult)
                        V.bn_stats(bn[:, t, 0:6], ki).then_inc(dve_step, 1)
                        dve.wait_ge(dve_step, t_step.next())
                        V.bn_aggr(mean_var[:, t, :], bn[:, t, 0:6]).then_inc(dve_step, 1)
                        dve.wait_ge(dve_step, t_step.next())
                        rstd = rsqrt(mean_var[:, t, 1:2], ALU.add, LN_EPS)
                        V.scalar_tensor_tensor(ki, ki, mean_var[:, t, 0:1], ring[:, s, 0:DH], ALU.subtract, ALU.mult).then_inc(dve_step, 1)
                        dve.wait_ge(dve_step, t_step.next())
                        V.scalar_tensor_tensor(ki, ki, rstd, ring[:, s, DH:2 * DH], ALU.mult, ALU.add).then_inc(dve_step, 1)
                        dve.wait_ge(dve_step, t_step.next())
                        rotate(ki.unsqueeze(1), rope_cos[:, t, :], rope_sin[:, t, :], ROPE_HALF).then_inc(dve_step, 1)
                        dve.wait_ge(dve_step, t_step.next())
                        V.tensor_copy(ki2[:, t, 0, :], ki)
                        last = V.tensor_copy(ki2[:, t, 1, :], ki)
                        if t < NT - 1:
                            last.then_inc(dve_step, 1)
                            dve.wait_ge(dve_step, t_step.next())
                last.then_inc(rope_done, 1)
                if kind == 0:
                    select_keys(proj)
                attend(MEM_HEADS, 1, lambda g: None, DH ** -0.5)
                if kind == 0:
                    attend(HEADS, 1, lambda g: dsa_mask, DH ** -0.5)
                elif kind == 1:
                    s = own_slot(1)
                    masks = ring[:, s, 0:3 * NT * SEQ].rearrange("p (g t k) -> p g t k", g=3, t=NT)
                    attend(4, 3, lambda g: masks[:, g, :, :], DH ** -0.5)
                else:
                    attend(HEADS, 1, lambda g: causal[:, :, :], DH ** -0.5)
                passed(4)
                add_and_normalise(ALPHA)
                ffn()
                passed(3 * (D_FF // (2 * P)))
                add_and_normalise(ALPHA)
            for layer in range(SECOND_LAYERS):
                if layer % 2 == 0:
                    mixer_ab()
                else:
                    mla()
                passed(4)
                add_and_normalise(ALPHA_2)
                if layer == 0:
                    passed(1)
                passed(4 + 8)
                t_proj.skip(2 + 4)
                attend(XA_HEADS, 1, lambda g: None, (D // XA_HEADS) ** -0.5)
                passed(4)
                add_and_normalise(ALPHA_2)
                moe(layer)


_INS = ["x", "mem", "positions", "mem_ln_g", "mem_ln_b", "w_in_a", "idx_kn_g", "idx_kn_b", "w_in_b", "w_in_c", "w_mem_kv",
        "w_out", "ln1_g", "ln1_b", "w_gate_up", "w_down", "ln2_g", "ln2_b", "mem_2", "ab_w_in_2", "ab_mu_2", "rw_w0_2",
        "rw_w2_2", "rw_a0_2", "rw_a2_2", "rw_g2_2", "rw_k_k_2", "rw_k_a_2", "rw_r_k_2", "rw_gn_g_2", "rw_gn_b_2",
        "sg_ln_g_2", "sg_ln_b_2", "sg_ws_2", "sg_b_2", "ab_w_out_2", "mla_w_in_2", "mla_q_norm_2", "mla_kv_norm_2",
        "mla_wq_b_2", "mla_wkv_b_2", "mla_w_out_2", "ln1_g_2", "ln1_b_2", "xa_wq_2", "xa_wkv_2", "xa_wo_2", "ln2_g_2",
        "ln2_b_2", "moe_w_group_2", "moe_b_group_2", "moe_w_expert_2", "moe_b_expert_2", "moe_w_gate_2",
        "moe_w_up_2", "moe_w_down_2", "ln3_g_2", "ln3_b_2"]


def kernel(**inputs):
    import concourse.bacc as _bacc
    from concourse.bass_utils import run_bass_kernel_spmd as _run

    nc = _bacc.Bacc("TRN2", target_bir_lowering=False, num_devices=1)
    arrays, args = {}, {}
    for name in _INS + ["consts"]:
        a = shape_constants() if name == "consts" else np.ascontiguousarray(inputs[name])
        if name == "positions":
            a = np.ascontiguousarray(a.reshape(NT, P).T)
        if name == "sg_b_2":
            a = np.ascontiguousarray(a.transpose(0, 2, 1))
        arrays[f"in_{name}"] = a
        args[name] = nc.dram_tensor(f"in_{name}", a.shape, mybir.dt.from_np(a.dtype), kind="ExternalInput").ap()
    o = nc.dram_tensor("out_0", (1, SEQ, D), F32, kind="ExternalOutput").ap()
    build(nc, args, o)
    r = _run(nc, [arrays], core_ids=[0])
    return r.results[0]["out_0"]
```
